# Optimizing a Trainium2 kernel written in Bass

```python
import math
import jax, jax.numpy as jnp
from jax import lax
import numpy as np

D_MODEL = 1024
BATCH = 1
SEQ = 256
DEPTH = 1

HEAD_DIM = 64
N_HEADS_A = D_MODEL // (2 * HEAD_DIM)
N_HEADS_B = D_MODEL // (2 * HEAD_DIM)
WIDTH_A = N_HEADS_A * HEAD_DIM
WIDTH_B = N_HEADS_B * HEAD_DIM
MIX_WIDTH = WIDTH_A + WIDTH_B
N_IDX_HEADS = 8
IDX_DIM = 64
TOPK_MAX = 256
D_FF = 2816
N_BUCKETS = 32
MAX_DISTANCE = 128
SPARSE_BLOCK = 32
SB_BLOCK = 128
N_SUBLAYERS = 3
N_MOD = 3 * N_SUBLAYERS
EPS = 1e-6

IN_SIZES = [WIDTH_A, WIDTH_A, WIDTH_A, N_IDX_HEADS * IDX_DIM, IDX_DIM, N_IDX_HEADS,
            WIDTH_B, WIDTH_B, WIDTH_B]
IN_COLS = sum(IN_SIZES)
IN_SPLITS = list(np.cumsum(IN_SIZES)[:-1])


def rmsnorm(x, g):
    xf = x.astype(jnp.float32)
    y = xf * lax.rsqrt(jnp.mean(xf * xf, axis=-1, keepdims=True) + EPS)
    return (y * g.astype(jnp.float32)).astype(x.dtype)

def modulate(x, shift, scale):
    return x * (1 + scale[:, None, :]) + shift[:, None, :]

def swiglu(x, w_gate, w_up, w_down):
    return (jax.nn.silu(x @ w_gate) * (x @ w_up)) @ w_down

def t5_bucket(n):
    n = jnp.maximum(n, 0)
    max_exact = N_BUCKETS // 2
    nf = jnp.maximum(n, 1).astype(jnp.float32)
    large = max_exact + (jnp.log(nf / max_exact) / math.log(MAX_DISTANCE / max_exact)
                         * (N_BUCKETS - max_exact)).astype(jnp.int32)
    large = jnp.minimum(large, N_BUCKETS - 1)
    return jnp.where(n < max_exact, n, large)

def dsa_sparse_attention(q, k, v, q_idx, k_idx, w_idx, rel_bias):
    B, S, H, D = q.shape
    topk = min(TOPK_MAX, S // 4)
    nb = S // SPARSE_BLOCK
    key_pos = jnp.arange(S)

    def blocks(a):
        return jnp.swapaxes(a.reshape(B, nb, SPARSE_BLOCK, *a.shape[2:]), 0, 1)

    def one(args):
        qb, qib, wb, t0 = args
        tpos = t0 + jnp.arange(SPARSE_BLOCK)
        sc = jax.nn.relu(jnp.einsum('bthd,bsd->bths', qib, k_idx).astype(jnp.float32))
        score = jnp.einsum('bths,bth->bts', sc, wb.astype(jnp.float32))
        causal = key_pos[None, :] <= tpos[:, None]
        score = jnp.where(causal[None], score, -jnp.inf)
        _, idx = lax.top_k(score, topk)
        kg = jax.vmap(lambda kk, ii: kk[ii])(k, idx)
        vg = jax.vmap(lambda vv, ii: vv[ii])(v, idx)
        dist = tpos[None, :, None] - idx
        valid = dist >= 0
        bias = jnp.swapaxes(rel_bias[t5_bucket(dist)], -1, -2)
        logits = (jnp.einsum('bthd,btkhd->bthk', qb, kg).astype(jnp.float32) * (D ** -0.5)
                  + bias.astype(jnp.float32))
        logits = jnp.where(valid[:, :, None, :], logits, -jnp.inf)
        p = jax.nn.softmax(logits, axis=-1)
        return jnp.einsum('bthk,btkhd->bthd', p.astype(v.dtype), vg)

    starts = jnp.arange(nb) * SPARSE_BLOCK
    out = lax.map(one, (blocks(q), blocks(q_idx), blocks(w_idx), starts))
    return jnp.swapaxes(out, 0, 1).reshape(B, S, H * D)

def stick_breaking_attention(q, k, v):
    B, S, H, D = q.shape
    nb = S // SB_BLOCK
    key_pos = jnp.arange(S)
    q_blocks = jnp.swapaxes(q.reshape(B, nb, SB_BLOCK, H, D), 0, 1)

    def one(args):
        qb, t0 = args
        tpos = t0 + jnp.arange(SB_BLOCK)
        z = jnp.einsum('bthd,bshd->bhts', qb, k).astype(jnp.float32) * (D ** -0.5)
        mask = (key_pos[None, :] < tpos[:, None])[None, None]
        u = jnp.where(mask, jax.nn.log_sigmoid(-z), 0.0)
        between = lax.cumsum(u, axis=3, reverse=True) - u
        a = jnp.where(mask, jnp.exp(jax.nn.log_sigmoid(z) + between), 0.0)
        return jnp.einsum('bhts,bshd->bthd', a.astype(v.dtype), v)

    starts = jnp.arange(nb) * SB_BLOCK
    out = lax.map(one, (q_blocks, starts))
    return jnp.swapaxes(out, 0, 1).reshape(B, S, H * D)

def first_inputs(seed: int = 0) -> dict:
    key = jax.random.key(seed)
    ks = jax.random.split(key, 20)
    f32 = jnp.float32
    nrm = lambda k, shape, s: jax.random.normal(k, shape, f32) * s
    return {
        "x": nrm(ks[0], (BATCH, SEQ, D_MODEL), 1.0),
        "c": nrm(ks[1], (BATCH, D_MODEL), 1.0),
        "w_ada": nrm(ks[2], (DEPTH, D_MODEL, N_MOD * D_MODEL), 0.5 * D_MODEL ** -0.5),
        "b_ada": nrm(ks[3], (DEPTH, N_MOD * D_MODEL), 0.02),
        "g_pre": 1.0 + nrm(ks[4], (DEPTH, N_SUBLAYERS, D_MODEL), 0.05),
        "g_post": 1.0 + nrm(ks[5], (DEPTH, N_SUBLAYERS, D_MODEL), 0.05),
        "w_ffn_gate": nrm(ks[6], (DEPTH, 2, D_MODEL, D_FF), D_MODEL ** -0.5),
        "w_ffn_up": nrm(ks[7], (DEPTH, 2, D_MODEL, D_FF), D_MODEL ** -0.5),
        "w_ffn_down": nrm(ks[8], (DEPTH, 2, D_FF, D_MODEL), D_FF ** -0.5),
        "w_in": nrm(ks[9], (DEPTH, D_MODEL, IN_COLS), D_MODEL ** -0.5),
        "g_kidx": 1.0 + nrm(ks[10], (DEPTH, IDX_DIM), 0.05),
        "rel_bias": nrm(ks[11], (N_BUCKETS, N_HEADS_A), 0.5),
        "g_out_a": 1.0 + nrm(ks[12], (DEPTH, WIDTH_A), 0.05),
        "g_out_b": 1.0 + nrm(ks[13], (DEPTH, WIDTH_B), 0.05),
        "w_out": nrm(ks[14], (DEPTH, MIX_WIDTH, D_MODEL), MIX_WIDTH ** -0.5),
    }

def first_block(x, c, w_ada, b_ada, g_pre, g_post, w_ffn_gate, w_ffn_up, w_ffn_down,
              w_in, g_kidx, rel_bias, g_out_a, g_out_b, w_out):
    B, S, _ = x.shape
    h = x
    for l in range(DEPTH):
        mods = (jax.nn.silu(c) @ w_ada[l] + b_ada[l]).reshape(B, N_MOD, D_MODEL)
        shift = lambda i: mods[:, 3 * i]
        scale = lambda i: mods[:, 3 * i + 1]
        gate = lambda i: mods[:, 3 * i + 2][:, None, :]

        n = modulate(rmsnorm(h, g_pre[l, 0]), shift(0), scale(0))
        f = swiglu(n, w_ffn_gate[l, 0], w_ffn_up[l, 0], w_ffn_down[l, 0])
        h = h + 0.5 * gate(0) * rmsnorm(f, g_post[l, 0])

        n = modulate(rmsnorm(h, g_pre[l, 1]), shift(1), scale(1))
        p = n @ w_in[l]
        qa, ka, va, qi, ki, wi, qb, kb, vb = jnp.split(p, IN_SPLITS, axis=-1)
        qa = qa.reshape(B, S, N_HEADS_A, HEAD_DIM)
        ka = ka.reshape(B, S, N_HEADS_A, HEAD_DIM)
        va = va.reshape(B, S, N_HEADS_A, HEAD_DIM)
        qi = qi.reshape(B, S, N_IDX_HEADS, IDX_DIM)
        ki = rmsnorm(ki, g_kidx[l])
        wi = wi * ((N_IDX_HEADS * IDX_DIM) ** -0.5)
        qb = qb.reshape(B, S, N_HEADS_B, HEAD_DIM)
        kb = kb.reshape(B, S, N_HEADS_B, HEAD_DIM)
        vb = vb.reshape(B, S, N_HEADS_B, HEAD_DIM)

        oa = rmsnorm(dsa_sparse_attention(qa, ka, va, qi, ki, wi, rel_bias), g_out_a[l])
        ob = rmsnorm(stick_breaking_attention(qb, kb, vb), g_out_b[l])
        o = jnp.concatenate([oa, ob], axis=-1) @ w_out[l]
        h = h + gate(1) * rmsnorm(o, g_post[l, 1])

        n = modulate(rmsnorm(h, g_pre[l, 2]), shift(2), scale(2))
        f = swiglu(n, w_ffn_gate[l, 1], w_ffn_up[l, 1], w_ffn_down[l, 1])
        h = h + 0.5 * gate(2) * rmsnorm(f, g_post[l, 2])
    return h


FOURIER_GROUPS = 4
FOURIER_WIDTH = D_MODEL // 2
FOURIER_GROUP_DIM = FOURIER_WIDTH // FOURIER_GROUPS
MLA_HEADS = 8
QK_NOPE_DIM = 64
QK_ROPE_DIM = 32
V_HEAD_DIM = (D_MODEL // 2) // MLA_HEADS
Q_LORA_RANK = 384
KV_LORA_RANK = 256
Q_BLOCK = 128
ROPE_THETA = 10000.0
NORM_EPS = 1e-6
N_ADA = 9
W_IN_COLS = FOURIER_WIDTH + Q_LORA_RANK + KV_LORA_RANK + QK_ROPE_DIM + 2 * D_MODEL
SPLIT_1 = FOURIER_WIDTH
SPLIT_2 = SPLIT_1 + Q_LORA_RANK
SPLIT_3 = SPLIT_2 + KV_LORA_RANK
SPLIT_4 = SPLIT_3 + QK_ROPE_DIM


def rms_norm(x, g):
    x32 = x.astype(jnp.float32)
    y = x32 * lax.rsqrt(jnp.mean(x32 * x32, axis=-1, keepdims=True) + NORM_EPS)
    return (y * g.astype(jnp.float32)).astype(x.dtype)

def modulate_2(h, shift, scale):
    return h * (1 + scale[:, None, :]) + shift[:, None, :]

def swiglu_2(h, w_gate, w_up, w_down):
    return (jax.nn.silu(h @ w_gate) * (h @ w_up)) @ w_down

def rope_tables(positions):
    half = QK_ROPE_DIM // 2
    inv_freq = 1.0 / (ROPE_THETA ** (jnp.arange(half, dtype=jnp.float32) * 2.0 / QK_ROPE_DIM))
    ang = positions.astype(jnp.float32)[..., None] * inv_freq
    return jnp.cos(ang), jnp.sin(ang)

def apply_rope(x, cos, sin):
    x32 = x.astype(jnp.float32)
    x1, x2 = jnp.split(x32, 2, axis=-1)
    out = jnp.concatenate([x1 * cos - x2 * sin, x2 * cos + x1 * sin], axis=-1)
    return out.astype(x.dtype)

def fourier_mix(u):
    b, s, _ = u.shape
    ug = u.reshape(b, s, FOURIER_GROUPS, FOURIER_GROUP_DIM).astype(jnp.float32)
    f = jnp.fft.fft2(ug, axes=(1, 3), norm="ortho").real
    return f.reshape(b, s, FOURIER_WIDTH).astype(u.dtype)

def mla_attention(q_lat, kv_lat, k_rope, positions, q_norm, w_q_up, kv_norm, w_kv_up):
    b, s, _ = q_lat.shape
    q = (rms_norm(q_lat, q_norm) @ w_q_up).reshape(b, s, MLA_HEADS, QK_NOPE_DIM + QK_ROPE_DIM)
    kv = (rms_norm(kv_lat, kv_norm) @ w_kv_up).reshape(b, s, MLA_HEADS, QK_NOPE_DIM + V_HEAD_DIM)
    q_nope, q_rot = q[..., :QK_NOPE_DIM], q[..., QK_NOPE_DIM:]
    k_nope, v = kv[..., :QK_NOPE_DIM], kv[..., QK_NOPE_DIM:]
    cos, sin = rope_tables(positions)
    q_rot = apply_rope(q_rot, cos[:, :, None, :], sin[:, :, None, :])
    k_rot = apply_rope(k_rope, cos, sin)
    sm_scale = (QK_NOPE_DIM + QK_ROPE_DIM) ** -0.5
    q_nope = q_nope * sm_scale
    q_rot = q_rot * sm_scale
    n_blk = s // Q_BLOCK
    qn_b = q_nope.reshape(b, n_blk, Q_BLOCK, MLA_HEADS, QK_NOPE_DIM).transpose(1, 0, 2, 3, 4)
    qr_b = q_rot.reshape(b, n_blk, Q_BLOCK, MLA_HEADS, QK_ROPE_DIM).transpose(1, 0, 2, 3, 4)

    def attend(blk):
        qn_i, qr_i = blk
        scores = (jnp.einsum('bqhd,bkhd->bhqk', qn_i, k_nope)
                  + jnp.einsum('bqhr,bkr->bhqk', qr_i, k_rot))
        p = jax.nn.softmax(scores.astype(jnp.float32), axis=-1).astype(v.dtype)
        return jnp.einsum('bhqk,bkhd->bqhd', p, v)

    o = lax.map(attend, (qn_b, qr_b))
    return o.transpose(1, 0, 2, 3, 4).reshape(b, s, MLA_HEADS * V_HEAD_DIM)

def second_inputs(seed: int = 0) -> dict:
    key = jax.random.key(seed)
    ks = jax.random.split(key, 24)
    f32 = jnp.float32

    def w(k, shape, fan_in, gain=1.0):
        return (jax.random.normal(k, shape, f32) * (gain * fan_in ** -0.5)).astype(f32)

    def gain(k, shape):
        return 1.0 + 0.02 * jax.random.normal(k, shape, f32)

    L, D = DEPTH, D_MODEL
    x = jax.random.normal(ks[0], (BATCH, SEQ, D), f32)
    c = jax.random.normal(ks[1], (BATCH, D), f32)
    offs = jax.random.randint(ks[2], (BATCH, 1), 0, 1024, dtype=jnp.int32)
    positions = (offs + jnp.arange(SEQ, dtype=jnp.int32)[None, :]).astype(jnp.int32)
    return {
        "x": x,
        "c": c,
        "positions": positions,
        "ada_w": w(ks[3], (L, D, N_ADA * D), D, 0.2),
        "ada_b": 0.02 * jax.random.normal(ks[4], (L, N_ADA * D), f32),
        "ffn1_norm": gain(ks[5], (L, D)),
        "ffn1_w_gate": w(ks[6], (L, D, D_FF), D),
        "ffn1_w_up": w(ks[7], (L, D, D_FF), D),
        "ffn1_w_down": w(ks[8], (L, D_FF, D), D_FF),
        "mix_norm": gain(ks[9], (L, D)),
        "w_in": w(ks[10], (L, D, W_IN_COLS), D),
        "q_norm": gain(ks[11], (L, Q_LORA_RANK)),
        "w_q_up": w(ks[12], (L, Q_LORA_RANK, MLA_HEADS * (QK_NOPE_DIM + QK_ROPE_DIM)), Q_LORA_RANK),
        "kv_norm": gain(ks[13], (L, KV_LORA_RANK)),
        "w_kv_up": w(ks[14], (L, KV_LORA_RANK, MLA_HEADS * (QK_NOPE_DIM + V_HEAD_DIM)), KV_LORA_RANK),
        "w_fourier_out": w(ks[15], (L, FOURIER_WIDTH, D), FOURIER_WIDTH),
        "w_mla_out": w(ks[16], (L, MLA_HEADS * V_HEAD_DIM, D), MLA_HEADS * V_HEAD_DIM),
        "w_out": w(ks[17], (L, D, D), D),
        "ffn2_norm": gain(ks[18], (L, D)),
        "ffn2_w_gate": w(ks[19], (L, D, D_FF), D),
        "ffn2_w_up": w(ks[20], (L, D, D_FF), D),
        "ffn2_w_down": w(ks[21], (L, D_FF, D), D_FF),
        "final_norm": gain(ks[22], (D,)),
    }

def second_block(x, c, positions, ada_w, ada_b, ffn1_norm, ffn1_w_gate, ffn1_w_up, ffn1_w_down,
              mix_norm, w_in, q_norm, w_q_up, kv_norm, w_kv_up, w_fourier_out, w_mla_out, w_out,
              ffn2_norm, ffn2_w_gate, ffn2_w_up, ffn2_w_down, final_norm):
    c_act = jax.nn.silu(c)
    for l in range(DEPTH):
        mod = c_act @ ada_w[l] + ada_b[l]
        (sh1, sc1, g1, sh2, sc2, g2, sh3, sc3, g3) = jnp.split(mod, N_ADA, axis=-1)

        h = modulate_2(rms_norm(x, ffn1_norm[l]), sh1, sc1)
        x = x + 0.5 * g1[:, None, :] * swiglu_2(h, ffn1_w_gate[l], ffn1_w_up[l], ffn1_w_down[l])

        h = modulate_2(rms_norm(x, mix_norm[l]), sh2, sc2)
        z = h @ w_in[l]
        u_f, q_lat, kv_lat, k_rope, gate_logits = jnp.split(
            z, [SPLIT_1, SPLIT_2, SPLIT_3, SPLIT_4], axis=-1)
        y_a = fourier_mix(u_f) @ w_fourier_out[l]
        y_b = mla_attention(q_lat, kv_lat, k_rope, positions, q_norm[l], w_q_up[l],
                            kv_norm[l], w_kv_up[l]) @ w_mla_out[l]
        gate_a, gate_b = jnp.split(jax.nn.sigmoid(gate_logits), 2, axis=-1)
        y = (gate_a * y_a + gate_b * y_b) @ w_out[l]
        x = x + g2[:, None, :] * y

        h = modulate_2(rms_norm(x, ffn2_norm[l]), sh3, sc3)
        x = x + 0.5 * g3[:, None, :] * swiglu_2(h, ffn2_w_gate[l], ffn2_w_up[l], ffn2_w_down[l])
    return rms_norm(x, final_norm)


def setup_inputs(seed=0):
    out = dict(first_inputs(seed))
    for name, value in second_inputs(seed + 1).items():
        if name != "x":
            out[name + "_2"] = value
    return out


def reference(
    x, c, w_ada, b_ada, g_pre, g_post, w_ffn_gate, w_ffn_up, w_ffn_down, w_in, g_kidx, rel_bias,
    g_out_a, g_out_b, w_out, c_2, positions_2, ada_w_2, ada_b_2, ffn1_norm_2, ffn1_w_gate_2,
    ffn1_w_up_2, ffn1_w_down_2, mix_norm_2, w_in_2, q_norm_2, w_q_up_2, kv_norm_2, w_kv_up_2,
    w_fourier_out_2, w_mla_out_2, w_out_2, ffn2_norm_2, ffn2_w_gate_2, ffn2_w_up_2,
    ffn2_w_down_2, final_norm_2,
):
    x = first_block(
        x, c, w_ada, b_ada, g_pre, g_post, w_ffn_gate, w_ffn_up, w_ffn_down, w_in, g_kidx,
        rel_bias, g_out_a, g_out_b, w_out,
    )
    return second_block(
        x, c_2, positions_2, ada_w_2, ada_b_2, ffn1_norm_2, ffn1_w_gate_2, ffn1_w_up_2,
        ffn1_w_down_2, mix_norm_2, w_in_2, q_norm_2, w_q_up_2, kv_norm_2, w_kv_up_2,
        w_fourier_out_2, w_mla_out_2, w_out_2, ffn2_norm_2, ffn2_w_gate_2, ffn2_w_up_2,
        ffn2_w_down_2, final_norm_2,
    )


_drawn_inputs = setup_inputs


def setup_inputs(seed=0):
    import zlib

    import numpy as np

    out = dict(_drawn_inputs(seed))
    spreads = {}
    factors = {'g_out_a': 5.218,
     'g_out_b': 5.179,
     'ada_b_2': 4.914,
     'ffn1_norm_2': 8.0,
     'mix_norm_2': 8.0,
     'q_norm_2': 8.0,
     'w_q_up_2': 8.0,
     'kv_norm_2': 8.0,
     'w_kv_up_2': 3.713,
     'w_mla_out_2': 3.765,
     'ffn2_norm_2': 55.033,
     'final_norm_2': 8.753}
    for name, (base, spread) in spreads.items():
        noise = np.random.default_rng([zlib.crc32(name.encode()), seed]).standard_normal(out[name].shape)
        drawn = base * np.exp(spread * noise) if base else spread * noise
        out[name] = __import__('jax').numpy.asarray(drawn.astype(out[name].dtype))
    for name, factor in factors.items():
        out[name] = (out[name] * factor).astype(out[name].dtype)
    return out
```

```python
from contextlib import ExitStack

import concourse.bass as bass
from concourse import mybir

F32 = mybir.dt.float32
F32R = mybir.dt.float32r
I32 = mybir.dt.int32
ALU = mybir.AluOpType
ACT = mybir.ActivationFunctionType
AX = mybir.AxisListType

P = 128
D = 1024
S = 256
T = S // P
KD = D // P
F = 2816
FC = 256
NC = F // FC
NB = 512
PIECE = 2048
H = 8
DH = 64
CAUSAL = 384
TOPK = 64
BUCKETS = 32
EPS = 1e-6
DONE = -3.0e38
FUTURE = -2.0e38
OFF = -1.0e30
ROUND = 12582912.0
TWO_PI = (6.28125, 0.0019350051879882812, 3.0199159819e-07)
PI = 3.1415925
SLOT_A, SLOT_B, SLOT_D = 0, 1, 2
ADA = 3072
ARENA = 18944
QK, ROPE, QH = 64, 32, 96
QL, KVL = 384, 256


def program(nc, a, out):
    ctx = ExitStack()
    with ctx:
        def sb(name, shape, dt=F32):
            return ctx.enter_context(nc.sbuf_tensor(name, shape, dt))

        def sem(name):
            return ctx.enter_context(nc.semaphore(name))

        x_res = sb("x_res", [P, T, D])
        y_row = sb("y_row", [P, T, D])
        nT = sb("nT", [P, KD, S])
        nT_hi = sb("nT_hi", [P, KD, S], F32R)
        nT_lo = sb("nT_lo", [P, KD, S], F32R)
        w_raw = sb("w_raw", [P, 3, PIECE])
        w_hi = sb("w_hi", [P, 3, PIECE], F32R)
        w_lo = sb("w_lo", [P, 3, PIECE], F32R)
        sil = sb("sil", [P, T, FC])
        h_row = sb("h_row", [P, T, FC])
        hT_hi = sb("hT_hi", [P, 2, S], F32R)
        hT_lo = sb("hT_lo", [P, 2, S], F32R)
        gate = sb("gate", [P, 2, D])
        arena = sb("arena", [P, ARENA])
        ident = sb("ident", [P, P])
        ones = sb("ones", [P, P])
        tri = sb("tri", [P, P])
        vec_rows = sb("vec_rows", [P, 2, P])
        vec_col = sb("vec_col", [P, 2, P])
        mod_col = sb("mod_col", [P, 6, 2, KD])
        c_in = sb("c_in", [P, 2, KD])
        c_act = sb("c_act", [P, 2, KD])
        stat = sb("stat", [P, 64])
        minus_half = sb("minus_half", [P, 4])
        angle = sb("angle", [P, T, 16])
        trig = sb("trig", [P, 6, T, 16])
        pos_i = sb("pos_i", [P, T], I32)
        pos_f = sb("pos_f", [P, T])
        freq = sb("freq", [P, 16])
        gki = sb("gki", [P, DH])
        ps = ctx.enter_context(nc.psum_tensor("ps", [P, 8, NB], F32))
        toe_dram = nc.dram_tensor("toe_scratch", [P * 3 * P * H], F32, kind="Internal").ap()

        def carve(at, *shape):
            n = 1
            for s in shape:
                n *= s
            assert at + n <= ARENA, (at, shape)
            v = arena[:, at:at + n]
            if len(shape) == 2:
                v = v.rearrange("p (a b) -> p a b", b=shape[1])
            if len(shape) == 3:
                v = v.rearrange("p (a b c) -> p a b c", b=shape[1], c=shape[2])
            return v

        mod_acc = carve(0, 2, ADA)
        ada_raw = carve(2 * ADA, 2, ADA)
        post_gain = carve(4 * ADA, 2, D)
        first_acc = carve(4 * ADA + 2 * D, 2 * D)
        qkT = carve(0, 5, 4, S)
        v_row = carve(5120, 2, T, NB)
        z_sb = carve(7168, H, CAUSAL)
        u_sb = carve(10240, H, CAUSAL)
        e_sb = carve(13312, H, CAUSAL)
        score = carve(16384, CAUSAL)
        work = carve(16768, CAUSAL)
        relu = carve(17152, 4, CAUSAL)
        kw_row = h_row[:, :, 0:72]
        ki2 = sil[:, :, 0:P]
        kiT = h_row[:, 0, :]
        wi = stat[:, 32:48]
        toe_bc = carve(0, H, CAUSAL)
        rel_bc = carve(3072, H, P)
        rel_in = carve(4096, H)
        onehot = carve(4104, CAUSAL)
        bias = nT
        TQI, TQB, TKB, TKA, TQA = range(5)
        sig = carve(0, T, 2 * D)
        uf = carve(4096, T, NB)
        dft = carve(5120, 2, NB)
        dftd = carve(6144, 2, P)
        cu = carve(6400, 4, NB)
        lat = carve(8448, T, QL + KVL + ROPE)
        q_row = carve(9792, T, H * QH)
        k_row = carve(11328, T, H * QH)
        kv_row = carve(12864, T, H * P)
        qT = carve(14912, H, S)
        kT = carve(4096, H, S)
        prob = carve(6144, 2, NB * 2)
        probT = carve(16960, 2, NB)

        raw_loaded = [sem(f"raw_loaded{s}") for s in range(3)]
        hi_ready = [sem(f"hi_ready{s}") for s in range(3)]
        lo_ready = [sem(f"lo_ready{s}") for s in range(3)]
        w_used = [sem(f"w_used{s}") for s in range(3)]
        small_loaded = sem("small_loaded")
        x_loaded = sem("x_loaded")
        const_ready = sem("const_ready")
        pool_step = sem("pool_step")
        c_loaded = sem("c_loaded")
        c_ready = sem("c_ready")
        vec_tr = sem("vec_tr")
        vec_ready = sem("vec_ready")
        toe_mm = sem("toe_mm")
        toe_sb = sem("toe_sb")
        toe_stored = sem("toe_stored")
        bias_loaded = sem("bias_loaded")
        rel_ready = sem("rel_ready")
        ada_loaded = [sem(f"ada_loaded{s}") for s in range(2)]
        ada_done = [sem(f"ada_done{s}") for s in range(2)]
        acc_zero = sem("acc_zero")
        acc_cols = sem("acc_cols")
        cols_out = sem("cols_out")
        acc_gate = sem("acc_gate")
        gate_out = sem("gate_out")
        gate_loaded = [sem(f"gate_loaded{s}") for s in range(2)]
        post_loaded = [sem(f"post_loaded{s}") for s in range(2)]
        sq_done = sem("sq_done")
        ki_sq = sem("ki_sq")
        rms_done = sem("rms_done")
        y_ready = sem("y_ready")
        n_tr = sem("n_tr")
        n_ready = sem("n_ready")
        n_hi = sem("n_hi")
        n_lo = sem("n_lo")
        h_done = sem("h_done")
        silu_done = sem("silu_done")
        h_ready = sem("h_ready")
        ht_tr = sem("ht_tr")
        ht_hi = sem("ht_hi")
        ht_lo = sem("ht_lo")
        down_done = sem("down_done")
        fsq_done = sem("fsq_done")
        dve_step = sem("dve_step")
        grp_out = sem("grp_out")
        out_stored = sem("out_stored")
        sp_settled = sem("sp_settled")

        def S_(n):
            return sem(n)
        ki_ready, ki_tr, kiT_ready = map(S_, ["ki_ready", "ki_tr", "kiT_ready"])
        idx_mm, idx_relu, idx_acc = map(S_, ["idx_mm", "idx_relu", "idx_acc"])
        score_causal, sel_ready, mask_ready = map(S_, ["score_causal", "sel_ready", "mask_ready"])
        z_mm, z_out, z_ln, u_ready, u_masked = map(S_, ["z_mm", "z_out", "z_ln", "u_ready", "u_masked"])
        r_mm, r_out, loga_ready, a_exp, a_masked, ob_mm, ob_out = map(
            S_, ["r_mm", "r_out", "loga_ready", "a_exp", "a_masked", "ob_mm", "ob_out"])
        l_mm, l_out, lmax_ready, p_exp, p_tr, pT_out, oa_mm, oa_out = map(
            S_, ["l_mm", "l_out", "lmax_ready", "p_exp", "p_tr", "pT_out", "oa_mm", "oa_out"])
        osq_done = sem("osq_done")
        dft_loaded, cu_mm, cu_out, f_mm, f_out, f_hi, f_lo = map(
            S_, ["dft_loaded", "cu_mm", "cu_out", "f_mm", "f_out", "f_hi", "f_lo"])
        trig_arg, trig_done, trig_ready = map(S_, ["trig_arg", "trig_done", "trig_ready"])
        lat_sq, lat_ready, lat_tr, lat_out, lat_hi, lat_lo = map(
            S_, ["lat_sq", "lat_ready", "lat_tr", "lat_out", "lat_hi", "lat_lo"])
        up_out, qk_ready, qk_tr, qkT_out = map(S_, ["up_out", "qk_ready", "qk_tr", "qkT_out"])
        ya_out, yb_out = map(S_, ["ya_out", "yb_out"])
        s_mm, smax_ready, s_exp, s_tr, sT_out, om_mm, om_out = map(
            S_, ["s_mm", "smax_ready", "s_exp", "s_tr", "sT_out", "om_mm", "om_out"])
        omT_mm, omT_out, omT_hi, omT_lo = map(S_, ["omT_mm", "omT_out", "omT_hi", "omT_lo"])

        top_found, top_taken, o_ready = map(S_, ["top_found", "top_taken", "o_ready"])
        SMALL = 16 * 15
        VECS = (104, 101)

        AB0 = {"F0": 0, "M1": NC, "F1": NC + 9, "F2": 2 * NC + 9, "M2": 3 * NC + 9, "F3": 3 * NC + 21}
        D0 = {"F0": 0, "M1": NC, "F1": NC + 1, "F2": 2 * NC + 1, "M2": 3 * NC + 1, "F3": 3 * NC + 2}
        FFN = ["F0", "F1", "F2", "F3"]
        ffn_w = {
            "F0": (a["w_ffn_gate"][0, 0], a["w_ffn_up"][0, 0], a["w_ffn_down"][0, 0]),
            "F1": (a["w_ffn_gate"][0, 1], a["w_ffn_up"][0, 1], a["w_ffn_down"][0, 1]),
            "F2": (a["ffn1_w_gate_2"][0], a["ffn1_w_up_2"][0], a["ffn1_w_down_2"][0]),
            "F3": (a["ffn2_w_gate_2"][0], a["ffn2_w_up_2"][0], a["ffn2_w_down_2"][0]),
        }
        NORM = {"F0": 0, "M1": 1, "F1": 2, "F2": 3, "M2": 4, "F3": 5, "end": 6}
        w1, w2 = a["w_ada"][0], a["ada_w_2"][0]
        ada_steps = {
            "F0": [(w1, 2 * D, 3 * D, 0), (w1, 5 * D, 3 * D, 0)],
            "F1": [(w1, 8 * D, D, 0), (w2, 0, 2 * D, 1)],
            "F2": [(w2, 2 * D, 3 * D, 1), (w2, 5 * D, 3 * D, 1)],
            "F3": [(w2, 8 * D, D, 1)],
        }
        col_sums = {
            "F0": [(D, 0, 3, 1), (2 * D, 0, 4, 1), (4 * D, 0, 6, 2), (5 * D, 0, 7, 2)],
            "F1": [(ADA, 1, 0, 3), (ADA + D, 1, 1, 3)],
            "F2": [(D, 1, 3, 4), (2 * D, 1, 4, 4), (4 * D, 1, 6, 5), (5 * D, 1, 7, 5)],
            "F3": [],
        }
        b1, b2 = a["b_ada"][0], a["ada_b_2"][0]
        gates = {
            "F0": [(0, b1[2 * D:3 * D], 0, a["g_post"][0, 0], 0.5), (3 * D, b1[5 * D:6 * D], 1, a["g_post"][0, 1], 1.0)],
            "F1": [(0, b1[8 * D:9 * D], 0, a["g_post"][0, 2], 0.5)],
            "F2": [(0, b2[2 * D:3 * D], 0, None, 0.5), (3 * D, b2[5 * D:6 * D], 1, None, 1.0)],
            "F3": [(0, b2[8 * D:9 * D], 0, None, 0.5)],
        }
        n_gates = {"F0": 0, "F1": 2, "F2": 3, "F3": 5}
        n_cols = {"F0": 1, "F1": 2, "F2": 3, "F3": 4}
        n_buf = {"F0": (0, 0), "F1": (1, 1), "F2": (2, 1), "F3": (3, 2)}
        n_ada = {"F0": (4, 4), "F1": (12, 12), "F2": (20, 20), "F3": (28, 28)}
        gain_at = {1: (0, 80), 2: (0, 88), 3: (1, 72), 4: (1, 80), 5: (1, 88)}
        w_in = a["w_in"][0].rearrange("(k p) n -> p k n", p=P)
        w_in2 = a["w_in_2"][0].rearrange("(k p) n -> p k n", p=P)
        w_out = a["w_out"][0].rearrange("(k p) n -> p k n", p=P)
        w_out2 = a["w_out_2"][0].rearrange("(k p) n -> p k n", p=P)
        GROUPS1 = [("qi", 1536), ("qb", 2120), ("kb", 2632), ("vb", 3144), ("ka", 512), ("qa", 0), ("va", 1024)]
        GROUPS2 = [("uf", 0, 512), ("q", 512, 384), ("kv", 896, 288)] + [("g", 1184 + 512 * i, 512) for i in range(4)]

        RMS = [f"F0 {t}" for t in range(T)]
        for stage, after in (("F0", "M1"), ("M1", "F1"), ("F1", "F2"), ("F2", "M2"), ("M2", "F3"), ("F3", "end")):
            if stage == "M1":
                RMS += ["index keys", "M1 out"]
            if stage == "M2":
                RMS += ["q latent", "kv latent"]
            if stage in ("F0", "M1", "F1"):
                RMS += [f"post {stage} {t}" for t in range(T)]
            RMS += [f"{after} {t}" for t in range(T)]
        TR = {"F0": 0, "M1": 1, "O1": 2, "F1": 3, "F2": 4, "M2": 5, "O2": 6, "F3": 7}

        def slot(t, s, n):
            return t[:, s, 0:n]

        def wait(e, s, v):
            if not (isinstance(v, int) and v <= 0):
                e.wait_ge(s, v)

        def x_junk(half):
            return sil[:].rearrange("p t n -> p (t n)") if half == 0 else gate[:, 0, 0:NB]

        prob4 = prob.rearrange("p a (b n) -> p (a b) n", n=NB)

        def rms_ready(e, name):
            e.wait_ge(rms_done, RMS.index(name) + 1)

        def output_ready(e, stage, t):
            if stage[0] == "F" and t == 0:
                e.wait_ge(down_done, FFN.index(stage) + 1)
            elif stage[0] == "F":
                e.wait_ge(w_used[SLOT_D], D0[stage] + NC)
            else:
                e.wait_ge(w_used[SLOT_B], AB0["F1" if stage == "M1" else "F3"])

        block = ctx.enter_context(nc.Block())

        @block.sync
        def _(sp):
            def raw_free(s, use):
                wait(sp, lo_ready[s], use)
                settle(use)

            def settle(v):
                if not isinstance(v, int):
                    sp.sem_inc(sp_settled, 1)

            def load(s, use, parts):
                raw_free(s, use)
                for dst, src in parts:
                    sp.dma_start(dst, src).then_inc(raw_loaded[s], 16)

            def load_k4(s, use, src, k0, c0, n, nk=4):
                dst = slot(w_raw, s, nk * n).rearrange("p (k n) -> p k n", n=n)
                m = nk // 2
                load(s, use, [(dst[:, 0:m], src[:, k0:k0 + m, c0:c0 + n]),
                              (dst[:, m:nk], src[:, k0 + m:k0 + nk, c0:c0 + n])])

            def load_gu(f, s, c):
                wg, wu, _ = ffn_w[f]
                dst = w_raw[:, s, :].rearrange("p (k g n) -> p k g n", g=2, n=FC)
                raw_free(s, c + AB0[f])
                for g, w in enumerate((wg, wu)):
                    src = w.rearrange("(k p) n -> p k n", p=P)[:, 4 * s:4 * s + 4, bass.ds(c * FC, FC)]
                    sp.dma_start(dst[:, :, g, :], src).then_inc(raw_loaded[s], 16)

            def load_down(f, c):
                src = ffn_w[f][2].rearrange("(c p) n -> p c n", p=P)
                dst = w_raw[:, SLOT_D, :].rearrange("p (k n) -> p k n", n=D)
                raw_free(SLOT_D, c + D0[f])
                for j in range(2):
                    sp.dma_start(dst[:, j], src[:, bass.ds(c * 2 + j, 1), :].rearrange("p a n -> p (a n)")
                                 if not isinstance(c, int) else src[:, c * 2 + j, :]).then_inc(raw_loaded[SLOT_D], 16)

            def load_ada(f, half, j):
                if half >= len(ada_steps[f]):
                    return
                w, c0, n, _ = ada_steps[f][half]
                src = w.rearrange("(p j) n -> p j n", j=KD)
                wait(sp, ada_done[half], j + n_ada[f][half])
                settle(j)
                sp.dma_start(ada_raw[:, half, 0:n], src[:, bass.ds(j, 1), c0:c0 + n].rearrange("p a n -> p (a n)")
                             if not isinstance(j, int) else src[:, j, c0:c0 + n]).then_inc(ada_loaded[half], 16)

            def ffn_loads(f, next_a, next_b):
                load_gu(f, SLOT_A, 1)
                load_gu(f, SLOT_B, 1)
                wait(sp, h_done, 2 * NORM[f])
                for i, (_, b, buf, post, _) in enumerate(gates[f]):
                    sp.dma_start(gate[:, buf, :], b.rearrange("(a n) -> a n", a=1).broadcast_to([P, D]))\
                        .then_inc(gate_loaded[buf], 16)
                    if post is not None:
                        sp.dma_start(post_gain[:, i, :], post.rearrange("(a n) -> a n", a=1).broadcast_to([P, D]))\
                            .then_inc(post_loaded[i], 16)

                def chunk(c):
                    load_down(f, c - 1)
                    load_ada(f, 0, c - 1)
                    load_ada(f, 1, c - 1)
                    load_gu(f, SLOT_A, c + 1)
                    load_gu(f, SLOT_B, c + 1)

                chunk(1)
                with sp.Fori(2, KD + 1) as c:
                    chunk(c)
                load_down(f, NC - 3)
                load_gu(f, SLOT_A, NC - 1)
                load_gu(f, SLOT_B, NC - 1)
                load_down(f, NC - 2)
                next_a()
                next_b()
                load_down(f, NC - 1)

            sp.dma_start(c_in[:, 0, :], a["c"].rearrange("a (p j) -> (a p) j", j=KD)).then_inc(c_loaded, 16)
            sp.dma_start(c_in[:, 1, :], a["c_2"].rearrange("a (p j) -> (a p) j", j=KD)).then_inc(c_loaded, 16)
            src = w1.rearrange("(p j) n -> p j n", j=KD)
            for j in range(2):
                sp.dma_start(ada_raw[:, j % 2, 0:2 * D], src[:, j, 0:2 * D]).then_inc(ada_loaded[j % 2], 16)
            for t in range(T):
                sp.dma_start(x_res[:, t, :], a["x"][0, t * P:(t + 1) * P, :]).then_inc(x_loaded, 16)
            for blk, rows in enumerate((
                [("b_ada", 72), ("g_pre", 24), ("g_out_a", 4), ("g_out_b", 4)],
                [("ada_b_2", 72), ("ffn1_norm_2", 8), ("mix_norm_2", 8), ("ffn2_norm_2", 8), ("q_norm_2", 3), ("kv_norm_2", 2)],
            )):
                at = 0
                for name, n in rows:
                    v = a[name]
                    v = v.rearrange("a b n -> (a b n)") if len(v.shape) == 3 else v.rearrange("a n -> (a n)")
                    sp.dma_start(vec_rows[at:at + n, blk, :], v.rearrange("(r q) -> r q", q=P)).then_inc(small_loaded, 16)
                    at += n
            sp.dma_start(rel_in[0:BUCKETS, :], a["rel_bias"]).then_inc(small_loaded, 16)
            sp.dma_start(onehot[0:BUCKETS, :], a["onehot"]).then_inc(small_loaded, 16)
            sp.dma_start(gki[:], a["g_kidx"].broadcast_to([P, DH])).then_inc(small_loaded, 16)
            sp.dma_start(freq[:], a["inv_freq"].broadcast_to([P, 16])).then_inc(small_loaded, 16)
            sp.dma_start(pos_i[:], a["positions_2"].rearrange("a (t p) -> p (a t)", p=P), allow_slow_non_contiguous=True)\
                .then_inc(small_loaded, 16)
            for j in range(2, KD):
                wait(sp, ada_done[j % 2], j // 2)
                sp.dma_start(ada_raw[:, j % 2, 0:2 * D], src[:, j, 0:2 * D]).then_inc(ada_loaded[j % 2], 16)
            load_gu("F0", SLOT_A, 0)
            load_gu("F0", SLOT_B, 0)
            sp.wait_ge(toe_sb, H)
            sp.dma_start(toe_dram.rearrange("(p n) -> p n", p=P), toe_bc.rearrange("p h n -> p (h n)"))\
                .then_inc(toe_stored, 16)
            m1, m2 = AB0["M1"], AB0["M2"]

            def group1(i, s):
                load_k4(s, m1 + i, w_in, 4 * s, GROUPS1[i][1], NB)

            def group2(i, s):
                load_k4(s, m2 + i, w_in2, 4 * s, GROUPS2[i][1], GROUPS2[i][2])

            sp.wait_ge(toe_stored, 16)
            ffn_loads("F0", lambda: group1(0, SLOT_A), lambda: group1(0, SLOT_B))
            raw_free(SLOT_D, D0["M1"])
            dst = slot(w_raw, SLOT_D, KD * 72).rearrange("p (k n) -> p k n", n=72)
            for j in range(2):
                sp.dma_start(dst[:, 4 * j:4 * j + 4], w_in[:, 4 * j:4 * j + 4, 2048:2120]).then_inc(raw_loaded[SLOT_D], 16)
            for i in range(1, len(GROUPS1)):
                group1(i, SLOT_A)
                group1(i, SLOT_B)
                if i == 4:
                    sp.wait_ge(n_lo, 4 * (TR["M1"] + 1))
                    pitch = H * CAUSAL
                    for h in range(H):
                        skew = bass.AP(toe_dram.tensor, toe_dram.offset + h * CAUSAL + P - 1, [[pitch - 1, P], [1, S]])
                        sp.dma_start(bias[:, h, :], skew).then_inc(bias_loaded, 16)
            for n in range(2):
                for s in (SLOT_A, SLOT_B):
                    load_k4(s, m1 + 7 + n, w_out, 4 * s, n * NB, NB)
            load_gu("F1", SLOT_A, 0)
            load_gu("F1", SLOT_B, 0)
            ffn_loads("F1", lambda: load_gu("F2", SLOT_A, 0), lambda: load_gu("F2", SLOT_B, 0))
            ffn_loads("F2", lambda: group2(0, SLOT_A), lambda: group2(0, SLOT_B))
            sp.wait_ge(h_done, 2 * NORM["M2"])
            sp.dma_start(dft[:], a["dft_s"].rearrange("(k p) n -> p k n", p=P)).then_inc(dft_loaded, 16)
            sp.dma_start(dftd[:], a["dft_d"].rearrange("p (k n) -> p k n", n=P)).then_inc(dft_loaded, 16)
            for i in range(1, len(GROUPS2)):
                group2(i, SLOT_A)
                group2(i, SLOT_B)
            wf = a["w_fourier_out_2"][0].rearrange("(k p) n -> p k n", p=P)
            wm = a["w_mla_out_2"][0].rearrange("(k p) n -> p k n", p=P)
            for w, use in ((wf, m2 + 7),):
                for s in (SLOT_A, SLOT_B):
                    load_k4(s, use, w, 0, s * NB, NB)
            wq = a["w_q_up_2"][0].rearrange("(k p) n -> p k n", p=P)
            for s in (SLOT_A, SLOT_B):
                dst = slot(w_raw, s, 3 * QL).rearrange("p (k n) -> p k n", n=QL)
                load(s, m2 + 8, [(dst[:, 0:2], wq[:, 0:2, s * QL:(s + 1) * QL]), (dst[:, 2:3], wq[:, 2:3, s * QL:(s + 1) * QL])])
            wkv = a["w_kv_up_2"][0].rearrange("(k p) n -> p k n", p=P)
            dst = w_raw[:, SLOT_D, :].rearrange("p (k n) -> p k n", n=D)
            load(SLOT_D, D0["M2"], [(dst[:, j], wkv[:, j, :]) for j in range(2)])
            for s in (SLOT_A, SLOT_B):
                load_k4(s, m2 + 9, wm, 0, s * NB, NB)
            for n in range(2):
                for s in (SLOT_A, SLOT_B):
                    load_k4(s, m2 + 10 + n, w_out2, 4 * s, n * NB, NB)
            load_gu("F3", SLOT_A, 0)
            load_gu("F3", SLOT_B, 0)
            nothing = lambda: None
            ffn_loads("F3", nothing, nothing)
            sp.wait_ge(gate_out, 12)
            sp.dma_start(post_gain[:, 0, :], a["final_norm_2"].rearrange("(a n) -> a n", a=1).broadcast_to([P, D]))\
                .then_inc(post_loaded[0], 16)
            for t in range(T):
                sp.wait_ge(y_ready, 12 + t + 1)
                sp.dma_start(out[0, t * P:(t + 1) * P, :], y_row[:, t, :]).then_inc(out_stored, 16)
            sp.wait_ge(out_stored, 16 * T)

        @block.gpsimd
        def _(pool):
            pool.memset(ones[:], 1.0).then_inc(pool_step, 1)
            pool.memset(minus_half[:], -0.5).then_inc(pool_step, 1)
            pool.wait_ge(pool_step, 2)
            pool.affine_select(out=ident[:], in_=ones[:], compare_op=ALU.is_equal, fill=0.0, base=0,
                               pattern=[[-1, P]], channel_multiplier=1).then_inc(const_ready, 1)
            pool.affine_select(out=tri[:], in_=ones[:], compare_op=ALU.is_ge, fill=0.0, base=0,
                               pattern=[[-1, P]], channel_multiplier=1).then_inc(const_ready, 1)
            pool.memset(first_acc, 0.0).then_inc(acc_zero, 1)

            def zero_acc(f):
                wait(pool, h_done, 2 * NORM[f])
                if f == "F0":
                    pool.wait_ge(toe_stored, 16)
                elif f == "F2":
                    pool.wait_ge(gate_out, 6)
                    pool.wait_ge(cols_out, 3)
                for half, (_, _, n, _) in enumerate(ada_steps[f]):
                    pool.memset(mod_acc[:, half, 0:n], 0.0).then_inc(acc_zero, 1)

            def rms(name, dst, ss, s, v):
                pool.wait_ge(s, v)
                pool.tensor_scalar(ss, ss, EPS, None, ALU.add).then_inc(pool_step, 1)
                pool.wait_ge(pool_step, 3 + len(made))
                pool.tensor_tensor(dst, ss, minus_half[:, 0:dst.shape[1]], ALU.pow).then_inc(rms_done, 1)
                made.append(name)

            def norm_rms(f):
                for t in range(T):
                    rms(f"{f} {t}", stat[:, 8 + t:9 + t], stat[:, t:t + 1], sq_done, 2 * NORM[f] + 1 + t)

            def post_rms(f):
                for t in range(T):
                    rms(f"post {f} {t}", stat[:, 10 + t:11 + t], stat[:, 2 + t:3 + t], fsq_done,
                        2 * {"F0": 0, "M1": 1, "F1": 2}[f] + 1 + t)

            made = []
            norm_rms("F0")
            zero_acc("F0")
            post_rms("F0")
            norm_rms("M1")
            rms("index keys", stat[:, 14:16], stat[:, 12:14], ki_sq, 1)

            def causal(v, reps, fill, strict_from=None):
                if strict_from is None:
                    return pool.affine_select(out=v, in_=v, compare_op=ALU.is_ge, fill=fill, base=0,
                                              pattern=[[0, reps], [-1, P]], channel_multiplier=1)
                return pool.affine_select(out=v, in_=v, compare_op=ALU.is_ge, fill=fill, base=-1,
                                          pattern=[[0, reps], [1, P]], channel_multiplier=-1)

            diag = lambda v: v[:, P:CAUSAL].rearrange("p (r x) -> p r x", x=P)
            pool.wait_ge(idx_acc, 2 * H)
            causal(diag(score), 2, FUTURE).then_inc(score_causal, 1)
            pool.wait_ge(u_ready, 1)
            for c0 in (0, 2 * P):
                causal(u_sb[:, :, c0:c0 + P], H, 0.0, True).then_inc(u_masked, 1)
            pool.wait_ge(sel_ready, 1)
            causal(diag(work), 2, OFF).then_inc(mask_ready, 1)
            pool.wait_ge(a_exp, 1)
            for c0 in (0, 2 * P):
                causal(z_sb[:, :, c0:c0 + P], H, 0.0, True).then_inc(a_masked, 1)
            rms("M1 out", stat[:, 48:52], stat[:, 4:8], osq_done, 4)
            post_rms("M1")
            norm_rms("F1")
            zero_acc("F1")
            post_rms("F1")
            norm_rms("F2")
            zero_acc("F2")
            norm_rms("M2")
            rms("q latent", stat[:, 48:50], stat[:, 4:6], lat_sq, 4)
            rms("kv latent", stat[:, 50:52], stat[:, 6:8], lat_sq, 4)
            norm_rms("F3")
            zero_acc("F3")
            norm_rms("end")
            assert made == RMS

        @block.scalar
        def _(act):
            copy = lambda o, i: act.activation(o, i, ACT.Copy)

            def split_hi(s, use, n=PIECE):
                act.wait_ge(raw_loaded[s], use * 32 + 32)
                wait(act, w_used[s], use)
                copy(slot(w_hi, s, n), slot(w_raw, s, n)).then_inc(hi_ready[s], 1)

            def norm(f):
                r = NORM[f]
                for t in range(T):
                    if r:
                        act.wait_ge(h_done, 2 * r - 1 + t)
                    else:
                        act.wait_ge(x_loaded, 16 * T)
                    act.activation(y_row[:, t, :], x_res[:, t, :], ACT.Square, scale=D ** -0.5, accum_out=stat[:, t:t + 1]).then_inc(sq_done, 1)
                norm_hi(TR[f])

            def norm_hi(r):
                for j in range(KD // 2):
                    act.wait_ge(n_ready, 8 * r + 2 * j + 2)
                    copy(nT_hi[:, 2 * j:2 * j + 2, :], nT[:, 2 * j:2 * j + 2, :]).then_inc(n_hi, 1)

            def body(f, c, down=True, gu=True, nxt=PIECE):
                i = FFN.index(f) * NC
                if down:
                    split_hi(SLOT_D, c - 1 + D0[f])
                    act.wait_ge(ht_tr, c + i)
                    copy(hT_hi[:], ps[:, 2, :].rearrange("p (k n) -> p k n", n=S)).then_inc(ht_hi, 1)
                if nxt:
                    split_hi(SLOT_A, c + 1 + AB0[f], nxt)
                if gu:
                    act.wait_ge(w_used[SLOT_B], c + 1 + AB0[f])
                    for t in range(T):
                        wait(act, h_ready, 2 * c + 2 * i - 1 + t)
                        act.activation(sil[:, t, :], ps[:, t, 0:FC], ACT.Silu).then_inc(silu_done, 1)
                if nxt:
                    split_hi(SLOT_B, c + 1 + AB0[f], nxt)

            def ffn(f, nxt=PIECE):
                norm(f)
                body(f, 0, down=False)
                body(f, 1)
                with act.Fori(2, NC - 1) as c:
                    body(f, c)
                body(f, NC - 1, nxt=nxt)
                body(f, NC, gu=False, nxt=0)

            def residual_sq(stage):
                for t in range(T):
                    output_ready(act, stage, t)
                    act.activation(y_row[:, t, :], ps[:, 4 + 2 * t:6 + 2 * t, :].rearrange("p b n -> p (b n)"),
                                   ACT.Square, scale=D ** -0.5, accum_out=stat[:, 2 + t:3 + t]).then_inc(fsq_done, 1)

            act.wait_ge(c_loaded, 32)
            act.activation(c_act[:], c_in[:], ACT.Silu).then_inc(c_ready, 1)
            for h in range(H):
                act.wait_ge(toe_mm, h + 1)
                copy(toe_bc[:, h, :], ps[:, h % 4, 0:CAUSAL]).then_inc(toe_sb, 1)
            split_hi(SLOT_A, 0)
            split_hi(SLOT_B, 0)
            ffn("F0")
            residual_sq("F0")
            norm("M1")

            m1 = AB0["M1"]

            def transposed_group(g, i):
                act.wait_ge(w_used[SLOT_B], m1 + g + 1)
                for b in range(2):
                    copy(qkT[:, i, 2 * b:2 * b + 2, :],
                         ps[:, 2 * (g % 2) + b, :].rearrange("p (k n) -> p k n", n=S)).then_inc(grp_out, 1)

            def row_group(g, i):
                act.wait_ge(w_used[SLOT_B], m1 + g + 1)
                for t in range(T):
                    copy(v_row[:, i, t, :], ps[:, 2 * (g % 2) + t, :]).then_inc(grp_out, 1)

            split_hi(SLOT_D, D0["M1"], KD * 72)
            split_hi(SLOT_A, m1 + 1)
            split_hi(SLOT_B, m1 + 1)
            transposed_group(0, TQI)
            split_hi(SLOT_A, m1 + 2)
            split_hi(SLOT_B, m1 + 2)
            transposed_group(1, TQB)
            for h in range(H):
                act.wait_ge(idx_mm, h + 1)
                if h >= 4:
                    act.wait_ge(idx_acc, 2 * (h - 3))
                act.activation(relu[:, h % 4, :], ps[:, 4 + h % 4, 0:CAUSAL], ACT.Relu).then_inc(idx_relu, 1)
            split_hi(SLOT_A, m1 + 3)
            split_hi(SLOT_B, m1 + 3)
            transposed_group(2, TKB)
            for h in range(H):
                act.wait_ge(z_mm, h + 1)
                act.activation(z_sb[:, h, :], ps[:, 4 + h % 4, 0:CAUSAL], ACT.Copy, scale=DH ** -0.5).then_inc(z_out, 1)
            split_hi(SLOT_A, m1 + 4)
            split_hi(SLOT_B, m1 + 4)
            row_group(3, 1)
            act.wait_ge(z_out, H)
            act.activation(e_sb[:], z_sb[:], ACT.Abs).then_inc(z_ln, 1)
            act.wait_ge(z_ln, 1)
            act.activation(e_sb[:], e_sb[:], ACT.Exp, scale=-1.0).then_inc(z_ln, 1)
            act.wait_ge(z_ln, 2)
            act.activation(e_sb[:], e_sb[:], ACT.Ln, bias=1.0).then_inc(z_ln, 1)
            split_hi(SLOT_A, m1 + 5)
            split_hi(SLOT_B, m1 + 5)
            transposed_group(4, TKA)
            split_hi(SLOT_A, m1 + 6)
            act.wait_ge(loga_ready, 1)
            act.activation(z_sb[:], z_sb[:], ACT.Exp).then_inc(a_exp, 1)
            split_hi(SLOT_B, m1 + 6)
            transposed_group(5, TQA)
            split_hi(SLOT_A, m1 + 7)
            split_hi(SLOT_B, m1 + 7)
            row_group(6, 0)
            for h in range(H):
                for t in range(T):
                    act.wait_ge(lmax_ready, h + 1)
                    cols = slice(0, S) if t else slice(S, CAUSAL)
                    act.activation(z_sb[:, h, cols], z_sb[:, h, cols], ACT.Exp,
                                   bias=stat[:, 16 + 2 * h + t:17 + 2 * h + t],
                                   accum_out=trig[:, 0, t, h:h + 1]).then_inc(p_exp, 1)
                if h >= 1:
                    act.wait_ge(p_tr, h)
                    copy(e_sb[:, h - 1, :], ps[:, 4 + (h - 1) % 4, 0:CAUSAL]).then_inc(pT_out, 1)
            act.wait_ge(p_tr, H)
            copy(e_sb[:, H - 1, :], ps[:, 4 + (H - 1) % 4, 0:CAUSAL]).then_inc(pT_out, 1)
            act.wait_ge(ob_out, T)
            act.wait_ge(oa_out, T)
            for t in range(T):
                for half in range(2):
                    wait(act, osq_done, 2 * t + half - 1)
                    act.activation(x_junk(half), y_row[:, t, half * NB:(half + 1) * NB], ACT.Square, scale=NB ** -0.5,
                                   accum_out=stat[:, 4 + 2 * t + half:5 + 2 * t + half]).then_inc(osq_done, 1)
            norm_hi(TR["O1"])
            split_hi(SLOT_A, m1 + 8)
            split_hi(SLOT_B, m1 + 8)
            split_hi(SLOT_A, AB0["F1"])
            split_hi(SLOT_B, AB0["F1"])
            residual_sq("M1")
            ffn("F1")
            residual_sq("F1")
            ffn("F2")
            norm("M2")

            m2 = AB0["M2"]

            def row_out(g, dst, n):
                act.wait_ge(w_used[SLOT_B], m2 + g + 1)
                for t in range(T):
                    copy(dst[:, t], ps[:, 2 * (g % 2) + t, 0:n]).then_inc(grp_out, 1)

            split_hi(SLOT_A, m2 + 1, 4 * 384)
            split_hi(SLOT_B, m2 + 1, 4 * 384)
            row_out(0, uf, NB)
            split_hi(SLOT_A, m2 + 2, 4 * 288)
            split_hi(SLOT_B, m2 + 2, 4 * 288)
            row_out(1, lat[:, :, 0:QL], QL)
            split_hi(SLOT_A, m2 + 3)
            split_hi(SLOT_B, m2 + 3)
            row_out(2, lat[:, :, QL:], KVL + ROPE)
            act.wait_ge(grp_out, 14 + 6)
            for t in range(T):
                wait(act, lat_sq, 2 * t)
                act.activation(x_junk(0)[:, 0:QL], lat[:, t, 0:QL], ACT.Square, scale=QL ** -0.5,
                               accum_out=stat[:, 4 + t:5 + t]).then_inc(lat_sq, 1)
                act.activation(x_junk(1)[:, 0:KVL], lat[:, t, QL:QL + KVL], ACT.Square, scale=KVL ** -0.5,
                               accum_out=stat[:, 6 + t:7 + t]).then_inc(lat_sq, 1)
            act.wait_ge(trig_arg, 1)
            act.activation(trig[:, 1], trig[:, 0], ACT.Sin).then_inc(trig_done, 1)
            act.activation(trig[:, 2], trig[:, 0], ACT.Sin, scale=0.5).then_inc(trig_done, 1)
            split_hi(SLOT_A, m2 + 4)
            for g in range(4):
                act.wait_ge(cu_mm, g + 1)
                copy(cu[:, g, :], ps[:, 4 + g, :]).then_inc(cu_out, 1)
            split_hi(SLOT_B, m2 + 4)

            def gate_group(i):
                act.wait_ge(w_used[SLOT_B], m2 + 3 + i + 1)
                for t in range(T):
                    act.activation(sig[:, t, i * NB:(i + 1) * NB], ps[:, 2 * ((3 + i) % 2) + t, :], ACT.Sigmoid).then_inc(grp_out, 1)

            gate_group(0)
            split_hi(SLOT_A, m2 + 5)
            split_hi(SLOT_B, m2 + 5)
            gate_group(1)
            split_hi(SLOT_A, m2 + 6)
            split_hi(SLOT_B, m2 + 6)
            gate_group(2)
            split_hi(SLOT_A, m2 + 7)
            split_hi(SLOT_B, m2 + 7)
            split_hi(SLOT_D, D0["M2"])
            gate_group(3)
            act.wait_ge(w_used[SLOT_B], m2 + 7)
            act.wait_ge(f_out, 4)
            copy(nT_hi[:, 4:8, :], nT[:, 4:8, :]).then_inc(f_hi, 1)
            act.wait_ge(lat_out, 5)
            copy(nT_hi[:, 0:3, :], nT[:, 0:3, :]).then_inc(lat_hi, 1)
            copy(hT_hi[:], h_row[:]).then_inc(lat_hi, 1)
            split_hi(SLOT_A, m2 + 8, 3 * QL)
            split_hi(SLOT_B, m2 + 8, 3 * QL)
            act.wait_ge(w_used[SLOT_D], D0["M2"] + 1)
            for t in range(T):
                for n in range(2):
                    copy(kv_row[:, t, n * NB:(n + 1) * NB], ps[:, 2 * t + n, :]).then_inc(up_out, 1)
            split_hi(SLOT_A, m2 + 9)
            split_hi(SLOT_B, m2 + 9)
            for i in range(8):
                act.wait_ge(qk_tr, i + 1)
                dst = kT if i < 4 else qT
                copy(dst[0:QH, 2 * (i % 4):2 * (i % 4) + 2, :],
                     ps[0:QH, i % 4, :].rearrange("p (k n) -> p k n", n=S)).then_inc(qkT_out, 1)
            for h in range(H):
                act.wait_ge(smax_ready, h + 1)
                if h >= 4:
                    act.wait_ge(s_tr, h - 3)
                for t in range(T):
                    act.activation(prob4[:, h % 4, t * S:(t + 1) * S], ps[:, (4, 5, 2, 3)[h % 4], t * S:(t + 1) * S], ACT.Exp,
                                   bias=stat[:, 16 + 2 * h + t:17 + 2 * h + t],
                                   accum_out=trig[:, 0, t, h:h + 1]).then_inc(s_exp, 1)
            act.wait_ge(omT_out, 4)
            copy(nT_hi[:, 0:4, :], nT[:, 0:4, :]).then_inc(omT_hi, 1)
            split_hi(SLOT_A, m2 + 10)
            split_hi(SLOT_B, m2 + 10)
            norm_hi(TR["O2"])
            split_hi(SLOT_A, m2 + 11)
            split_hi(SLOT_B, m2 + 11)
            split_hi(SLOT_A, AB0["F3"])
            split_hi(SLOT_B, AB0["F3"])
            ffn("F3", nxt=0)
            for t in range(T):
                act.wait_ge(h_done, 11 + t)
                act.activation(y_row[:, t, :], x_res[:, t, :], ACT.Square, scale=D ** -0.5, accum_out=stat[:, t:t + 1]).then_inc(sq_done, 1)

        @block.vector
        def _(dve):
            steps = [0]

            def link(ins):
                steps[0] += 1
                ins.then_inc(dve_step, 1)
                dve.wait_ge(dve_step, steps[0])

            def split_lo(s, use, n=PIECE):
                dve.wait_ge(hi_ready[s], use + 1)
                dve.tensor_tensor(slot(w_lo, s, n), slot(w_raw, s, n), slot(w_hi, s, n).bitcast(F32),
                                  ALU.subtract).then_inc(lo_ready[s], 1)

            def norm(f):
                r = NORM[f]
                for t in range(T):
                    rms_ready(dve, f"{f} {t}")
                    dve.tensor_scalar(y_row[:, t, :], x_res[:, t, :], stat[:, 8 + t:9 + t], None, ALU.mult).then_inc(y_ready, 1)
                if r == 0:
                    first_mods()
                cols = mod_col[:, r]
                norm_out(TR[f], lambda k, src: (dve.tensor_scalar(nT[:, k, :], src, cols[:, 0, k:k + 1], cols[:, 1, k:k + 1],
                                                              ALU.mult, ALU.add)))

            def norm_out(r, scaled):
                def lo(j):
                    dve.wait_ge(n_hi, 4 * r + j + 1)
                    dve.tensor_tensor(nT_lo[:, 2 * j:2 * j + 2, :], nT[:, 2 * j:2 * j + 2, :],
                                      nT_hi[:, 2 * j:2 * j + 2, :].bitcast(F32), ALU.subtract).then_inc(n_lo, 1)
                for j in range(KD // 2):
                    dve.wait_ge(n_tr, 4 * r + j + 1)
                    for k in (2 * j, 2 * j + 1):
                        scaled(k, ps[:, 4 + j, (k % 2) * S:(k % 2 + 1) * S]).then_inc(n_ready, 1)
                    if j:
                        lo(j - 1)
                lo(KD // 2 - 1)

            def cols_out_(sums, n):
                dve.wait_ge(acc_cols, n + 1)
                for i, (_, blk, m, r) in enumerate(sums):
                    src = ps[:, 3, KD * i:KD * i + KD]
                    b = vec_col[:, blk, KD * m:KD * m + KD]
                    if m % 3 == 0:
                        last = dve.tensor_tensor(mod_col[:, r, 1, :], src, b, ALU.add)
                        link(last)
                    else:
                        g = gain_at.get(r, (0, 72))
                        link(dve.tensor_tensor(mod_col[:, r, 0, :], src, b, ALU.add))
                        link(dve.scalar_tensor_tensor(mod_col[:, r, 0, :], mod_col[:, r, 0, :], 1.0,
                                                      vec_col[:, g[0], g[1]:g[1] + KD], ALU.add, ALU.mult))
                dve.sem_inc(cols_out, 1)

            def gate_half(f, i, half):
                _, _, buf, post, factor = gates[f][i]
                n = 2 * (n_gates[f] + i) + half
                v = gate[:, buf, half * NB:(half + 1) * NB]
                dve.wait_ge(gate_loaded[buf], 16 * (n_buf[f][buf] + 1))
                dve.wait_ge(acc_gate, n + 1)
                link(dve.tensor_tensor(v, ps[:, 3, :], v, ALU.add))
                if post is None:
                    dve.tensor_scalar(v, v, factor, None, ALU.mult).then_inc(gate_out, 1)
                else:
                    dve.wait_ge(post_loaded[i], 16 * {"F0": 1, "F1": 2}[f])
                    dve.scalar_tensor_tensor(v, v, factor, post_gain[:, i, half * NB:(half + 1) * NB],
                                             ALU.mult, ALU.mult).then_inc(gate_out, 1)

            def ada(f, half, j):
                if half >= len(ada_steps[f]):
                    return
                _, _, n, blk = ada_steps[f][half]
                dve.wait_ge(ada_loaded[half], j * 16 + 16 * (n_ada[f][half] + 1))
                wait(dve, ada_done[half], j + n_ada[f][half])
                cj = c_act[:, blk, bass.ds(j, 1)] if not isinstance(j, int) else c_act[:, blk, j:j + 1]
                dve.scalar_tensor_tensor(mod_acc[:, half, 0:n], ada_raw[:, half, 0:n], cj, mod_acc[:, half, 0:n],
                                         ALU.mult, ALU.add).then_inc(ada_done[half], 1)

            def body(f, c, down=True, gu=True, nxt=PIECE, mods=False, hooks=((), (), ())):
                i = FFN.index(f) * NC
                if down:
                    split_lo(SLOT_D, c - 1 + D0[f])
                    for hook in hooks[0]:
                        hook()
                    if mods:
                        ada(f, 0, c - 1)
                    dve.wait_ge(ht_hi, c + i)
                    dve.tensor_tensor(hT_lo[:], ps[:, 2, :].rearrange("p (k n) -> p k n", n=S),
                                      hT_hi[:].bitcast(F32), ALU.subtract).then_inc(ht_lo, 1)
                    for hook in hooks[1]:
                        hook()
                    if mods:
                        ada(f, 1, c - 1)
                if nxt:
                    split_lo(SLOT_A, c + 1 + AB0[f], nxt)
                if gu:
                    for t in range(T):
                        dve.wait_ge(silu_done, 2 * c + 2 * i + 1 + t)
                        wait(dve, ht_tr, c + i)
                        dve.tensor_tensor(h_row[:, t, :], ps[:, t, FC:2 * FC], sil[:, t, :], ALU.mult).then_inc(h_ready, 1)
                if nxt:
                    split_lo(SLOT_B, c + 1 + AB0[f], nxt)
                for hook in hooks[2]:
                    hook()

            def ffn(f, nxt=PIECE):
                norm(f)
                body(f, 0, down=False)
                dve.wait_ge(acc_zero, 1 + {"F0": 2, "F1": 4, "F2": 6, "F3": 7}[f])
                with dve.Fori(1, KD + 1) as c:
                    body(f, c, mods=True)
                g = [lambda i=i, h=h: gate_half(f, i, h) for i in range(len(gates[f])) for h in range(2)]
                body(f, NC - 2, hooks=((), [lambda: cols_out_(col_sums[f], n_cols[f])] if col_sums[f] else (), g[0:1]))
                body(f, NC - 1, nxt=nxt, hooks=((), g[1:2], g[2:3]))
                body(f, NC, gu=False, nxt=0, hooks=((), g[3:4], ()))

            def residual(stage, buf, post):
                for t in range(T):
                    src = ps[:, 4 + 2 * t:6 + 2 * t, :].rearrange("p b n -> p (b n)")
                    if post:
                        rms_ready(dve, f"post {stage} {t}")
                        link(dve.scalar_tensor_tensor(y_row[:, t, :], src, stat[:, 10 + t:11 + t], gate[:, buf, :],
                                                      ALU.mult, ALU.mult))
                    else:
                        output_ready(dve, stage, t)
                        link(dve.tensor_tensor(y_row[:, t, :], src, gate[:, buf, :], ALU.mult))
                    dve.tensor_tensor(x_res[:, t, :], x_res[:, t, :], y_row[:, t, :], ALU.add).then_inc(h_done, 1)

            def first_mods():
                dve.wait_ge(vec_tr, 1)
                for b in range(2):
                    dve.tensor_copy(vec_col[:, b, 0:VECS[b]], ps[:, 7, b * P:b * P + VECS[b]]).then_inc(vec_ready, 1)
                dve.wait_ge(vec_ready, 2)
                cols_out_([(0, 0, 0, 0), (D, 0, 1, 0)], 0)

            dve.wait_ge(c_ready, 1)
            dve.wait_ge(acc_zero, 1)
            for j in range(KD):
                dve.wait_ge(ada_loaded[j % 2], 16 * (j // 2 + 1))
                if j:
                    dve.wait_ge(ada_done[(j - 1) % 2], (j - 1) // 2 + 1)
                dve.scalar_tensor_tensor(first_acc, ada_raw[:, j % 2, 0:2 * D], c_act[:, 0, j:j + 1], first_acc,
                                         ALU.mult, ALU.add).then_inc(ada_done[j % 2], 1)
                if j == 2:
                    dve.wait_ge(small_loaded, SMALL)
                    dve.tensor_copy(rel_bc[0:BUCKETS], rel_in[0:BUCKETS, :].rearrange("p (h o) -> p h o", o=1)
                                    .broadcast_to([BUCKETS, H, P])).then_inc(rel_ready, 1)
            split_lo(SLOT_A, 0)
            split_lo(SLOT_B, 0)
            ffn("F0")
            residual("F0", 0, True)

            m1 = AB0["M1"]
            norm("M1")
            split_lo(SLOT_D, D0["M1"], KD * 72)
            split_lo(SLOT_A, m1 + 1)
            split_lo(SLOT_B, m1 + 1)
            dve.wait_ge(w_used[SLOT_D], D0["M1"] + 1)
            for t in range(T):
                link(dve.tensor_copy(kw_row[:, t, :], ps[:, 4 + t, 0:72]))
                link(dve.tensor_scalar(wi[:, t * H:(t + 1) * H], kw_row[:, t, 64:72], (H * DH) ** -0.5, None, ALU.mult))
            link(dve.scalar_tensor_tensor(ki2[:, :, 0:DH], kw_row[:, :, 0:DH], 1.0 / DH, kw_row[:, :, 0:DH], ALU.mult, ALU.mult))
            dve.tensor_reduce(stat[:, 12:14], ki2[:, :, 0:DH], AX.X, ALU.add).then_inc(ki_sq, 1)
            rms_ready(dve, "index keys")
            for t in range(T):
                for half in range(2):
                    link(dve.scalar_tensor_tensor(ki2[:, t, half * DH:(half + 1) * DH], kw_row[:, t, 0:DH], stat[:, 14 + t:15 + t],
                                                  gki[:], ALU.mult, ALU.mult))
            dve.sem_inc(ki_ready, 1)
            split_lo(SLOT_A, m1 + 2)
            split_lo(SLOT_B, m1 + 2)
            dve.wait_ge(ki_tr, 1)
            dve.tensor_copy(kiT[:], ps[:, 6, 0:S]).then_inc(kiT_ready, 1)
            for h in range(H):
                dve.wait_ge(idx_relu, h + 1)
                for t in (1, 0):
                    cols = slice(0, S) if t else slice(S, CAUSAL)
                    w = wi[:, t * H + h:t * H + h + 1]
                    if h == 0:
                        dve.tensor_scalar(score[:, cols], relu[:, 0, cols], w, None, ALU.mult).then_inc(idx_acc, 1)
                    else:
                        dve.wait_ge(idx_acc, 2 * h)
                        dve.scalar_tensor_tensor(score[:, cols], relu[:, h % 4, cols], w, score[:, cols],
                                                 ALU.mult, ALU.add).then_inc(idx_acc, 1)
            split_lo(SLOT_A, m1 + 3)
            split_lo(SLOT_B, m1 + 3)
            dve.wait_ge(score_causal, 1)

            def topk(first, last):
                for r in range(first, last):
                    for t in (1, 0):
                        cols = slice(0, S) if t else slice(S, CAUSAL)
                        src = score if r == 0 else work
                        dve.max(stat[:, 48 + 8 * t:56 + 8 * t], src[:, cols]).then_inc(top_found, 1)
                    for t in (1, 0):
                        cols = slice(0, S) if t else slice(S, CAUSAL)
                        src = score if r == 0 else work
                        dve.wait_ge(top_found, 2 * r + 2 - t)
                        dve.match_replace(out=work[:, cols], in_to_replace=stat[:, 48 + 8 * t:56 + 8 * t],
                                          in_values=src[:, cols], imm_value=DONE).then_inc(top_taken, 1)
                    dve.wait_ge(top_taken, 2 * r + 2)

            topk(0, 4)
            split_lo(SLOT_A, m1 + 4)
            split_lo(SLOT_B, m1 + 4)
            topk(4, TOPK // 8)
            dve.tensor_scalar(work[:], work[:], DONE, OFF, ALU.not_equal, ALU.mult).then_inc(sel_ready, 1)
            dve.wait_ge(z_ln, 3)
            dve.scalar_tensor_tensor(u_sb[:], z_sb[:], 0.0, e_sb[:], ALU.max, ALU.add).then_inc(u_ready, 1)
            split_lo(SLOT_A, m1 + 5)
            split_lo(SLOT_B, m1 + 5)
            for h in range(H):
                dve.wait_ge(r_mm, h + 1)
                dve.tensor_tensor(z_sb[:, h, :], z_sb[:, h, :], ps[:, 4 + h % 4, 0:CAUSAL], ALU.subtract).then_inc(r_out, 1)
            dve.wait_ge(r_out, H)
            dve.tensor_scalar(z_sb[:], z_sb[:], 0.0, None, ALU.min).then_inc(loga_ready, 1)
            split_lo(SLOT_A, m1 + 6)
            split_lo(SLOT_B, m1 + 6)
            dve.wait_ge(bias_loaded, 16 * H)
            dve.wait_ge(mask_ready, 1)
            dve.wait_ge(r_mm, H)
            for cols, src in ((slice(0, S), bias[:, :, :]), (slice(S, CAUSAL), bias[:, :, P:S])):
                w = work[:, cols]
                n = w.shape[1]
                link(dve.tensor_tensor(u_sb[:, :, cols], src, w.rearrange("p (o n) -> p o n", o=1).broadcast_to([P, H, n]), ALU.add))
            for t in range(T):
                dve.wait_ge(ob_mm, 1)
                dve.tensor_copy(y_row[:, t, NB:2 * NB], ps[:, 4 + t, :]).then_inc(ob_out, 1)
            split_lo(SLOT_A, m1 + 7)
            split_lo(SLOT_B, m1 + 7)
            dve.wait_ge(ob_mm, 1)
            for h in range(H):
                dve.wait_ge(l_mm, h + 1)
                link(dve.scalar_tensor_tensor(z_sb[:, h, :], ps[:, 4 + h % 4, 0:CAUSAL], DH ** -0.5, u_sb[:, h, :],
                                              ALU.mult, ALU.add))
                dve.sem_inc(l_out, 1)
                for t in range(T):
                    cols = slice(0, S) if t else slice(S, CAUSAL)
                    m = stat[:, 16 + 2 * h + t:17 + 2 * h + t]
                    link(dve.tensor_reduce(m, z_sb[:, h, cols], AX.X, ALU.max, negate=True))
                dve.sem_inc(lmax_ready, 1)
            dve.wait_ge(p_exp, 2 * H)
            link(dve.reciprocal(trig[:, 1, :, 0:H], trig[:, 0, :, 0:H]))
            dve.wait_ge(oa_mm, 1)
            for t in range(T):
                rs = trig[:, 1, t, 0:H].rearrange("p (h o) -> p h o", o=1).broadcast_to([P, H, DH])
                dve.tensor_tensor(y_row[:, t, 0:NB].rearrange("p (h d) -> p h d", d=DH),
                                  ps[:, t, :].rearrange("p (h d) -> p h d", d=DH), rs, ALU.mult).then_inc(oa_out, 1)
            rms_ready(dve, "M1 out")
            for t in range(T):
                for half in range(2):
                    v = y_row[:, t, half * NB:(half + 1) * NB]
                    link(dve.tensor_scalar(v, v, stat[:, 48 + 2 * t + half:49 + 2 * t + half], None, ALU.mult))
            dve.sem_inc(o_ready, 1)
            norm_out(TR["O1"], lambda k, src: dve.tensor_scalar(nT[:, k, :], src, vec_col[:, 0, 96 + k:97 + k], None, ALU.mult))
            split_lo(SLOT_A, m1 + 8)
            split_lo(SLOT_B, m1 + 8)
            split_lo(SLOT_A, AB0["F1"])
            split_lo(SLOT_B, AB0["F1"])
            residual("M1", 1, True)
            ffn("F1")
            residual("F1", 0, True)
            ffn("F2")
            residual("F2", 0, False)

            m2 = AB0["M2"]
            norm("M2")
            link(dve.tensor_copy(pos_f[:], pos_i[:]))
            for t in range(T):
                link(dve.tensor_scalar(angle[:, t, :], freq[:], pos_f[:, t:t + 1], None, ALU.mult))
            link(dve.tensor_scalar(trig[:, 3], angle[:], 0.15915494309189535, ROUND, ALU.mult, ALU.add))
            link(dve.tensor_scalar(trig[:, 3], trig[:, 3], ROUND, None, ALU.subtract))
            for part in TWO_PI:
                link(dve.scalar_tensor_tensor(angle[:], trig[:, 3], -part, angle[:], ALU.mult, ALU.add))
            dve.tensor_scalar(trig[:, 0], angle[:], PI, -PI, ALU.min, ALU.max).then_inc(trig_arg, 1)
            split_lo(SLOT_A, m2 + 1, 4 * 384)
            split_lo(SLOT_B, m2 + 1, 4 * 384)
            split_lo(SLOT_A, m2 + 2, 4 * 288)
            split_lo(SLOT_B, m2 + 2, 4 * 288)
            split_lo(SLOT_A, m2 + 3)
            split_lo(SLOT_B, m2 + 3)
            dve.wait_ge(trig_done, 2)
            link(dve.tensor_tensor(trig[:, 4], trig[:, 2], trig[:, 2], ALU.mult))
            link(dve.tensor_scalar(trig[:, 4], trig[:, 4], -2.0, 1.0, ALU.mult, ALU.add))
            rms_ready(dve, "kv latent")
            for t in range(T):
                dve.tensor_scalar(lat[:, t, 0:QL], lat[:, t, 0:QL], stat[:, 48 + t:49 + t], None, ALU.mult).then_inc(lat_ready, 1)
                dve.tensor_scalar(lat[:, t, QL:QL + KVL], lat[:, t, QL:QL + KVL], stat[:, 50 + t:51 + t], None, ALU.mult)\
                    .then_inc(lat_ready, 1)
            split_lo(SLOT_A, m2 + 4)
            split_lo(SLOT_B, m2 + 4)
            split_lo(SLOT_A, m2 + 5)
            split_lo(SLOT_B, m2 + 5)
            dve.wait_ge(f_mm, 1)
            for g in range(4):
                dve.tensor_copy(nT[:, 4 + g, :], ps[:, 4 + g // 2, (g % 2) * S:(g % 2 + 1) * S]).then_inc(f_out, 1)
            split_lo(SLOT_A, m2 + 6)
            split_lo(SLOT_B, m2 + 6)
            dve.wait_ge(lat_tr, 1)
            for k in range(5):
                src = ps[:, (6, 6, 7, 7, 4)[k], (k % 2) * S:(k % 2 + 1) * S]
                dst = nT[:, k, :] if k < 3 else h_row[:, k - 3, :]
                dve.tensor_scalar(dst, src, vec_col[:, 1, 96 + k:97 + k], None, ALU.mult).then_inc(lat_out, 1)
            split_lo(SLOT_A, m2 + 7)
            split_lo(SLOT_B, m2 + 7)
            split_lo(SLOT_D, D0["M2"])
            dve.wait_ge(f_hi, 1)
            dve.tensor_tensor(nT_lo[:, 4:8, :], nT[:, 4:8, :], nT_hi[:, 4:8, :].bitcast(F32), ALU.subtract).then_inc(f_lo, 1)
            dve.wait_ge(lat_hi, 2)
            dve.tensor_tensor(nT_lo[:, 0:3, :], nT[:, 0:3, :], nT_hi[:, 0:3, :].bitcast(F32), ALU.subtract).then_inc(lat_lo, 1)
            dve.tensor_tensor(hT_lo[:], h_row[:], hT_hi[:].bitcast(F32), ALU.subtract).then_inc(lat_lo, 1)
            dve.wait_ge(grp_out, 28)
            dve.wait_ge(w_used[SLOT_B], m2 + 8)
            for t in range(T):
                dve.tensor_tensor(sig[:, t, 0:D], ps[:, 4 + 2 * t:6 + 2 * t, :].rearrange("p b n -> p (b n)"),
                                  sig[:, t, 0:D], ALU.mult).then_inc(ya_out, 1)
            split_lo(SLOT_A, m2 + 8, 3 * QL)
            split_lo(SLOT_B, m2 + 8, 3 * QL)
            cos, sin = trig[:, 4], trig[:, 1]

            def rotate(x1, x2, o1, o2, tmp, co, si):
                link(dve.tensor_tensor(tmp[:, 0], x1, co, ALU.mult))
                link(dve.tensor_tensor(tmp[:, 1], x2, si, ALU.mult))
                link(dve.tensor_tensor(tmp[:, 2], x2, co, ALU.mult))
                link(dve.tensor_tensor(tmp[:, 3], x1, si, ALU.mult))
                link(dve.tensor_tensor(o1, tmp[:, 0], tmp[:, 1], ALU.subtract))
                link(dve.tensor_tensor(o2, tmp[:, 2], tmp[:, 3], ALU.add))

            tmp = sil[:].rearrange("p t n -> p (t n)").rearrange("p (q h r) -> p q h r", q=4, r=16)
            k_rot = trig[:, 2, :, :]
            k_rot2 = trig[:, 5, :, :]
            for t in range(T):
                r = lat[:, t, QL + KVL:QL + KVL + ROPE]
                rotate(r[:, 0:16], r[:, 16:32], k_rot[:, t, :], k_rot2[:, t, :],
                       tmp[:, :, 0, :], cos[:, t, :], sin[:, t, :])
            dve.wait_ge(up_out, 4)
            for t in range(T):
                kr = k_row[:, t, :].rearrange("p (h d) -> p h d", d=QH)
                link(dve.tensor_copy(kr[:, :, 0:QK], kv_row[:, t, :].rearrange("p (h d) -> p h d", d=P)[:, :, 0:QK]))
                for o, src in ((QK, k_rot), (QK + 16, k_rot2)):
                    link(dve.tensor_copy(kr[:, :, o:o + 16], src[:, t, :].rearrange("p (o r) -> p o r", o=1).broadcast_to([P, H, 16])))
            dve.sem_inc(qk_ready, 1)
            dve.wait_ge(w_used[SLOT_B], m2 + 9)
            for t in range(T):
                for n in range(2):
                    link(dve.tensor_scalar(q_row[:, t, n * QL:(n + 1) * QL], ps[:, 4 + 2 * t + n, 0:QL], QH ** -0.5, None, ALU.mult))
            for t in range(T):
                qr = q_row[:, t, :].rearrange("p (h d) -> p h d", d=QH)
                co = cos[:, t, :].rearrange("p (o r) -> p o r", o=1).broadcast_to([P, H, 16])
                si = sin[:, t, :].rearrange("p (o r) -> p o r", o=1).broadcast_to([P, H, 16])
                rotate(qr[:, :, QK:QK + 16], qr[:, :, QK + 16:QH], qr[:, :, QK:QK + 16], qr[:, :, QK + 16:QH], tmp, co, si)
            dve.sem_inc(qk_ready, 1)
            split_lo(SLOT_A, m2 + 9)
            split_lo(SLOT_B, m2 + 9)

            def softmax_max(h):
                dve.wait_ge(s_mm, h + 1)
                m = stat[:, 16 + 2 * h:18 + 2 * h]
                dve.tensor_reduce(m, ps[:, (4, 5, 2, 3)[h % 4], :].rearrange("p (t n) -> p t n", n=S), AX.X, ALU.max,
                                  negate=True).then_inc(smax_ready, 1)

            def probs_out(h):
                dve.wait_ge(s_tr, h + 1)
                if h >= 2:
                    dve.wait_ge(om_mm, h - 1)
                dve.tensor_copy(probT[:, h % 2, :], ps[:, 6 + h % 2, :]).then_inc(sT_out, 1)

            softmax_max(0)
            softmax_max(1)
            for h in range(H):
                if h + 2 < H:
                    softmax_max(h + 2)
                probs_out(h)
            dve.wait_ge(s_exp, 2 * H)
            link(dve.reciprocal(trig[:, 2, :, 0:H], trig[:, 0, :, 0:H]))
            dve.wait_ge(om_mm, H)
            for t in range(T):
                rs = trig[:, 2, t, 0:H].rearrange("p (h o) -> p h o", o=1).broadcast_to([P, H, DH])
                dve.tensor_tensor(y_row[:, t, 0:NB].rearrange("p (h d) -> p h d", d=DH),
                                  ps[:, t, :].rearrange("p (h d) -> p h d", d=DH), rs, ALU.mult).then_inc(om_out, 1)
            dve.wait_ge(omT_mm, 1)
            for k in range(4):
                dve.tensor_copy(nT[:, k, :], ps[:, 4 + k // 2, (k % 2) * S:(k % 2 + 1) * S]).then_inc(omT_out, 1)
            dve.wait_ge(omT_hi, 1)
            dve.tensor_tensor(nT_lo[:, 0:4, :], nT[:, 0:4, :], nT_hi[:, 0:4, :].bitcast(F32), ALU.subtract).then_inc(omT_lo, 1)
            split_lo(SLOT_A, m2 + 10)
            split_lo(SLOT_B, m2 + 10)
            dve.wait_ge(w_used[SLOT_B], m2 + 10)
            for t in range(T):
                src = ps[:, 2 * t:2 * t + 2, :].rearrange("p b n -> p (b n)")
                link(dve.tensor_tensor(sig[:, t, D:2 * D], src, sig[:, t, D:2 * D], ALU.mult))
                dve.tensor_tensor(y_row[:, t, :], sig[:, t, 0:D], sig[:, t, D:2 * D], ALU.add).then_inc(yb_out, 1)
            norm_out(TR["O2"], lambda k, src: dve.tensor_copy(nT[:, k, :], src))
            split_lo(SLOT_A, m2 + 11)
            split_lo(SLOT_B, m2 + 11)
            split_lo(SLOT_A, AB0["F3"])
            split_lo(SLOT_B, AB0["F3"])
            residual("M2", 1, False)
            ffn("F3", nxt=0)
            residual("F3", 0, False)
            dve.wait_ge(post_loaded[0], 48)
            for t in range(T):
                rms_ready(dve, f"end {t}")
                dve.scalar_tensor_tensor(y_row[:, t, :], x_res[:, t, :], stat[:, 8 + t:9 + t], post_gain[:, 0, :],
                                         ALU.mult, ALU.mult).then_inc(y_ready, 1)


        @block.tensor
        def _(pe):
            def mm3(o, xh, xl, wh, wl, start, stop):
                pe.matmul(o, xh, wh, start=start, stop=False, skip_group_check=True)
                pe.matmul(o, xh, wl, start=False, stop=False, skip_group_check=True)
                return pe.matmul(o, xl, wh, start=False, stop=stop, skip_group_check=True)

            def weights(s, use):
                pe.wait_ge(lo_ready[s], use + 1)

            def norm_transposes(ready):
                for j in range(KD // 2):
                    for k in (2 * j, 2 * j + 1):
                        for t in range(T):
                            if j == 0 and k == 0:
                                ready(t)
                            last = pe.transpose(ps[:, 4 + j, (k % 2) * S + t * P:(k % 2) * S + (t + 1) * P],
                                                y_row[:, t, k * P:(k + 1) * P], ident[:])
                    last.then_inc(n_tr, 1)

            def norm(f):
                r = NORM[f]
                norm_transposes(lambda t: pe.wait_ge(y_ready, 2 * r + 1 + t))

            def row_group(s, out_banks, n, first_norm=None, k_at=None, nk=4, xh=None, xl=None, start=None, stop=None):
                for k in range(nk):
                    kk = k_at + k
                    if first_norm is not None and kk % 2 == 0:
                        pe.wait_ge(n_lo, 4 * first_norm + kk // 2 + 1)
                    for t in range(T):
                        last = mm3(out_banks[t], nT_hi[:, kk, t * P:(t + 1) * P], nT_lo[:, kk, t * P:(t + 1) * P],
                                   w_hi[:, s, k * n:(k + 1) * n], w_lo[:, s, k * n:(k + 1) * n],
                                   start=(k == 0 and bool(start)), stop=(k == nk - 1 and bool(stop)))
                return last

            def body(f, c, down=True, gu=True, first_norm=None, first=False, hooks=((), (), ())):
                i = FFN.index(f) * NC
                if gu:
                    wait(pe, h_ready, 2 * c + 2 * i)
                    weights(SLOT_A, c + AB0[f])
                    banks = [ps[:, t, :] for t in range(T)]
                    row_group(SLOT_A, banks, NB, first_norm, 0, start=True).then_inc(w_used[SLOT_A], 1)
                for hook in hooks[0]:
                    hook()
                if down:
                    pe.wait_ge(h_ready, 2 * c + 2 * i)
                    wait(pe, ht_lo, c - 1 + i)
                    for j in range(2):
                        for t in range(T):
                            last = pe.transpose(ps[:, 2, j * S + t * P:j * S + (t + 1) * P],
                                                h_row[:, t, j * P:(j + 1) * P], ident[:])
                    last.then_inc(ht_tr, 1)
                if gu:
                    weights(SLOT_B, c + AB0[f])
                    row_group(SLOT_B, banks, NB, first_norm, 4, stop=True).then_inc(w_used[SLOT_B], 1)
                for hook in hooks[1]:
                    hook()
                if down:
                    weights(SLOT_D, c - 1 + D0[f])
                    pe.wait_ge(ht_lo, c + i)
                    last_chunk = not gu
                    for t in range(T):
                        for j in range(2):
                            for n in range(2):
                                last = mm3(ps[:, 4 + 2 * t + n, :], hT_hi[:, j, t * P:(t + 1) * P], hT_lo[:, j, t * P:(t + 1) * P],
                                           w_hi[:, SLOT_D, j * D + n * NB:j * D + (n + 1) * NB],
                                           w_lo[:, SLOT_D, j * D + n * NB:j * D + (n + 1) * NB],
                                           start=(first and j == 0), stop=(last_chunk and j == 1))
                        if last_chunk and t == 0:
                            last.then_inc(down_done, 1)
                    last.then_inc(w_used[SLOT_D], 1)
                for hook in hooks[2]:
                    hook()

            def sum_columns(f_sums, n, acc):
                if n:
                    pe.wait_ge(ada_done[0], 4 + 8 * n)
                    pe.wait_ge(ada_done[1], 4 + 8 * n)
                wait(pe, gate_out, 2 * n_gates[FFN[n - 1]] if n else 0)
                wait(pe, cols_out, n)
                for i, (off, *_) in enumerate(f_sums):
                    for k in range(KD):
                        last = pe.matmul(ps[:, 3, KD * i + k:KD * i + k + 1], acc[:, off + k * P:off + (k + 1) * P],
                                         ones[:, 0:1], start=True, stop=True, skip_group_check=True)
                last.then_inc(acc_cols, 1)

            acc_flat = mod_acc.rearrange("p a b -> p (a b)")

            def sum_gate(f, i, half):
                off = gates[f][i][0] + half * NB
                n = 2 * (n_gates[f] + i) + half
                pe.wait_ge(ada_done[0], n_ada[f][0] + KD)
                wait(pe, gate_out, n)
                if i == 0 and half == 0:
                    wait(pe, cols_out, n_cols[f] + 1 if col_sums[f] else 0)
                pe.matmul(ps[:, 3, :], ones[:], acc_flat[:, off:off + NB], start=True, stop=True).then_inc(acc_gate, 1)

            def ffn(f):
                r = NORM[f]
                norm(f)
                body(f, 0, down=False, first_norm=TR[f])
                body(f, 1, first=True)
                with pe.Fori(2, NC - 2) as c:
                    body(f, c)
                g = [lambda i=i, h=h: sum_gate(f, i, h) for i in range(len(gates[f])) for h in range(2)]
                body(f, NC - 2, hooks=([lambda: sum_columns(col_sums[f], n_cols[f], acc_flat)] if col_sums[f] else (), g[0:1], ()))
                body(f, NC - 1, hooks=(g[1:2], g[2:3], ()))
                body(f, NC, gu=False, hooks=(g[3:4], (), ()))

            pe.wait_ge(const_ready, 2)
            pe.wait_ge(small_loaded, SMALL)
            for b in range(2):
                last = pe.transpose(ps[:, 7, b * P:b * P + VECS[b]], vec_rows[0:VECS[b], b, :], ident[0:VECS[b], 0:VECS[b]])
            last.then_inc(vec_tr, 1)
            pe.wait_ge(rel_ready, 1)
            for h in range(H):
                if h >= 4:
                    pe.wait_ge(toe_sb, h - 3)
                pe.matmul(ps[:, h % 4, 0:CAUSAL], rel_bc[0:BUCKETS, h, :], onehot[0:BUCKETS, :], start=True, stop=True)\
                    .then_inc(toe_mm, 1)
            pe.wait_ge(toe_sb, H)
            pe.wait_ge(ada_done[0], 4)
            pe.wait_ge(ada_done[1], 4)
            sum_columns([(0,), (D,)], 0, first_acc)
            pe.wait_ge(vec_ready, 2)
            ffn("F0")

            m1 = AB0["M1"]
            norm("M1")

            def group_free(g):
                wait(pe, grp_out, 2 * (g - 1))

            def t_group(g, first=False):
                group_free(g)
                for s in (SLOT_A, SLOT_B):
                    weights(s, m1 + g)
                    for k in range(4):
                        kk = 4 * s + k
                        if first and kk % 2 == 0:
                            pe.wait_ge(n_lo, 4 * TR["M1"] + kk // 2 + 1)
                        for i in range(4):
                            o = ps[:, 2 * (g % 2) + i // 2, (i % 2) * S:(i % 2 + 1) * S]
                            cols = slice(k * NB + i * P, k * NB + (i + 1) * P)
                            pe.matmul(o, w_hi[:, s, cols], nT_hi[:, kk, :], start=(kk == 0 and i % 2 == 0), stop=False,
                                      skip_group_check=True)
                            pe.matmul(o, w_hi[:, s, cols], nT_lo[:, kk, :], start=False, stop=False, skip_group_check=True)
                            last = pe.matmul(o, w_lo[:, s, cols], nT_hi[:, kk, :], start=False, stop=(kk == 7),
                                             skip_group_check=True)
                    last.then_inc(w_used[s], 1)

            def r_group(g, base, use, n, first_norm=None):
                group_free(g + base)
                banks = [ps[:, 2 * (g % 2) + t, 0:n] for t in range(T)]
                weights(SLOT_A, use)
                row_group(SLOT_A, banks, n, first_norm, 0, start=True).then_inc(w_used[SLOT_A], 1)
                weights(SLOT_B, use)
                row_group(SLOT_B, banks, n, first_norm, 4, stop=True).then_inc(w_used[SLOT_B], 1)

            def head(i, h):
                return qkT[DH * (h % 2):DH * (h % 2) + DH, i, h // 2, :]

            t_group(0, first=True)
            weights(SLOT_D, D0["M1"])
            for k in range(KD):
                for t in range(T):
                    last = mm3(ps[:, 4 + t, 0:72], nT_hi[:, k, t * P:(t + 1) * P], nT_lo[:, k, t * P:(t + 1) * P],
                               w_hi[:, SLOT_D, k * 72:(k + 1) * 72], w_lo[:, SLOT_D, k * 72:(k + 1) * 72],
                               start=(k == 0), stop=(k == KD - 1))
            last.then_inc(w_used[SLOT_D], 1)
            t_group(1)
            pe.wait_ge(ki_ready, 1)
            for t in range(T):
                last = pe.transpose(ps[:, 6, t * P:(t + 1) * P], ki2[:, t, :], ident[:])
            last.then_inc(ki_tr, 1)
            pe.wait_ge(kiT_ready, 1)
            pe.wait_ge(grp_out, 2)
            for h in range(H):
                if h >= 4:
                    pe.wait_ge(idx_relu, h - 3)
                q = head(TQI, h)
                k = kiT[DH * (h % 2):DH * (h % 2) + DH, :]
                pe.matmul(ps[:, 4 + h % 4, 0:S], q[:, P:S], k, start=True, stop=True, skip_group_check=True)
                pe.matmul(ps[:, 4 + h % 4, S:CAUSAL], q[:, 0:P], k[:, 0:P], start=True, stop=True,
                          skip_group_check=True).then_inc(idx_mm, 1)
            t_group(2)
            pe.wait_ge(grp_out, 6)
            for h in range(H):
                if h >= 4:
                    pe.wait_ge(z_out, h - 3)
                else:
                    pe.wait_ge(idx_relu, h + 5)
                q, k = head(TQB, h), head(TKB, h)
                pe.matmul(ps[:, 4 + h % 4, 0:S], k[:, 0:P], q, start=True, stop=True, skip_group_check=True)
                pe.matmul(ps[:, 4 + h % 4, S:CAUSAL], k[:, P:S], q[:, P:S], start=True, stop=True,
                          skip_group_check=True).then_inc(z_mm, 1)
            r_group(3, 0, m1 + 3, NB)
            t_group(4)
            pe.wait_ge(u_masked, 2)
            for h in range(H):
                if h >= 4:
                    pe.wait_ge(r_out, h - 3)
                else:
                    pe.wait_ge(z_out, h + 5)
                b = ps[:, 4 + h % 4, :]
                pe.matmul(b[:, 0:CAUSAL], tri[:], u_sb[:, h, :], start=True, stop=False, skip_group_check=True)
                pe.matmul(b[:, P:S], ones[:], u_sb[:, h, S:CAUSAL], start=False, stop=True,
                          skip_group_check=True).then_inc(r_mm, 1)
            t_group(5)
            pe.wait_ge(a_masked, 2)
            pe.wait_ge(r_out, H)
            pe.wait_ge(grp_out, 8)
            for h in range(H):
                v = [v_row[:, 1, s, h * DH:(h + 1) * DH] for s in range(2)]
                o = [ps[:, 4 + t, h * DH:(h + 1) * DH] for t in range(T)]
                pe.matmul(o[0], z_sb[:, h, 0:P], v[0], start=True, stop=True, skip_group_check=True)
                pe.matmul(o[1], z_sb[:, h, P:S], v[0], start=True, stop=False, skip_group_check=True)
                last = pe.matmul(o[1], z_sb[:, h, S:CAUSAL], v[1], start=False, stop=True, skip_group_check=True)
            last.then_inc(ob_mm, 1)
            r_group(6, 0, m1 + 6, NB)
            pe.wait_ge(grp_out, 12)
            pe.wait_ge(ob_out, T)
            def logits(h):
                if h >= 4:
                    pe.wait_ge(l_out, h - 3)
                q, k = head(TQA, h), head(TKA, h)
                pe.matmul(ps[:, 4 + h % 4, 0:S], q[:, P:S], k, start=True, stop=True, skip_group_check=True)
                pe.matmul(ps[:, 4 + h % 4, S:CAUSAL], q[:, 0:P], k[:, 0:P], start=True, stop=True,
                          skip_group_check=True).then_inc(l_mm, 1)
            for h in range(H):
                logits(h)
            pe.wait_ge(l_out, H)
            for h in range(H):
                if h >= 4:
                    pe.wait_ge(pT_out, h - 3)
                pe.wait_ge(p_exp, 2 * h + 2)
                for i in range(3):
                    last = pe.transpose(ps[:, 4 + h % 4, i * P:(i + 1) * P], z_sb[:, h, i * P:(i + 1) * P], ident[:])
                last.then_inc(p_tr, 1)
            pe.wait_ge(grp_out, 14)
            for h in range(H):
                pe.wait_ge(pT_out, h + 1)
                v = [v_row[:, 0, s, h * DH:(h + 1) * DH] for s in range(2)]
                o = [ps[:, t, h * DH:(h + 1) * DH] for t in range(T)]
                pe.matmul(o[1], e_sb[:, h, 0:P], v[0], start=True, stop=False, skip_group_check=True)
                pe.matmul(o[1], e_sb[:, h, P:S], v[1], start=False, stop=True, skip_group_check=True)
                last = pe.matmul(o[0], e_sb[:, h, S:CAUSAL], v[0], start=True, stop=True, skip_group_check=True)
            last.then_inc(oa_mm, 1)
            pe.wait_ge(pT_out, H)
            norm_transposes(lambda t: pe.wait_ge(o_ready, 1))

            def out_linear(r, use):
                pe.wait_ge(n_lo, 4 * r + 4)
                for n in range(2):
                    banks = [ps[:, 4 + 2 * t + n, :] for t in range(T)]
                    for s in (SLOT_A, SLOT_B):
                        weights(s, use + n)
                        last = row_group(s, banks, NB, None, 4 * s, start=(s == SLOT_A), stop=(s == SLOT_B))
                        last.then_inc(w_used[s], 1)

            out_linear(TR["O1"], m1 + 7)
            ffn("F1")
            ffn("F2")

            m2 = AB0["M2"]
            norm("M2")
            r_group(0, 7, m2, NB, first_norm=TR["M2"])
            r_group(1, 7, m2 + 1, QL)
            r_group(2, 7, m2 + 2, KVL + ROPE)
            pe.wait_ge(dft_loaded, 32)
            pe.wait_ge(grp_out, 14 + 2)
            for g in range(4):
                for k in range(2):
                    last = pe.matmul(ps[:, 4 + g, :], uf[:, k, g * P:(g + 1) * P], dft[:, k, :], start=(k == 0), stop=(k == 1))
                last.then_inc(cu_mm, 1)
            r_group(3, 7, m2 + 3, NB)
            r_group(4, 7, m2 + 4, NB)
            pe.wait_ge(cu_out, 4)
            for g in range(4):
                o = ps[:, 4 + g // 2, (g % 2) * S:(g % 2 + 1) * S]
                pe.matmul(o, dftd[:, 0, :], cu[:, g, 0:S], start=True, stop=False, skip_group_check=True)
                last = pe.matmul(o, dftd[:, 1, :], cu[:, g, S:2 * S], start=False, stop=True, skip_group_check=True)
            last.then_inc(f_mm, 1)
            r_group(5, 7, m2 + 5, NB)
            pe.wait_ge(lat_ready, 4)
            pe.wait_ge(f_out, 4)
            for k in range(5):
                for t in range(T):
                    last = pe.transpose(ps[:, (6, 6, 7, 7, 4)[k], (k % 2) * S + t * P:(k % 2) * S + (t + 1) * P],
                                        lat[:, t, k * P:(k + 1) * P], ident[:])
            last.then_inc(lat_tr, 1)
            r_group(6, 7, m2 + 6, NB)
            pe.wait_ge(f_lo, 1)
            pe.wait_ge(lat_out, 5)
            for s in (SLOT_A, SLOT_B):
                weights(s, m2 + 7)
                banks = [ps[:, 4 + 2 * t + s, :] for t in range(T)]
                row_group(s, banks, NB, None, 4, start=True, stop=True).then_inc(w_used[s], 1)
            pe.wait_ge(lat_lo, 2)
            pe.wait_ge(grp_out, 28)
            weights(SLOT_D, D0["M2"])
            for t in range(T):
                for n in range(2):
                    for k in range(2):
                        last = mm3(ps[:, 2 * t + n, :], hT_hi[:, k, t * P:(t + 1) * P], hT_lo[:, k, t * P:(t + 1) * P],
                                   w_hi[:, SLOT_D, k * D + n * NB:k * D + (n + 1) * NB],
                                   w_lo[:, SLOT_D, k * D + n * NB:k * D + (n + 1) * NB], start=(k == 0), stop=(k == 1))
            last.then_inc(w_used[SLOT_D], 1)
            pe.wait_ge(ya_out, T)
            for s in (SLOT_A, SLOT_B):
                weights(s, m2 + 8)
                banks = [ps[:, 4 + 2 * t + s, 0:QL] for t in range(T)]
                row_group(s, banks, QL, None, 0, nk=3, start=True, stop=True).then_inc(w_used[s], 1)
            for i in range(8):
                src = k_row if i < 4 else q_row
                if i % 4 == 0:
                    pe.wait_ge(qk_ready, i // 4 + 1)
                    pe.wait_ge(up_out, 4)
                if i >= 4:
                    pe.wait_ge(qkT_out, i - 3)
                for j in range(2):
                    h = 2 * (i % 4) + j
                    for t in range(T):
                        last = pe.transpose(ps[0:QH, i % 4, j * S + t * P:j * S + (t + 1) * P], src[:, t, h * QH:(h + 1) * QH], ident[:])
                last.then_inc(qk_tr, 1)
            pe.wait_ge(qkT_out, 8)

            def scores(h):
                if h >= 4:
                    pe.wait_ge(s_exp, 2 * (h - 3))
                for t in range(T):
                    last = pe.matmul(ps[:, (4, 5, 2, 3)[h % 4], t * S:(t + 1) * S], qT[0:QH, h, t * P:(t + 1) * P], kT[0:QH, h, :],
                                     start=True, stop=True, skip_group_check=True)
                last.then_inc(s_mm, 1)

            for h in range(3):
                scores(h)
            for h in range(H):
                pe.wait_ge(s_exp, 2 * h + 2)
                if h >= 2:
                    pe.wait_ge(sT_out, h - 1)
                for s in range(2):
                    for t in range(T):
                        last = pe.transpose(ps[:, 6 + h % 2, s * S + t * P:s * S + (t + 1) * P],
                                            prob4[:, h % 4, t * S + s * P:t * S + (s + 1) * P], ident[:])
                last.then_inc(s_tr, 1)
                if h + 3 < H:
                    scores(h + 3)
                pe.wait_ge(sT_out, h + 1)
                for t in range(T):
                    for s in range(2):
                        last = pe.matmul(ps[:, t, h * DH:(h + 1) * DH], probT[:, h % 2, s * S + t * P:s * S + (t + 1) * P],
                                         kv_row[:, s, h * P + QK:(h + 1) * P], start=(s == 0), stop=(s == 1),
                                         skip_group_check=True)
                last.then_inc(om_mm, 1)
            pe.wait_ge(om_out, T)
            for k in range(4):
                for t in range(T):
                    last = pe.transpose(ps[:, 4 + k // 2, (k % 2) * S + t * P:(k % 2) * S + (t + 1) * P],
                                        y_row[:, t, k * P:(k + 1) * P], ident[:])
            last.then_inc(omT_mm, 1)
            pe.wait_ge(omT_lo, 1)
            for s in (SLOT_A, SLOT_B):
                weights(s, m2 + 9)
                banks = [ps[:, 2 * t + s, :] for t in range(T)]
                row_group(s, banks, NB, None, 0, start=True, stop=True).then_inc(w_used[s], 1)
            norm_transposes(lambda t: pe.wait_ge(yb_out, t + 1))
            out_linear(TR["O2"], m2 + 10)
            ffn("F3")


def onehot_buckets():
    import math
    import numpy as np
    n = np.maximum(255 - np.arange(CAUSAL), 0)
    exact = BUCKETS // 2
    large = exact + (np.log(np.maximum(n, 1).astype(np.float32) / exact) / math.log(128 / exact)
                     * (BUCKETS - exact)).astype(np.int32)
    bucket = np.where(n < exact, n, np.minimum(large, BUCKETS - 1))
    return (bucket[None, :] == np.arange(BUCKETS)[:, None]).astype(np.float32)


def dft_tables():
    import numpy as np
    s, d = np.arange(S), np.arange(P)
    ws = 2 * np.pi * ((s[:, None] * s[None, :]) % S) / S
    wd = 2 * np.pi * ((d[:, None] * d[None, :]) % P) / P
    over_s = np.concatenate([np.cos(ws), np.sin(ws)], 1) / np.sqrt(S)
    over_d = np.concatenate([np.cos(wd), -np.sin(wd)], 1) / np.sqrt(P)
    return over_s.astype(np.float32), over_d.astype(np.float32)


def inverse_frequencies():
    import numpy as np
    e = np.arange(16, dtype=np.float32) * np.float32(2.0) / np.float32(32)
    return (np.float32(1.0) / (np.float32(10000.0) ** e)).astype(np.float32)[None, :]


_OUTS = [((1, 256, 1024), "float32")]


def kernel(**inputs):
    import numpy as np
    import concourse.bacc as bacc
    from concourse.bass_utils import run_bass_kernel_spmd

    nc = bacc.Bacc("TRN2", target_bir_lowering=False, num_devices=1)
    arrays, aps = {}, {}
    over_s, over_d = dft_tables()
    shape_constants = {"onehot": onehot_buckets(), "dft_s": over_s, "dft_d": over_d, "inv_freq": inverse_frequencies()}
    for name, v in {**inputs, **shape_constants}.items():
        v = np.ascontiguousarray(v)
        arrays[f"in_{name}"] = v
        aps[name] = nc.dram_tensor(f"in_{name}", v.shape, mybir.dt.from_np(v.dtype), kind="ExternalInput").ap()
    out = nc.dram_tensor("out", _OUTS[0][0], F32, kind="ExternalOutput").ap()
    program(nc, aps, out)
    r = run_bass_kernel_spmd(nc, [arrays], core_ids=[0])
    return r.results[0]["out"]
```

```python
from contextlib import ExitStack

import concourse.bass as bass
from concourse import mybir

F32 = mybir.dt.float32
F32R = mybir.dt.float32r
I32 = mybir.dt.int32
ALU = mybir.AluOpType
ACT = mybir.ActivationFunctionType
AX = mybir.AxisListType

P = 128
D = 1024
S = 256
T = S // P
KD = D // P
F = 2816
FC = 256
NC = F // FC
NB = 512
PIECE = 2048
H = 8
DH = 64
CAUSAL = 384
TOPK = 64
BUCKETS = 32
EPS = 1e-6
DONE = -3.0e38
FUTURE = -2.0e38
OFF = -1.0e30
ROUND = 12582912.0
TWO_PI = (6.28125, 0.0019350051879882812, 3.0199159819e-07)
PI = 3.1415925
SLOT_A, SLOT_B, SLOT_D = 0, 1, 2
ADA = 3072
ARENA = 18944
QK, ROPE, QH = 64, 32, 96
QL, KVL = 384, 256


def program(nc, a, out):
    ctx = ExitStack()
    with ctx:
        def sb(name, shape, dt=F32):
            return ctx.enter_context(nc.sbuf_tensor(name, shape, dt))

        def sem(name):
            return ctx.enter_context(nc.semaphore(name))

        x_res = sb("x_res", [P, T, D])
        y_row = sb("y_row", [P, T, D])
        nT = sb("nT", [P, KD, S])
        nT_hi = sb("nT_hi", [P, KD, S], F32R)
        nT_lo = sb("nT_lo", [P, KD, S], F32R)
        w_raw = sb("w_raw", [P, 3, PIECE])
        w_hi = sb("w_hi", [P, 3, PIECE], F32R)
        w_lo = sb("w_lo", [P, 3, PIECE], F32R)
        sil = sb("sil", [P, 2, S])
        h_act = sb("h_act", [P, 2, S])
        hT_hi = sb("hT_hi", [P, 2, S], F32R)
        hT_lo = sb("hT_lo", [P, 2, S], F32R)
        gate = sb("gate", [P, 2, D])
        arena = sb("arena", [P, ARENA])
        ident = sb("ident", [P, P])
        ones = sb("ones", [P, P])
        tri = sb("tri", [P, P])
        vec_rows = sb("vec_rows", [P, 2, P])
        vec_col = sb("vec_col", [P, 2, P])
        mod_col = sb("mod_col", [P, 6, 2, KD])
        c_in = sb("c_in", [P, 2, KD])
        c_act = sb("c_act", [P, 2, KD])
        stat = sb("stat", [P, 64])
        minus_half = sb("minus_half", [P, 4])
        angle = sb("angle", [P, T, 16])
        trig = sb("trig", [P, 6, T, 16])
        pos_i = sb("pos_i", [P, T], I32)
        pos_f = sb("pos_f", [P, T])
        freq = sb("freq", [P, 16])
        gki = sb("gki", [P, DH])
        ps = ctx.enter_context(nc.psum_tensor("ps", [P, 8, NB], F32))
        toe_dram = nc.dram_tensor("toe_scratch", [P * 3 * P * H], F32, kind="Internal").ap()

        def carve(at, *shape):
            n = 1
            for s in shape:
                n *= s
            assert at + n <= ARENA, (at, shape)
            v = arena[:, at:at + n]
            if len(shape) == 2:
                v = v.rearrange("p (a b) -> p a b", b=shape[1])
            if len(shape) == 3:
                v = v.rearrange("p (a b c) -> p a b c", b=shape[1], c=shape[2])
            return v

        mod_acc = carve(0, 2, ADA)
        ada_raw = carve(2 * ADA, 2, ADA)
        post_gain = carve(4 * ADA, 2, D)
        first_acc = carve(4 * ADA + 2 * D, 2 * D)
        qkT = carve(0, 5, 4, S)
        TQI, TQB, TKB, TKA, TQA = range(5)
        v_row = carve(5120, 2, T, NB)
        z_sb = carve(7168, H, CAUSAL)
        u_sb = carve(10240, H, CAUSAL)
        e_sb = carve(13312, H, CAUSAL)
        score = carve(16384, CAUSAL)
        work = carve(16768, CAUSAL)
        relu = carve(17152, 4, CAUSAL)
        kw_row = h_act[:, :, 0:72]
        ki2 = sil[:, :, 0:P]
        kiT = h_act[:, 0, :]
        wi = stat[:, 32:48]
        ob_T = qkT[:, TQI]
        toe_bc = carve(0, H, CAUSAL)
        rel_bc = carve(3072, H, P)
        rel_in = carve(4096, H)
        onehot = carve(4104, CAUSAL)
        bias = nT
        sig = carve(0, T, 2 * D)
        uf = carve(4096, T, NB)
        dft = carve(5120, 2, NB)
        dftd = carve(6144, 2, P)
        cu = carve(6400, 4, NB)
        lat = carve(8448, T, QL + KVL + ROPE)
        q_row = carve(9792, T, H * QH)
        k_row = carve(11328, T, H * QH)
        kv_row = carve(12864, T, H * P)
        qT = carve(14912, H, S)
        kT = carve(4096, H, S)
        prob = carve(6144, 2, NB * 2)
        probT = carve(16960, 2, NB)

        raw_loaded = [sem(f"raw_loaded{s}") for s in range(3)]
        hi_ready = [sem(f"hi_ready{s}") for s in range(3)]
        lo_ready = [sem(f"lo_ready{s}") for s in range(3)]
        w_used = [sem(f"w_used{s}") for s in range(3)]
        small_loaded = sem("small_loaded")
        x_loaded = sem("x_loaded")
        const_ready = sem("const_ready")
        pool_step = sem("pool_step")
        c_loaded = sem("c_loaded")
        c_ready = sem("c_ready")
        vec_tr = sem("vec_tr")
        vec_ready = sem("vec_ready")
        toe_mm = sem("toe_mm")
        toe_sb = sem("toe_sb")
        toe_stored = sem("toe_stored")
        bias_loaded = sem("bias_loaded")
        rel_ready = sem("rel_ready")
        ada_loaded = [sem(f"ada_loaded{s}") for s in range(2)]
        ada_done = [sem(f"ada_done{s}") for s in range(2)]
        acc_zero = sem("acc_zero")
        acc_cols = sem("acc_cols")
        cols_out = sem("cols_out")
        acc_gate = sem("acc_gate")
        gate_out = sem("gate_out")
        gate_loaded = [sem(f"gate_loaded{s}") for s in range(2)]
        post_loaded = [sem(f"post_loaded{s}") for s in range(2)]
        sq_done = sem("sq_done")
        ki_sq = sem("ki_sq")
        rms_done = sem("rms_done")
        y_ready = sem("y_ready")
        n_tr = sem("n_tr")
        n_ready = sem("n_ready")
        n_hi = sem("n_hi")
        n_lo = sem("n_lo")
        h_done = sem("h_done")
        silu_done = sem("silu_done")
        h_ready = sem("h_ready")
        ht_hi = sem("ht_hi")
        ht_lo = sem("ht_lo")
        mix_half = sem("mix_half")
        down_done = sem("down_done")
        fsq_done = sem("fsq_done")
        dve_step = sem("dve_step")
        grp_out = sem("grp_out")
        out_stored = sem("out_stored")
        sp_settled = sem("sp_settled")

        def S_(n):
            return sem(n)
        ki_ready, ki_tr, kiT_ready = map(S_, ["ki_ready", "ki_tr", "kiT_ready"])
        idx_mm, idx_relu, idx_acc = map(S_, ["idx_mm", "idx_relu", "idx_acc"])
        score_causal, sel_ready, mask_ready = map(S_, ["score_causal", "sel_ready", "mask_ready"])
        z_mm, z_out, z_ln, u_ready, u_masked = map(S_, ["z_mm", "z_out", "z_ln", "u_ready", "u_masked"])
        r_mm, r_out, loga_ready, a_exp, a_masked, ob_mm, ob_out = map(
            S_, ["r_mm", "r_out", "loga_ready", "a_exp", "a_masked", "ob_mm", "ob_out"])
        l_mm, l_out, lmax_ready, p_exp, p_tr, pT_out, oa_mm, oa_out = map(
            S_, ["l_mm", "l_out", "lmax_ready", "p_exp", "p_tr", "pT_out", "oa_mm", "oa_out"])
        osq_done = sem("osq_done")
        dft_loaded, cu_mm, cu_out, f_mm, f_out, f_hi, f_lo = map(
            S_, ["dft_loaded", "cu_mm", "cu_out", "f_mm", "f_out", "f_hi", "f_lo"])
        trig_arg, trig_done, trig_ready = map(S_, ["trig_arg", "trig_done", "trig_ready"])
        lat_sq, lat_ready, lat_tr, lat_out, lat_hi, lat_lo = map(
            S_, ["lat_sq", "lat_ready", "lat_tr", "lat_out", "lat_hi", "lat_lo"])
        up_out, qk_ready, qk_tr, qkT_out = map(S_, ["up_out", "qk_ready", "qk_tr", "qkT_out"])
        ya_out, yb_out = map(S_, ["ya_out", "yb_out"])
        s_mm, smax_ready, s_exp, s_tr, sT_out, om_mm, om_out = map(
            S_, ["s_mm", "smax_ready", "s_exp", "s_tr", "sT_out", "om_mm", "om_out"])
        omT_mm, omT_out, omT_hi, omT_lo = map(S_, ["omT_mm", "omT_out", "omT_hi", "omT_lo"])

        top_found, top_taken, o_ready, ob_ready = map(S_, ["top_found", "top_taken", "o_ready", "ob_ready"])
        SMALL = 16 * 15
        VECS = (104, 101)

        AB0 = {"F0": 0, "M1": NC, "F1": NC + 9, "F2": 2 * NC + 9, "M2": 3 * NC + 9, "F3": 3 * NC + 21}
        D0 = {"F0": 0, "M1": NC, "F1": NC + 1, "F2": 2 * NC + 1, "M2": 3 * NC + 1, "F3": 3 * NC + 2}
        FFN = ["F0", "F1", "F2", "F3"]
        ffn_w = {
            "F0": (a["w_ffn_gate"][0, 0], a["w_ffn_up"][0, 0], a["w_ffn_down"][0, 0]),
            "F1": (a["w_ffn_gate"][0, 1], a["w_ffn_up"][0, 1], a["w_ffn_down"][0, 1]),
            "F2": (a["ffn1_w_gate_2"][0], a["ffn1_w_up_2"][0], a["ffn1_w_down_2"][0]),
            "F3": (a["ffn2_w_gate_2"][0], a["ffn2_w_up_2"][0], a["ffn2_w_down_2"][0]),
        }
        NORM = {"F0": 0, "M1": 1, "F1": 2, "F2": 3, "M2": 4, "F3": 5, "end": 6}
        w1, w2 = a["w_ada"][0], a["ada_w_2"][0]
        ada_steps = {
            "F0": [(w1, 2 * D, 3 * D, 0, 0), (w1, 6 * D, 2 * D, 0, D)],
            "F1": [(w1, 8 * D, D, 0, 0), (w2, 0, 2 * D, 1, 0)],
            "F2": [(w2, 2 * D, 3 * D, 1, 0), (w2, 6 * D, 2 * D, 1, D)],
            "F3": [(w2, 8 * D, D, 1, 0)],
        }
        ada_rest = {"F0": (w1, 5 * D, 0), "F2": (w2, 5 * D, 1)}
        col_sums = {
            "F0": [(D, 0, 3, 1), (2 * D, 0, 4, 1), (4 * D, 0, 6, 2), (5 * D, 0, 7, 2)],
            "F1": [(ADA, 1, 0, 3), (ADA + D, 1, 1, 3)],
            "F2": [(D, 1, 3, 4), (2 * D, 1, 4, 4), (4 * D, 1, 6, 5), (5 * D, 1, 7, 5)],
            "F3": [],
        }
        b1, b2 = a["b_ada"][0], a["ada_b_2"][0]
        gates = {
            "F0": [(0, b1[2 * D:3 * D], 0, a["g_post"][0, 0], 0.5), (3 * D, b1[5 * D:6 * D], 1, a["g_post"][0, 1], 1.0)],
            "F1": [(0, b1[8 * D:9 * D], 0, a["g_post"][0, 2], 0.5)],
            "F2": [(0, b2[2 * D:3 * D], 0, None, 0.5), (3 * D, b2[5 * D:6 * D], 1, None, 1.0)],
            "F3": [(0, b2[8 * D:9 * D], 0, None, 0.5)],
        }
        n_gates = {"F0": 0, "F1": 2, "F2": 3, "F3": 5}
        n_cols = {"F0": 1, "F1": 2, "F2": 3, "F3": 4}
        n_buf = {"F0": (0, 0), "F1": (1, 1), "F2": (2, 1), "F3": (3, 2)}
        n_ada = {"F0": 4, "F1": 14, "F2": 22, "F3": 32}
        gain_at = {1: (0, 80), 2: (0, 88), 3: (1, 72), 4: (1, 80), 5: (1, 88)}
        w_in = a["w_in"][0].rearrange("(k p) n -> p k n", p=P)
        w_in2 = a["w_in_2"][0].rearrange("(k p) n -> p k n", p=P)
        w_out = a["w_out"][0].rearrange("(k p) n -> p k n", p=P)
        w_out2 = a["w_out_2"][0].rearrange("(k p) n -> p k n", p=P)
        GROUPS1 = [("qb", 2120), ("kb", 2632), ("qi", 1536), ("ka", 512), ("vb", 3144), ("qa", 0), ("va", 1024)]
        KI = 3
        GROUPS2 = [("uf", 0, 512), ("q", 512, 384), ("kv", 896, 288)] + [("g", 1184 + 512 * i, 512) for i in range(4)]

        RMS = [f"F0 {t}" for t in range(T)]
        for stage, after in (("F0", "M1"), ("M1", "F1"), ("F1", "F2"), ("F2", "M2"), ("M2", "F3"), ("F3", "end")):
            if stage == "M1":
                RMS += ["index keys", "M1 out b", "M1 out a"]
            if stage == "M2":
                RMS += ["q latent", "kv latent"]
            if stage in ("F0", "M1", "F1"):
                RMS += [f"post {stage} {t}" for t in range(T)]
            RMS += [f"{after} {t}" for t in range(T)]
        TR = {"F0": 0, "M1": 1, "O1": 2, "F1": 3, "F2": 4, "M2": 5, "O2": 6, "F3": 7}

        def slot(t, s, n):
            return t[:, s, 0:n]

        def wait(e, s, v):
            if not (isinstance(v, int) and v <= 0):
                e.wait_ge(s, v)

        def use1(s, g):
            return AB0["M1"] + g + (1 if s == SLOT_A and g >= KI else 0)

        def output_at(stage, t):
            return (4, 2)[t] if stage == "M1" else 4 + 2 * t

        def x_junk(half):
            return sil[:].rearrange("p t n -> p (t n)") if half == 0 else gate[:, 0, 0:NB]

        prob4 = prob.rearrange("p a (b n) -> p (a b) n", n=NB)

        def rms_ready(e, name):
            e.wait_ge(rms_done, RMS.index(name) + 1)

        def output_ready(e, stage, t):
            if stage[0] == "F" and t == 0:
                e.wait_ge(down_done, FFN.index(stage) + 1)
            elif stage[0] == "F":
                e.wait_ge(w_used[SLOT_D], D0[stage] + NC)
            elif stage == "M1" and t == 0:
                e.wait_ge(mix_half, 1)
            else:
                e.wait_ge(w_used[SLOT_B], AB0["F1" if stage == "M1" else "F3"])

        block = ctx.enter_context(nc.Block())

        @block.sync
        def _(sp):
            def raw_free(s, use):
                wait(sp, lo_ready[s], use)
                settle(use)

            def settle(v):
                if not isinstance(v, int):
                    sp.sem_inc(sp_settled, 1)

            def load(s, use, parts):
                raw_free(s, use)
                for dst, src in parts:
                    sp.dma_start(dst, src).then_inc(raw_loaded[s], 16)

            def load_k4(s, use, src, k0, c0, n, nk=4):
                dst = slot(w_raw, s, nk * n).rearrange("p (k n) -> p k n", n=n)
                m = nk // 2
                load(s, use, [(dst[:, 0:m], src[:, k0:k0 + m, c0:c0 + n]),
                              (dst[:, m:nk], src[:, k0 + m:k0 + nk, c0:c0 + n])])

            def load_gu(f, s, c):
                wg, wu, _ = ffn_w[f]
                dst = w_raw[:, s, :].rearrange("p (k g n) -> p k g n", g=2, n=FC)
                raw_free(s, c + AB0[f])
                for g, w in enumerate((wg, wu)):
                    src = w.rearrange("(k p) n -> p k n", p=P)[:, 4 * s:4 * s + 4, bass.ds(c * FC, FC)]
                    sp.dma_start(dst[:, :, g, :], src).then_inc(raw_loaded[s], 16)

            def load_down(f, c):
                src = ffn_w[f][2].rearrange("(c p) n -> p c n", p=P)
                dst = w_raw[:, SLOT_D, :].rearrange("p (k n) -> p k n", n=D)
                raw_free(SLOT_D, c + D0[f])
                for j in range(2):
                    sp.dma_start(dst[:, j], src[:, bass.ds(c * 2 + j, 1), :].rearrange("p a n -> p (a n)")
                                 if not isinstance(c, int) else src[:, c * 2 + j, :]).then_inc(raw_loaded[SLOT_D], 16)

            def load_ada(f, half, j):
                if half >= len(ada_steps[f]):
                    return
                w, c0, n, _, _ = ada_steps[f][half]
                src = w.rearrange("(p j) n -> p j n", j=KD)
                wait(sp, ada_done[half], j + n_ada[f])
                settle(j)
                sp.dma_start(ada_raw[:, half, 0:n], src[:, bass.ds(j, 1), c0:c0 + n].rearrange("p a n -> p (a n)")
                             if not isinstance(j, int) else src[:, j, c0:c0 + n]).then_inc(ada_loaded[half], 16)

            def load_ada_rest(f, step):
                if f not in ada_rest:
                    return
                w, c0, _ = ada_rest[f]
                half = step % 2
                sp.wait_ge(ada_done[half], n_ada[f] + KD + step // 2)
                sp.dma_start(ada_raw[:, half, 0:2 * D].rearrange("p (j n) -> p j n", n=D),
                             w.rearrange("(p j) n -> p j n", j=KD)[:, 2 * step:2 * step + 2, c0:c0 + D])\
                    .then_inc(ada_loaded[half], 16)

            def ffn_loads(f, next_a, next_b):
                load_gu(f, SLOT_A, 1)
                load_gu(f, SLOT_B, 1)
                wait(sp, h_done, 2 * NORM[f])
                for i, (_, b, buf, post, _) in enumerate(gates[f]):
                    sp.dma_start(gate[:, buf, :], b.rearrange("(a n) -> a n", a=1).broadcast_to([P, D]))\
                        .then_inc(gate_loaded[buf], 16)
                    if post is not None:
                        sp.dma_start(post_gain[:, i, :], post.rearrange("(a n) -> a n", a=1).broadcast_to([P, D]))\
                            .then_inc(post_loaded[i], 16)

                def chunk(c):
                    load_down(f, c - 1)
                    load_ada(f, 0, c - 1)
                    load_ada(f, 1, c - 1)
                    load_gu(f, SLOT_A, c + 1)
                    load_gu(f, SLOT_B, c + 1)

                chunk(1)
                with sp.Fori(2, KD + 1) as c:
                    chunk(c)
                load_down(f, NC - 3)
                load_ada_rest(f, 0)
                load_ada_rest(f, 1)
                load_gu(f, SLOT_A, NC - 1)
                load_gu(f, SLOT_B, NC - 1)
                load_down(f, NC - 2)
                load_ada_rest(f, 2)
                load_ada_rest(f, 3)
                next_a()
                next_b()
                load_down(f, NC - 1)

            sp.dma_start(c_in[:, 0, :], a["c"].rearrange("a (p j) -> (a p) j", j=KD)).then_inc(c_loaded, 16)
            sp.dma_start(c_in[:, 1, :], a["c_2"].rearrange("a (p j) -> (a p) j", j=KD)).then_inc(c_loaded, 16)
            src = w1.rearrange("(p j) n -> p j n", j=KD)
            for j in range(2):
                sp.dma_start(ada_raw[:, j % 2, 0:2 * D], src[:, j, 0:2 * D]).then_inc(ada_loaded[j % 2], 16)
            for t in range(T):
                sp.dma_start(x_res[:, t, :], a["x"][0, t * P:(t + 1) * P, :]).then_inc(x_loaded, 16)
            for blk, rows in enumerate((
                [("b_ada", 72), ("g_pre", 24), ("g_out_a", 4), ("g_out_b", 4)],
                [("ada_b_2", 72), ("ffn1_norm_2", 8), ("mix_norm_2", 8), ("ffn2_norm_2", 8), ("q_norm_2", 3), ("kv_norm_2", 2)],
            )):
                at = 0
                for name, n in rows:
                    v = a[name]
                    v = v.rearrange("a b n -> (a b n)") if len(v.shape) == 3 else v.rearrange("a n -> (a n)")
                    sp.dma_start(vec_rows[at:at + n, blk, :], v.rearrange("(r q) -> r q", q=P)).then_inc(small_loaded, 16)
                    at += n
            sp.dma_start(rel_in[0:BUCKETS, :], a["rel_bias"]).then_inc(small_loaded, 16)
            sp.dma_start(onehot[0:BUCKETS, :], a["onehot"]).then_inc(small_loaded, 16)
            sp.dma_start(gki[:], a["g_kidx"].broadcast_to([P, DH])).then_inc(small_loaded, 16)
            sp.dma_start(freq[:], a["inv_freq"].broadcast_to([P, 16])).then_inc(small_loaded, 16)
            sp.dma_start(pos_i[:], a["positions_2"].rearrange("a (t p) -> p (a t)", p=P), allow_slow_non_contiguous=True)\
                .then_inc(small_loaded, 16)
            for j in range(2, KD):
                wait(sp, ada_done[j % 2], j // 2)
                sp.dma_start(ada_raw[:, j % 2, 0:2 * D], src[:, j, 0:2 * D]).then_inc(ada_loaded[j % 2], 16)
            load_gu("F0", SLOT_A, 0)
            load_gu("F0", SLOT_B, 0)
            sp.wait_ge(toe_sb, H)
            sp.dma_start(toe_dram.rearrange("(p n) -> p n", p=P), toe_bc.rearrange("p h n -> p (h n)"))\
                .then_inc(toe_stored, 16)
            m1, m2 = AB0["M1"], AB0["M2"]

            def group1(i, s):
                load_k4(s, use1(s, i), w_in, 4 * s, GROUPS1[i][1], NB)

            def group2(i, s):
                load_k4(s, m2 + i, w_in2, 4 * s, GROUPS2[i][1], GROUPS2[i][2])

            sp.wait_ge(toe_stored, 16)
            ffn_loads("F0", lambda: group1(0, SLOT_A), lambda: group1(0, SLOT_B))
            load_k4(SLOT_D, D0["M1"], w_out, 4, NB, NB)
            for i in range(1, len(GROUPS1)):
                if i == KI:
                    dst = slot(w_raw, SLOT_A, KD * 72).rearrange("p (k n) -> p k n", n=72)
                    load(SLOT_A, m1 + KI, [(dst[:, 4 * j:4 * j + 4], w_in[:, 4 * j:4 * j + 4, 2048:2120]) for j in range(2)])
                for s in (SLOT_B, SLOT_A) if i == KI else (SLOT_A, SLOT_B):
                    load_k4(s, use1(s, i), w_in, 4 * s, GROUPS1[i][1], NB)
                if i == KI:
                    sp.wait_ge(n_lo, 4 * (TR["M1"] + 1))
                    pitch = H * CAUSAL
                    for h in range(H):
                        skew = bass.AP(toe_dram.tensor, toe_dram.offset + h * CAUSAL + P - 1, [[pitch - 1, P], [1, S]])
                        sp.dma_start(bias[:, h, :], skew).then_inc(bias_loaded, 16)
            load_k4(SLOT_B, m1 + 7, w_out, 4, 0, NB)
            load_k4(SLOT_A, m1 + 8, w_out, 0, 0, NB)
            load_k4(SLOT_B, m1 + 8, w_out, 0, NB, NB)
            load_gu("F1", SLOT_A, 0)
            load_gu("F1", SLOT_B, 0)
            ffn_loads("F1", lambda: load_gu("F2", SLOT_A, 0), lambda: load_gu("F2", SLOT_B, 0))
            ffn_loads("F2", lambda: group2(0, SLOT_A), lambda: group2(0, SLOT_B))
            sp.wait_ge(h_done, 2 * NORM["M2"])
            sp.dma_start(dft[:], a["dft_s"].rearrange("(k p) n -> p k n", p=P)).then_inc(dft_loaded, 16)
            sp.dma_start(dftd[:], a["dft_d"].rearrange("p (k n) -> p k n", n=P)).then_inc(dft_loaded, 16)
            for i in range(1, len(GROUPS2)):
                group2(i, SLOT_A)
                group2(i, SLOT_B)
            wf = a["w_fourier_out_2"][0].rearrange("(k p) n -> p k n", p=P)
            wm = a["w_mla_out_2"][0].rearrange("(k p) n -> p k n", p=P)
            for w, use in ((wf, m2 + 7),):
                for s in (SLOT_A, SLOT_B):
                    load_k4(s, use, w, 0, s * NB, NB)
            wq = a["w_q_up_2"][0].rearrange("(k p) n -> p k n", p=P)
            for s in (SLOT_A, SLOT_B):
                dst = slot(w_raw, s, 3 * QL).rearrange("p (k n) -> p k n", n=QL)
                load(s, m2 + 8, [(dst[:, 0:2], wq[:, 0:2, s * QL:(s + 1) * QL]), (dst[:, 2:3], wq[:, 2:3, s * QL:(s + 1) * QL])])
            wkv = a["w_kv_up_2"][0].rearrange("(k p) n -> p k n", p=P)
            dst = w_raw[:, SLOT_D, :].rearrange("p (k n) -> p k n", n=D)
            load(SLOT_D, D0["M2"], [(dst[:, j], wkv[:, j, :]) for j in range(2)])
            for s in (SLOT_A, SLOT_B):
                load_k4(s, m2 + 9, wm, 0, s * NB, NB)
            for n in range(2):
                for s in (SLOT_A, SLOT_B):
                    load_k4(s, m2 + 10 + n, w_out2, 4 * s, n * NB, NB)
            load_gu("F3", SLOT_A, 0)
            load_gu("F3", SLOT_B, 0)
            nothing = lambda: None
            ffn_loads("F3", nothing, nothing)
            sp.wait_ge(gate_out, 12)
            sp.dma_start(post_gain[:, 0, :], a["final_norm_2"].rearrange("(a n) -> a n", a=1).broadcast_to([P, D]))\
                .then_inc(post_loaded[0], 16)
            for t in range(T):
                sp.wait_ge(y_ready, 12 + t + 1)
                sp.dma_start(out[0, t * P:(t + 1) * P, :], y_row[:, t, :]).then_inc(out_stored, 16)
            sp.wait_ge(out_stored, 16 * T)

        @block.gpsimd
        def _(pool):
            pool.memset(ones[:], 1.0).then_inc(pool_step, 1)
            pool.memset(minus_half[:], -0.5).then_inc(pool_step, 1)
            pool.wait_ge(pool_step, 2)
            pool.affine_select(out=ident[:], in_=ones[:], compare_op=ALU.is_equal, fill=0.0, base=0,
                               pattern=[[-1, P]], channel_multiplier=1).then_inc(const_ready, 1)
            pool.affine_select(out=tri[:], in_=ones[:], compare_op=ALU.is_ge, fill=0.0, base=0,
                               pattern=[[-1, P]], channel_multiplier=1).then_inc(const_ready, 1)
            pool.memset(first_acc, 0.0).then_inc(acc_zero, 1)

            def zero_acc(f):
                wait(pool, h_done, 2 * NORM[f])
                if f == "F0":
                    pool.wait_ge(toe_stored, 16)
                elif f == "F2":
                    pool.wait_ge(gate_out, 6)
                    pool.wait_ge(cols_out, 3)
                for half, (_, _, n, _, at) in enumerate(ada_steps[f]):
                    pool.memset(mod_acc[:, half, 0:at + n], 0.0).then_inc(acc_zero, 1)

            def rms(name, dst, ss, s, v):
                pool.wait_ge(s, v)
                pool.tensor_scalar(ss, ss, EPS, None, ALU.add).then_inc(pool_step, 1)
                pool.wait_ge(pool_step, 3 + len(made))
                pool.tensor_tensor(dst, ss, minus_half[:, 0:dst.shape[1]], ALU.pow).then_inc(rms_done, 1)
                made.append(name)

            def norm_rms(f):
                for t in range(T):
                    rms(f"{f} {t}", stat[:, 8 + t:9 + t], stat[:, t:t + 1], sq_done, 2 * NORM[f] + 1 + t)

            def post_rms(f):
                for t in range(T):
                    rms(f"post {f} {t}", stat[:, 10 + t:11 + t], stat[:, 2 + t:3 + t], fsq_done,
                        2 * {"F0": 0, "M1": 1, "F1": 2}[f] + 1 + t)

            made = []
            norm_rms("F0")
            zero_acc("F0")
            post_rms("F0")
            norm_rms("M1")
            rms("index keys", stat[:, 14:16], stat[:, 12:14], ki_sq, 1)

            def causal(v, reps, fill, strict_from=None):
                if strict_from is None:
                    return pool.affine_select(out=v, in_=v, compare_op=ALU.is_ge, fill=fill, base=0,
                                              pattern=[[0, reps], [-1, P]], channel_multiplier=1)
                return pool.affine_select(out=v, in_=v, compare_op=ALU.is_ge, fill=fill, base=-1,
                                          pattern=[[0, reps], [1, P]], channel_multiplier=-1)

            diag = lambda v: v[:, P:CAUSAL].rearrange("p (r x) -> p r x", x=P)
            pool.wait_ge(u_ready, 1)
            for c0 in (0, 2 * P):
                causal(u_sb[:, :, c0:c0 + P], H, 0.0, True).then_inc(u_masked, 1)
            pool.wait_ge(idx_acc, 2 * H)
            causal(diag(score), 2, FUTURE).then_inc(score_causal, 1)
            pool.wait_ge(a_exp, 1)
            for c0 in (0, 2 * P):
                causal(z_sb[:, :, c0:c0 + P], H, 0.0, True).then_inc(a_masked, 1)
            rms("M1 out b", stat[:, 12:14], stat[:, 4:6], osq_done, 2)
            pool.wait_ge(sel_ready, 1)
            causal(diag(work), 2, OFF).then_inc(mask_ready, 1)
            rms("M1 out a", stat[:, 14:16], stat[:, 6:8], osq_done, 4)
            post_rms("M1")
            norm_rms("F1")
            zero_acc("F1")
            post_rms("F1")
            norm_rms("F2")
            zero_acc("F2")
            norm_rms("M2")
            rms("q latent", stat[:, 48:50], stat[:, 4:6], lat_sq, 4)
            rms("kv latent", stat[:, 50:52], stat[:, 6:8], lat_sq, 4)
            norm_rms("F3")
            zero_acc("F3")
            norm_rms("end")
            assert made == RMS

        @block.scalar
        def _(act):
            copy = lambda o, i: act.activation(o, i, ACT.Copy)

            def split_hi(s, use, n=PIECE):
                act.wait_ge(raw_loaded[s], use * 32 + 32)
                wait(act, w_used[s], use)
                copy(slot(w_hi, s, n), slot(w_raw, s, n)).then_inc(hi_ready[s], 1)

            def norm(f):
                r = NORM[f]
                for t in range(T):
                    if r:
                        act.wait_ge(h_done, 2 * r - 1 + t)
                    else:
                        act.wait_ge(x_loaded, 16 * T)
                    act.activation(y_row[:, t, :], x_res[:, t, :], ACT.Square, scale=D ** -0.5, accum_out=stat[:, t:t + 1]).then_inc(sq_done, 1)
                norm_hi(TR[f])

            def norm_hi(r):
                for j in range(KD // 2):
                    act.wait_ge(n_ready, 8 * r + 2 * j + 2)
                    copy(nT_hi[:, 2 * j:2 * j + 2, :], nT[:, 2 * j:2 * j + 2, :]).then_inc(n_hi, 1)

            def body(f, c, down=True, gu=True, nxt=PIECE):
                i = FFN.index(f) * NC
                if down:
                    split_hi(SLOT_D, c - 1 + D0[f])
                    act.wait_ge(h_ready, c + i)
                    copy(hT_hi[:], h_act[:]).then_inc(ht_hi, 1)
                if nxt:
                    split_hi(SLOT_A, c + 1 + AB0[f], nxt)
                if gu:
                    act.wait_ge(w_used[SLOT_B], c + 1 + AB0[f])
                    wait(act, h_ready, c + i)
                    act.activation(sil[:], ps[:, 0, :].rearrange("p (k n) -> p k n", n=S), ACT.Silu).then_inc(silu_done, 1)
                if nxt:
                    split_hi(SLOT_B, c + 1 + AB0[f], nxt)

            def ffn(f, nxt=PIECE):
                norm(f)
                body(f, 0, down=False)
                body(f, 1)
                with act.Fori(2, NC - 1) as c:
                    body(f, c)
                body(f, NC - 1, nxt=nxt)
                body(f, NC, gu=False, nxt=0)

            def residual_sq(stage):
                for t in range(T):
                    output_ready(act, stage, t)
                    b = output_at(stage, t)
                    act.activation(y_row[:, t, :], ps[:, b:b + 2, :].rearrange("p b n -> p (b n)"),
                                   ACT.Square, scale=D ** -0.5, accum_out=stat[:, 2 + t:3 + t]).then_inc(fsq_done, 1)

            act.wait_ge(c_loaded, 32)
            act.activation(c_act[:], c_in[:], ACT.Silu).then_inc(c_ready, 1)
            for h in range(H):
                act.wait_ge(toe_mm, h + 1)
                copy(toe_bc[:, h, :], ps[:, h % 4, 0:CAUSAL]).then_inc(toe_sb, 1)
            split_hi(SLOT_A, 0)
            split_hi(SLOT_B, 0)
            ffn("F0")
            residual_sq("F0")
            norm("M1")

            m1 = AB0["M1"]

            def transposed_group(g, i):
                s = SLOT_A if g == KI else SLOT_B
                act.wait_ge(w_used[s], use1(s, g) + 1)
                for b in range(2):
                    copy(qkT[:, i, 2 * b:2 * b + 2, :],
                         ps[:, 2 * (g % 2) + b, :].rearrange("p (k n) -> p k n", n=S)).then_inc(grp_out, 1)

            def row_group(g, i):
                act.wait_ge(w_used[SLOT_B], use1(SLOT_B, g) + 1)
                for t in range(T):
                    copy(v_row[:, i, t, :], ps[:, 2 * (g % 2) + t, :]).then_inc(grp_out, 1)

            def out_squares(half, i):
                for t in range(T):
                    wait(act, osq_done, 2 * i + t - 1)
                    act.activation(x_junk(t), y_row[:, t, half * NB:(half + 1) * NB], ACT.Square, scale=NB ** -0.5,
                                   accum_out=stat[:, 4 + 2 * i + t:5 + 2 * i + t]).then_inc(osq_done, 1)

            split_hi(SLOT_A, use1(SLOT_A, 1))
            split_hi(SLOT_B, use1(SLOT_B, 1))
            split_hi(SLOT_D, D0["M1"])
            transposed_group(0, TQB)
            split_hi(SLOT_A, use1(SLOT_A, 2))
            split_hi(SLOT_B, use1(SLOT_B, 2))
            transposed_group(1, TKB)
            split_hi(SLOT_A, m1 + KI, KD * 72)
            for h in range(H):
                act.wait_ge(z_mm, h + 1)
                act.activation(z_sb[:, h, :], ps[:, 4 + h % 4, 0:CAUSAL], ACT.Copy, scale=DH ** -0.5).then_inc(z_out, 1)
            act.wait_ge(z_out, H)
            act.activation(e_sb[:], z_sb[:], ACT.Abs).then_inc(z_ln, 1)
            split_hi(SLOT_B, use1(SLOT_B, 3))
            act.wait_ge(z_ln, 1)
            act.activation(e_sb[:], e_sb[:], ACT.Exp, scale=-1.0).then_inc(z_ln, 1)
            split_hi(SLOT_A, use1(SLOT_A, 3))
            transposed_group(2, TQI)
            act.wait_ge(z_ln, 2)
            act.activation(e_sb[:], e_sb[:], ACT.Ln, bias=1.0).then_inc(z_ln, 1)
            split_hi(SLOT_A, use1(SLOT_A, 4))
            for h in range(H):
                act.wait_ge(idx_mm, h + 1)
                if h >= 4:
                    act.wait_ge(idx_acc, 2 * (h - 3))
                act.activation(relu[:, h % 4, :], ps[:, 4 + h % 4, 0:CAUSAL], ACT.Relu).then_inc(idx_relu, 1)
            split_hi(SLOT_B, use1(SLOT_B, 4))
            transposed_group(3, TKA)
            split_hi(SLOT_A, use1(SLOT_A, 5))
            act.wait_ge(loga_ready, 1)
            act.activation(z_sb[:], z_sb[:], ACT.Exp).then_inc(a_exp, 1)
            row_group(4, 1)
            split_hi(SLOT_B, use1(SLOT_B, 5))
            split_hi(SLOT_A, use1(SLOT_A, 6))
            act.wait_ge(ob_out, T)
            out_squares(1, 0)
            transposed_group(5, TQA)
            split_hi(SLOT_B, use1(SLOT_B, 6))
            split_hi(SLOT_A, m1 + 8)
            for h in range(H):
                for t in range(T):
                    act.wait_ge(lmax_ready, h + 1)
                    cols = slice(0, S) if t else slice(S, CAUSAL)
                    act.activation(z_sb[:, h, cols], z_sb[:, h, cols], ACT.Exp,
                                   bias=stat[:, 16 + 2 * h + t:17 + 2 * h + t],
                                   accum_out=trig[:, 0, t, h:h + 1]).then_inc(p_exp, 1)
            row_group(6, 0)
            for j in range(2):
                act.wait_ge(n_ready, 8 * TR["O1"] + 2 * j + 2)
                copy(nT_hi[:, 4 + 2 * j:6 + 2 * j, :], ob_T[:, 2 * j:2 * j + 2, :]).then_inc(n_hi, 1)
            for h in range(H):
                if h == 4:
                    split_hi(SLOT_B, m1 + 7)
                act.wait_ge(p_tr, h + 1)
                copy(e_sb[:, h, :], ps[:, 6 + h % 2, 0:CAUSAL]).then_inc(pT_out, 1)
            act.wait_ge(oa_out, T)
            out_squares(0, 1)
            split_hi(SLOT_B, m1 + 8)
            for j in range(2):
                act.wait_ge(n_ready, 8 * TR["O1"] + 2 * j + 6)
                copy(nT_hi[:, 2 * j:2 * j + 2, :], nT[:, 2 * j:2 * j + 2, :]).then_inc(n_hi, 1)
            split_hi(SLOT_A, AB0["F1"])
            split_hi(SLOT_B, AB0["F1"])
            residual_sq("M1")
            ffn("F1")
            residual_sq("F1")
            ffn("F2")
            norm("M2")

            m2 = AB0["M2"]

            def row_out(g, dst, n):
                act.wait_ge(w_used[SLOT_B], m2 + g + 1)
                for t in range(T):
                    copy(dst[:, t], ps[:, 2 * (g % 2) + t, 0:n]).then_inc(grp_out, 1)

            split_hi(SLOT_A, m2 + 1, 4 * 384)
            split_hi(SLOT_B, m2 + 1, 4 * 384)
            row_out(0, uf, NB)
            split_hi(SLOT_A, m2 + 2, 4 * 288)
            split_hi(SLOT_B, m2 + 2, 4 * 288)
            row_out(1, lat[:, :, 0:QL], QL)
            split_hi(SLOT_A, m2 + 3)
            split_hi(SLOT_B, m2 + 3)
            row_out(2, lat[:, :, QL:], KVL + ROPE)
            act.wait_ge(grp_out, 14 + 6)
            for t in range(T):
                wait(act, lat_sq, 2 * t)
                act.activation(x_junk(0)[:, 0:QL], lat[:, t, 0:QL], ACT.Square, scale=QL ** -0.5,
                               accum_out=stat[:, 4 + t:5 + t]).then_inc(lat_sq, 1)
                act.activation(x_junk(1)[:, 0:KVL], lat[:, t, QL:QL + KVL], ACT.Square, scale=KVL ** -0.5,
                               accum_out=stat[:, 6 + t:7 + t]).then_inc(lat_sq, 1)
            act.wait_ge(trig_arg, 1)
            act.activation(trig[:, 1], trig[:, 0], ACT.Sin).then_inc(trig_done, 1)
            act.activation(trig[:, 2], trig[:, 0], ACT.Sin, scale=0.5).then_inc(trig_done, 1)
            split_hi(SLOT_A, m2 + 4)
            for g in range(4):
                act.wait_ge(cu_mm, g + 1)
                copy(cu[:, g, :], ps[:, 4 + g, :]).then_inc(cu_out, 1)
            split_hi(SLOT_B, m2 + 4)

            def gate_group(i):
                act.wait_ge(w_used[SLOT_B], m2 + 3 + i + 1)
                for t in range(T):
                    act.activation(sig[:, t, i * NB:(i + 1) * NB], ps[:, 2 * ((3 + i) % 2) + t, :], ACT.Sigmoid).then_inc(grp_out, 1)

            gate_group(0)
            split_hi(SLOT_A, m2 + 5)
            split_hi(SLOT_B, m2 + 5)
            gate_group(1)
            split_hi(SLOT_A, m2 + 6)
            split_hi(SLOT_B, m2 + 6)
            gate_group(2)
            split_hi(SLOT_A, m2 + 7)
            split_hi(SLOT_B, m2 + 7)
            split_hi(SLOT_D, D0["M2"])
            gate_group(3)
            act.wait_ge(w_used[SLOT_B], m2 + 7)
            act.wait_ge(f_out, 4)
            copy(nT_hi[:, 4:8, :], nT[:, 4:8, :]).then_inc(f_hi, 1)
            act.wait_ge(lat_out, 5)
            copy(nT_hi[:, 0:3, :], nT[:, 0:3, :]).then_inc(lat_hi, 1)
            copy(hT_hi[:], h_act[:]).then_inc(lat_hi, 1)
            split_hi(SLOT_A, m2 + 8, 3 * QL)
            split_hi(SLOT_B, m2 + 8, 3 * QL)
            act.wait_ge(w_used[SLOT_D], D0["M2"] + 1)
            for t in range(T):
                for n in range(2):
                    copy(kv_row[:, t, n * NB:(n + 1) * NB], ps[:, 2 * t + n, :]).then_inc(up_out, 1)
            split_hi(SLOT_A, m2 + 9)
            split_hi(SLOT_B, m2 + 9)
            for i in range(8):
                act.wait_ge(qk_tr, i + 1)
                dst = kT if i < 4 else qT
                copy(dst[0:QH, 2 * (i % 4):2 * (i % 4) + 2, :],
                     ps[0:QH, i % 4, :].rearrange("p (k n) -> p k n", n=S)).then_inc(qkT_out, 1)
            for h in range(H):
                act.wait_ge(smax_ready, h + 1)
                if h >= 4:
                    act.wait_ge(s_tr, h - 3)
                for t in range(T):
                    act.activation(prob4[:, h % 4, t * S:(t + 1) * S], ps[:, (4, 5, 2, 3)[h % 4], t * S:(t + 1) * S], ACT.Exp,
                                   bias=stat[:, 16 + 2 * h + t:17 + 2 * h + t],
                                   accum_out=trig[:, 0, t, h:h + 1]).then_inc(s_exp, 1)
            act.wait_ge(omT_out, 4)
            copy(nT_hi[:, 0:4, :], nT[:, 0:4, :]).then_inc(omT_hi, 1)
            split_hi(SLOT_A, m2 + 10)
            split_hi(SLOT_B, m2 + 10)
            norm_hi(TR["O2"])
            split_hi(SLOT_A, m2 + 11)
            split_hi(SLOT_B, m2 + 11)
            split_hi(SLOT_A, AB0["F3"])
            split_hi(SLOT_B, AB0["F3"])
            ffn("F3", nxt=0)
            for t in range(T):
                act.wait_ge(h_done, 11 + t)
                act.activation(y_row[:, t, :], x_res[:, t, :], ACT.Square, scale=D ** -0.5, accum_out=stat[:, t:t + 1]).then_inc(sq_done, 1)

        @block.vector
        def _(dve):
            steps = [0]

            def link(ins):
                steps[0] += 1
                ins.then_inc(dve_step, 1)
                dve.wait_ge(dve_step, steps[0])

            def split_lo(s, use, n=PIECE):
                dve.wait_ge(hi_ready[s], use + 1)
                dve.tensor_tensor(slot(w_lo, s, n), slot(w_raw, s, n), slot(w_hi, s, n).bitcast(F32),
                                  ALU.subtract).then_inc(lo_ready[s], 1)

            def norm(f):
                r = NORM[f]
                for t in range(T):
                    rms_ready(dve, f"{f} {t}")
                    dve.tensor_scalar(y_row[:, t, :], x_res[:, t, :], stat[:, 8 + t:9 + t], None, ALU.mult).then_inc(y_ready, 1)
                if r == 0:
                    first_mods()
                cols = mod_col[:, r]
                norm_out(TR[f], lambda k, src: (dve.tensor_scalar(nT[:, k, :], src, cols[:, 0, k:k + 1], cols[:, 1, k:k + 1],
                                                              ALU.mult, ALU.add)))

            def norm_out(r, scaled):
                def lo(j):
                    dve.wait_ge(n_hi, 4 * r + j + 1)
                    dve.tensor_tensor(nT_lo[:, 2 * j:2 * j + 2, :], nT[:, 2 * j:2 * j + 2, :],
                                      nT_hi[:, 2 * j:2 * j + 2, :].bitcast(F32), ALU.subtract).then_inc(n_lo, 1)
                for j in range(KD // 2):
                    dve.wait_ge(n_tr, 4 * r + j + 1)
                    for k in (2 * j, 2 * j + 1):
                        scaled(k, ps[:, 4 + j, (k % 2) * S:(k % 2 + 1) * S]).then_inc(n_ready, 1)
                    if j:
                        lo(j - 1)
                lo(KD // 2 - 1)

            def cols_out_(sums, n):
                dve.wait_ge(acc_cols, n + 1)
                for i, (_, blk, m, r) in enumerate(sums):
                    src = ps[:, 3, KD * i:KD * i + KD]
                    b = vec_col[:, blk, KD * m:KD * m + KD]
                    if m % 3 == 0:
                        last = dve.tensor_tensor(mod_col[:, r, 1, :], src, b, ALU.add)
                        link(last)
                    else:
                        g = gain_at.get(r, (0, 72))
                        link(dve.tensor_tensor(mod_col[:, r, 0, :], src, b, ALU.add))
                        link(dve.scalar_tensor_tensor(mod_col[:, r, 0, :], mod_col[:, r, 0, :], 1.0,
                                                      vec_col[:, g[0], g[1]:g[1] + KD], ALU.add, ALU.mult))
                dve.sem_inc(cols_out, 1)

            def gate_half(f, i, half):
                _, _, buf, post, factor = gates[f][i]
                n = 2 * (n_gates[f] + i) + half
                v = gate[:, buf, half * NB:(half + 1) * NB]
                dve.wait_ge(gate_loaded[buf], 16 * (n_buf[f][buf] + 1))
                dve.wait_ge(acc_gate, n + 1)
                link(dve.tensor_tensor(v, ps[:, 2 + half, :], v, ALU.add))
                if post is None:
                    dve.tensor_scalar(v, v, factor, None, ALU.mult).then_inc(gate_out, 1)
                else:
                    dve.wait_ge(post_loaded[i], 16 * {"F0": 1, "F1": 2}[f])
                    dve.scalar_tensor_tensor(v, v, factor, post_gain[:, i, half * NB:(half + 1) * NB],
                                             ALU.mult, ALU.mult).then_inc(gate_out, 1)

            def ada(f, half, j):
                if half >= len(ada_steps[f]):
                    return
                _, _, n, blk, at = ada_steps[f][half]
                dve.wait_ge(ada_loaded[half], j * 16 + 16 * (n_ada[f] + 1))
                wait(dve, ada_done[half], j + n_ada[f])
                cj = c_act[:, blk, bass.ds(j, 1)] if not isinstance(j, int) else c_act[:, blk, j:j + 1]
                acc = mod_acc[:, half, at:at + n]
                dve.scalar_tensor_tensor(acc, ada_raw[:, half, 0:n], cj, acc, ALU.mult, ALU.add).then_inc(ada_done[half], 1)

            def rest(f, step):
                if f not in ada_rest:
                    return
                blk, half = ada_rest[f][2], step % 2
                acc = mod_acc[:, 1, 0:D]
                dve.wait_ge(ada_loaded[half], 16 * (n_ada[f] + KD + step // 2 + 1))
                if step:
                    dve.wait_ge(ada_done[1 - half], n_ada[f] + KD + (step + 1) // 2)
                link(dve.scalar_tensor_tensor(acc, ada_raw[:, half, 0:D], c_act[:, blk, 2 * step:2 * step + 1], acc,
                                              ALU.mult, ALU.add))
                dve.scalar_tensor_tensor(acc, ada_raw[:, half, D:2 * D], c_act[:, blk, 2 * step + 1:2 * step + 2], acc,
                                         ALU.mult, ALU.add).then_inc(ada_done[half], 1)

            def body(f, c, down=True, gu=True, nxt=PIECE, mods=False, hooks=((), (), ())):
                i = FFN.index(f) * NC
                if down:
                    split_lo(SLOT_D, c - 1 + D0[f])
                    for hook in hooks[0]:
                        hook()
                    if mods:
                        ada(f, 0, c - 1)
                    dve.wait_ge(ht_hi, c + i)
                    dve.tensor_tensor(hT_lo[:], h_act[:], hT_hi[:].bitcast(F32), ALU.subtract).then_inc(ht_lo, 1)
                    for hook in hooks[1]:
                        hook()
                    if mods:
                        ada(f, 1, c - 1)
                if nxt:
                    split_lo(SLOT_A, c + 1 + AB0[f], nxt)
                if gu:
                    dve.wait_ge(silu_done, c + i + 1)
                    wait(dve, ht_lo, c + i)
                    dve.tensor_tensor(h_act[:], ps[:, 1, :].rearrange("p (k n) -> p k n", n=S), sil[:], ALU.mult)\
                        .then_inc(h_ready, 1)
                if nxt:
                    split_lo(SLOT_B, c + 1 + AB0[f], nxt)
                for hook in hooks[2]:
                    hook()

            def ffn(f, nxt=PIECE):
                norm(f)
                body(f, 0, down=False)
                dve.wait_ge(acc_zero, 1 + {"F0": 2, "F1": 4, "F2": 6, "F3": 7}[f])
                with dve.Fori(1, KD + 1) as c:
                    body(f, c, mods=True)
                body(f, NC - 2, hooks=([lambda: rest(f, 0)],
                                       [lambda: cols_out_(col_sums[f], n_cols[f])] if col_sums[f] else (),
                                       [lambda: rest(f, 1), lambda: gate_half(f, 0, 0)]))
                body(f, NC - 1, nxt=nxt, hooks=([lambda: rest(f, 2)], [lambda: gate_half(f, 0, 1)], [lambda: rest(f, 3)]))
                body(f, NC, gu=False, nxt=0)

            def residual(stage, buf, post):
                for t in range(T):
                    b = output_at(stage, t)
                    src = ps[:, b:b + 2, :].rearrange("p b n -> p (b n)")
                    if post:
                        rms_ready(dve, f"post {stage} {t}")
                        link(dve.scalar_tensor_tensor(y_row[:, t, :], src, stat[:, 10 + t:11 + t], gate[:, buf, :],
                                                      ALU.mult, ALU.mult))
                    else:
                        output_ready(dve, stage, t)
                        link(dve.tensor_tensor(y_row[:, t, :], src, gate[:, buf, :], ALU.mult))
                    dve.tensor_tensor(x_res[:, t, :], x_res[:, t, :], y_row[:, t, :], ALU.add).then_inc(h_done, 1)

            def first_mods():
                dve.wait_ge(vec_tr, 1)
                for b in range(2):
                    dve.tensor_copy(vec_col[:, b, 0:VECS[b]], ps[:, 7, b * P:b * P + VECS[b]]).then_inc(vec_ready, 1)
                dve.wait_ge(vec_ready, 2)
                cols_out_([(0, 0, 0, 0), (D, 0, 1, 0)], 0)

            dve.wait_ge(c_ready, 1)
            dve.wait_ge(acc_zero, 1)
            for j in range(KD):
                dve.wait_ge(ada_loaded[j % 2], 16 * (j // 2 + 1))
                if j:
                    dve.wait_ge(ada_done[(j - 1) % 2], (j - 1) // 2 + 1)
                dve.scalar_tensor_tensor(first_acc, ada_raw[:, j % 2, 0:2 * D], c_act[:, 0, j:j + 1], first_acc,
                                         ALU.mult, ALU.add).then_inc(ada_done[j % 2], 1)
                if j == 2:
                    dve.wait_ge(small_loaded, SMALL)
                    dve.tensor_copy(rel_bc[0:BUCKETS], rel_in[0:BUCKETS, :].rearrange("p (h o) -> p h o", o=1)
                                    .broadcast_to([BUCKETS, H, P])).then_inc(rel_ready, 1)
            split_lo(SLOT_A, 0)
            split_lo(SLOT_B, 0)
            ffn("F0")
            residual("F0", 0, True)

            m1 = AB0["M1"]
            norm("M1")
            gate_half("F0", 1, 0)
            gate_half("F0", 1, 1)
            split_lo(SLOT_A, use1(SLOT_A, 1))
            split_lo(SLOT_B, use1(SLOT_B, 1))
            split_lo(SLOT_D, D0["M1"])
            split_lo(SLOT_A, use1(SLOT_A, 2))
            split_lo(SLOT_B, use1(SLOT_B, 2))
            split_lo(SLOT_A, m1 + KI, KD * 72)
            split_lo(SLOT_B, use1(SLOT_B, 3))
            dve.wait_ge(w_used[SLOT_A], m1 + KI + 1)
            for t in range(T):
                link(dve.tensor_copy(kw_row[:, t, :], ps[:, 4 + t, 0:72]))
                link(dve.tensor_scalar(wi[:, t * H:(t + 1) * H], kw_row[:, t, 64:72], (H * DH) ** -0.5, None, ALU.mult))
            link(dve.scalar_tensor_tensor(ki2[:, :, 0:DH], kw_row[:, :, 0:DH], 1.0 / DH, kw_row[:, :, 0:DH], ALU.mult, ALU.mult))
            dve.tensor_reduce(stat[:, 12:14], ki2[:, :, 0:DH], AX.X, ALU.add).then_inc(ki_sq, 1)
            rms_ready(dve, "index keys")
            for t in range(T):
                for half in range(2):
                    link(dve.scalar_tensor_tensor(ki2[:, t, half * DH:(half + 1) * DH], kw_row[:, t, 0:DH], stat[:, 14 + t:15 + t],
                                                  gki[:], ALU.mult, ALU.mult))
            dve.sem_inc(ki_ready, 1)
            split_lo(SLOT_A, use1(SLOT_A, 3))
            dve.wait_ge(ki_tr, 1)
            dve.tensor_copy(kiT[:], ps[:, 6, 0:S]).then_inc(kiT_ready, 1)
            dve.wait_ge(z_ln, 3)
            dve.scalar_tensor_tensor(u_sb[:], z_sb[:], 0.0, e_sb[:], ALU.max, ALU.add).then_inc(u_ready, 1)
            split_lo(SLOT_A, use1(SLOT_A, 4))
            for h in range(H):
                dve.wait_ge(idx_relu, h + 1)
                for t in (1, 0):
                    cols = slice(0, S) if t else slice(S, CAUSAL)
                    w = wi[:, t * H + h:t * H + h + 1]
                    if h == 0:
                        dve.tensor_scalar(score[:, cols], relu[:, 0, cols], w, None, ALU.mult).then_inc(idx_acc, 1)
                    else:
                        dve.wait_ge(idx_acc, 2 * h)
                        dve.scalar_tensor_tensor(score[:, cols], relu[:, h % 4, cols], w, score[:, cols],
                                                 ALU.mult, ALU.add).then_inc(idx_acc, 1)

            def topk(first, last):
                for r in range(first, last):
                    for t in (1, 0):
                        cols = slice(0, S) if t else slice(S, CAUSAL)
                        src = score if r == 0 else work
                        dve.max(stat[:, 48 + 8 * t:56 + 8 * t], src[:, cols]).then_inc(top_found, 1)
                    for t in (1, 0):
                        cols = slice(0, S) if t else slice(S, CAUSAL)
                        src = score if r == 0 else work
                        dve.wait_ge(top_found, 2 * r + 2 - t)
                        dve.match_replace(out=work[:, cols], in_to_replace=stat[:, 48 + 8 * t:56 + 8 * t],
                                          in_values=src[:, cols], imm_value=DONE).then_inc(top_taken, 1)
                    dve.wait_ge(top_taken, 2 * r + 2)

            split_lo(SLOT_B, use1(SLOT_B, 4))
            dve.wait_ge(score_causal, 1)
            topk(0, 2)
            for h in range(H):
                dve.wait_ge(r_mm, h + 1)
                dve.tensor_tensor(z_sb[:, h, :], z_sb[:, h, :], ps[:, 4 + h % 4, 0:CAUSAL], ALU.subtract).then_inc(r_out, 1)
            dve.wait_ge(r_out, H)
            dve.tensor_scalar(z_sb[:], z_sb[:], 0.0, None, ALU.min).then_inc(loga_ready, 1)
            split_lo(SLOT_A, use1(SLOT_A, 5))
            topk(2, 5)
            split_lo(SLOT_B, use1(SLOT_B, 5))
            split_lo(SLOT_A, use1(SLOT_A, 6))
            for t in range(T):
                dve.wait_ge(ob_mm, 1)
                dve.tensor_copy(y_row[:, t, NB:2 * NB], ps[:, 4 + t, :]).then_inc(ob_out, 1)
            topk(5, TOPK // 8)
            dve.tensor_scalar(work[:], work[:], DONE, OFF, ALU.not_equal, ALU.mult).then_inc(sel_ready, 1)
            rms_ready(dve, "M1 out b")
            for t in range(T):
                v = y_row[:, t, NB:2 * NB]
                link(dve.tensor_scalar(v, v, stat[:, 12 + t:13 + t], None, ALU.mult))
            dve.sem_inc(ob_ready, 1)
            dve.wait_ge(bias_loaded, 16 * H)
            dve.wait_ge(mask_ready, 1)
            dve.wait_ge(r_mm, H)
            for cols, src in ((slice(0, S), bias[:, :, :]), (slice(S, CAUSAL), bias[:, :, P:S])):
                w = work[:, cols]
                n = w.shape[1]
                link(dve.tensor_tensor(u_sb[:, :, cols], src, w.rearrange("p (o n) -> p o n", o=1).broadcast_to([P, H, n]), ALU.add))
            split_lo(SLOT_B, use1(SLOT_B, 6))

            def out_half(first_bank, first_k, j0, o_T):
                for j in range(2):
                    dve.wait_ge(n_tr, 4 * TR["O1"] + j0 + j + 1)
                    for i in range(2):
                        k = 2 * j + i
                        dve.tensor_scalar(o_T[:, k, :], ps[:, first_bank + j, i * S:(i + 1) * S],
                                          vec_col[:, 0, 96 + first_k + k:97 + first_k + k], None, ALU.mult).then_inc(n_ready, 1)

            def out_lo(first_k, j0, o_T):
                for j in range(2):
                    dve.wait_ge(n_hi, 4 * TR["O1"] + j0 + j + 1)
                    k = slice(first_k + 2 * j, first_k + 2 * j + 2)
                    dve.tensor_tensor(nT_lo[:, k, :], o_T[:, 2 * j:2 * j + 2, :], nT_hi[:, k, :].bitcast(F32),
                                      ALU.subtract).then_inc(n_lo, 1)

            out_half(2, 4, 0, ob_T)
            for h in range(H):
                dve.wait_ge(l_mm, h + 1)
                link(dve.scalar_tensor_tensor(z_sb[:, h, :], ps[:, 4 + h % 4, 0:CAUSAL], DH ** -0.5, u_sb[:, h, :],
                                              ALU.mult, ALU.add))
                dve.sem_inc(l_out, 1)
                for t in range(T):
                    cols = slice(0, S) if t else slice(S, CAUSAL)
                    m = stat[:, 16 + 2 * h + t:17 + 2 * h + t]
                    link(dve.tensor_reduce(m, z_sb[:, h, cols], AX.X, ALU.max, negate=True))
                dve.sem_inc(lmax_ready, 1)
            split_lo(SLOT_A, m1 + 8)
            dve.wait_ge(p_exp, 2 * H)
            link(dve.reciprocal(trig[:, 1, :, 0:H], trig[:, 0, :, 0:H]))
            out_lo(4, 0, ob_T)
            split_lo(SLOT_B, m1 + 7)
            dve.wait_ge(oa_mm, 1)
            for t in range(T):
                rs = trig[:, 1, t, 0:H].rearrange("p (h o) -> p h o", o=1).broadcast_to([P, H, DH])
                dve.tensor_tensor(y_row[:, t, 0:NB].rearrange("p (h d) -> p h d", d=DH),
                                  ps[:, t, :].rearrange("p (h d) -> p h d", d=DH), rs, ALU.mult).then_inc(oa_out, 1)
            rms_ready(dve, "M1 out a")
            for t in range(T):
                v = y_row[:, t, 0:NB]
                link(dve.tensor_scalar(v, v, stat[:, 14 + t:15 + t], None, ALU.mult))
            dve.sem_inc(o_ready, 1)
            out_half(6, 0, 2, nT)
            out_lo(0, 2, nT)
            split_lo(SLOT_B, m1 + 8)
            split_lo(SLOT_A, AB0["F1"])
            split_lo(SLOT_B, AB0["F1"])
            residual("M1", 1, True)
            ffn("F1")
            residual("F1", 0, True)
            ffn("F2")
            residual("F2", 0, False)

            m2 = AB0["M2"]
            norm("M2")
            gate_half("F2", 1, 0)
            gate_half("F2", 1, 1)
            link(dve.tensor_copy(pos_f[:], pos_i[:]))
            for t in range(T):
                link(dve.tensor_scalar(angle[:, t, :], freq[:], pos_f[:, t:t + 1], None, ALU.mult))
            link(dve.tensor_scalar(trig[:, 3], angle[:], 0.15915494309189535, ROUND, ALU.mult, ALU.add))
            link(dve.tensor_scalar(trig[:, 3], trig[:, 3], ROUND, None, ALU.subtract))
            for part in TWO_PI:
                link(dve.scalar_tensor_tensor(angle[:], trig[:, 3], -part, angle[:], ALU.mult, ALU.add))
            dve.tensor_scalar(trig[:, 0], angle[:], PI, -PI, ALU.min, ALU.max).then_inc(trig_arg, 1)
            split_lo(SLOT_A, m2 + 1, 4 * 384)
            split_lo(SLOT_B, m2 + 1, 4 * 384)
            split_lo(SLOT_A, m2 + 2, 4 * 288)
            split_lo(SLOT_B, m2 + 2, 4 * 288)
            split_lo(SLOT_A, m2 + 3)
            split_lo(SLOT_B, m2 + 3)
            dve.wait_ge(trig_done, 2)
            link(dve.tensor_tensor(trig[:, 4], trig[:, 2], trig[:, 2], ALU.mult))
            link(dve.tensor_scalar(trig[:, 4], trig[:, 4], -2.0, 1.0, ALU.mult, ALU.add))
            rms_ready(dve, "kv latent")
            for t in range(T):
                dve.tensor_scalar(lat[:, t, 0:QL], lat[:, t, 0:QL], stat[:, 48 + t:49 + t], None, ALU.mult).then_inc(lat_ready, 1)
                dve.tensor_scalar(lat[:, t, QL:QL + KVL], lat[:, t, QL:QL + KVL], stat[:, 50 + t:51 + t], None, ALU.mult)\
                    .then_inc(lat_ready, 1)
            split_lo(SLOT_A, m2 + 4)
            split_lo(SLOT_B, m2 + 4)
            split_lo(SLOT_A, m2 + 5)
            split_lo(SLOT_B, m2 + 5)
            dve.wait_ge(f_mm, 1)
            for g in range(4):
                dve.tensor_copy(nT[:, 4 + g, :], ps[:, 4 + g // 2, (g % 2) * S:(g % 2 + 1) * S]).then_inc(f_out, 1)
            split_lo(SLOT_A, m2 + 6)
            split_lo(SLOT_B, m2 + 6)
            dve.wait_ge(lat_tr, 1)
            for k in range(5):
                src = ps[:, (6, 6, 7, 7, 4)[k], (k % 2) * S:(k % 2 + 1) * S]
                dst = nT[:, k, :] if k < 3 else h_act[:, k - 3, :]
                dve.tensor_scalar(dst, src, vec_col[:, 1, 96 + k:97 + k], None, ALU.mult).then_inc(lat_out, 1)
            split_lo(SLOT_A, m2 + 7)
            split_lo(SLOT_B, m2 + 7)
            split_lo(SLOT_D, D0["M2"])
            dve.wait_ge(f_hi, 1)
            dve.tensor_tensor(nT_lo[:, 4:8, :], nT[:, 4:8, :], nT_hi[:, 4:8, :].bitcast(F32), ALU.subtract).then_inc(f_lo, 1)
            dve.wait_ge(lat_hi, 2)
            dve.tensor_tensor(nT_lo[:, 0:3, :], nT[:, 0:3, :], nT_hi[:, 0:3, :].bitcast(F32), ALU.subtract).then_inc(lat_lo, 1)
            dve.tensor_tensor(hT_lo[:], h_act[:], hT_hi[:].bitcast(F32), ALU.subtract).then_inc(lat_lo, 1)
            dve.wait_ge(grp_out, 28)
            dve.wait_ge(w_used[SLOT_B], m2 + 8)
            for t in range(T):
                dve.tensor_tensor(sig[:, t, 0:D], ps[:, 4 + 2 * t:6 + 2 * t, :].rearrange("p b n -> p (b n)"),
                                  sig[:, t, 0:D], ALU.mult).then_inc(ya_out, 1)
            split_lo(SLOT_A, m2 + 8, 3 * QL)
            split_lo(SLOT_B, m2 + 8, 3 * QL)
            cos, sin = trig[:, 4], trig[:, 1]

            def rotate(x1, x2, o1, o2, tmp, co, si):
                link(dve.tensor_tensor(tmp[:, 0], x1, co, ALU.mult))
                link(dve.tensor_tensor(tmp[:, 1], x2, si, ALU.mult))
                link(dve.tensor_tensor(tmp[:, 2], x2, co, ALU.mult))
                link(dve.tensor_tensor(tmp[:, 3], x1, si, ALU.mult))
                link(dve.tensor_tensor(o1, tmp[:, 0], tmp[:, 1], ALU.subtract))
                link(dve.tensor_tensor(o2, tmp[:, 2], tmp[:, 3], ALU.add))

            tmp = sil[:].rearrange("p t n -> p (t n)").rearrange("p (q h r) -> p q h r", q=4, r=16)
            k_rot = trig[:, 2, :, :]
            k_rot2 = trig[:, 5, :, :]
            for t in range(T):
                r = lat[:, t, QL + KVL:QL + KVL + ROPE]
                rotate(r[:, 0:16], r[:, 16:32], k_rot[:, t, :], k_rot2[:, t, :],
                       tmp[:, :, 0, :], cos[:, t, :], sin[:, t, :])
            dve.wait_ge(up_out, 4)
            for t in range(T):
                kr = k_row[:, t, :].rearrange("p (h d) -> p h d", d=QH)
                link(dve.tensor_copy(kr[:, :, 0:QK], kv_row[:, t, :].rearrange("p (h d) -> p h d", d=P)[:, :, 0:QK]))
                for o, src in ((QK, k_rot), (QK + 16, k_rot2)):
                    link(dve.tensor_copy(kr[:, :, o:o + 16], src[:, t, :].rearrange("p (o r) -> p o r", o=1).broadcast_to([P, H, 16])))
            dve.sem_inc(qk_ready, 1)
            dve.wait_ge(w_used[SLOT_B], m2 + 9)
            for t in range(T):
                for n in range(2):
                    link(dve.tensor_scalar(q_row[:, t, n * QL:(n + 1) * QL], ps[:, 4 + 2 * t + n, 0:QL], QH ** -0.5, None, ALU.mult))
            for t in range(T):
                qr = q_row[:, t, :].rearrange("p (h d) -> p h d", d=QH)
                co = cos[:, t, :].rearrange("p (o r) -> p o r", o=1).broadcast_to([P, H, 16])
                si = sin[:, t, :].rearrange("p (o r) -> p o r", o=1).broadcast_to([P, H, 16])
                rotate(qr[:, :, QK:QK + 16], qr[:, :, QK + 16:QH], qr[:, :, QK:QK + 16], qr[:, :, QK + 16:QH], tmp, co, si)
            dve.sem_inc(qk_ready, 1)
            split_lo(SLOT_A, m2 + 9)
            split_lo(SLOT_B, m2 + 9)

            def softmax_max(h):
                dve.wait_ge(s_mm, h + 1)
                m = stat[:, 16 + 2 * h:18 + 2 * h]
                dve.tensor_reduce(m, ps[:, (4, 5, 2, 3)[h % 4], :].rearrange("p (t n) -> p t n", n=S), AX.X, ALU.max,
                                  negate=True).then_inc(smax_ready, 1)

            def probs_out(h):
                dve.wait_ge(s_tr, h + 1)
                if h >= 2:
                    dve.wait_ge(om_mm, h - 1)
                dve.tensor_copy(probT[:, h % 2, :], ps[:, 6 + h % 2, :]).then_inc(sT_out, 1)

            softmax_max(0)
            softmax_max(1)
            for h in range(H):
                if h + 2 < H:
                    softmax_max(h + 2)
                probs_out(h)
            dve.wait_ge(s_exp, 2 * H)
            link(dve.reciprocal(trig[:, 2, :, 0:H], trig[:, 0, :, 0:H]))
            dve.wait_ge(om_mm, H)
            for t in range(T):
                rs = trig[:, 2, t, 0:H].rearrange("p (h o) -> p h o", o=1).broadcast_to([P, H, DH])
                dve.tensor_tensor(y_row[:, t, 0:NB].rearrange("p (h d) -> p h d", d=DH),
                                  ps[:, t, :].rearrange("p (h d) -> p h d", d=DH), rs, ALU.mult).then_inc(om_out, 1)
            dve.wait_ge(omT_mm, 1)
            for k in range(4):
                dve.tensor_copy(nT[:, k, :], ps[:, 4 + k // 2, (k % 2) * S:(k % 2 + 1) * S]).then_inc(omT_out, 1)
            dve.wait_ge(omT_hi, 1)
            dve.tensor_tensor(nT_lo[:, 0:4, :], nT[:, 0:4, :], nT_hi[:, 0:4, :].bitcast(F32), ALU.subtract).then_inc(omT_lo, 1)
            split_lo(SLOT_A, m2 + 10)
            split_lo(SLOT_B, m2 + 10)
            dve.wait_ge(w_used[SLOT_B], m2 + 10)
            for t in range(T):
                src = ps[:, 2 * t:2 * t + 2, :].rearrange("p b n -> p (b n)")
                link(dve.tensor_tensor(sig[:, t, D:2 * D], src, sig[:, t, D:2 * D], ALU.mult))
                dve.tensor_tensor(y_row[:, t, :], sig[:, t, 0:D], sig[:, t, D:2 * D], ALU.add).then_inc(yb_out, 1)
            norm_out(TR["O2"], lambda k, src: dve.tensor_copy(nT[:, k, :], src))
            split_lo(SLOT_A, m2 + 11)
            split_lo(SLOT_B, m2 + 11)
            split_lo(SLOT_A, AB0["F3"])
            split_lo(SLOT_B, AB0["F3"])
            residual("M2", 1, False)
            ffn("F3", nxt=0)
            residual("F3", 0, False)
            dve.wait_ge(post_loaded[0], 48)
            for t in range(T):
                rms_ready(dve, f"end {t}")
                dve.scalar_tensor_tensor(y_row[:, t, :], x_res[:, t, :], stat[:, 8 + t:9 + t], post_gain[:, 0, :],
                                         ALU.mult, ALU.mult).then_inc(y_ready, 1)


        @block.tensor
        def _(pe):
            def mm3(o, xh, xl, wh, wl, start, stop):
                pe.matmul(o, xh, wh, start=start, stop=False, skip_group_check=True)
                pe.matmul(o, xh, wl, start=False, stop=False, skip_group_check=True)
                return pe.matmul(o, xl, wh, start=False, stop=stop, skip_group_check=True)

            def weights(s, use):
                pe.wait_ge(lo_ready[s], use + 1)

            def norm_transposes(ready):
                for j in range(KD // 2):
                    for k in (2 * j, 2 * j + 1):
                        for t in range(T):
                            if j == 0 and k == 0:
                                ready(t)
                            last = pe.transpose(ps[:, 4 + j, (k % 2) * S + t * P:(k % 2) * S + (t + 1) * P],
                                                y_row[:, t, k * P:(k + 1) * P], ident[:])
                    last.then_inc(n_tr, 1)

            def norm(f):
                r = NORM[f]
                norm_transposes(lambda t: pe.wait_ge(y_ready, 2 * r + 1 + t))

            def row_group(s, out_banks, n, first_norm=None, k_at=None, nk=4, start=None, stop=None, tiles=range(T)):
                for k in range(nk):
                    kk = k_at + k
                    if first_norm is not None and kk % 2 == 0:
                        pe.wait_ge(n_lo, 4 * first_norm + kk // 2 + 1)
                    for t in tiles:
                        last = mm3(out_banks[t], nT_hi[:, kk, t * P:(t + 1) * P], nT_lo[:, kk, t * P:(t + 1) * P],
                                   w_hi[:, s, k * n:(k + 1) * n], w_lo[:, s, k * n:(k + 1) * n],
                                   start=(k == 0 and bool(start)), stop=(k == nk - 1 and bool(stop)))
                return last

            def col_group(s, bank, first_norm=None, first_slot=SLOT_A):
                for k in range(4):
                    kk = 4 * s + k
                    if first_norm is not None and kk % 2 == 0:
                        pe.wait_ge(n_lo, 4 * first_norm + kk // 2 + 1)
                    for i in range(4):
                        o = ps[:, bank + i // 2, (i % 2) * S:(i % 2 + 1) * S]
                        cols = slice(k * NB + i * P, k * NB + (i + 1) * P)
                        pe.matmul(o, w_hi[:, s, cols], nT_hi[:, kk, :], start=(s == first_slot and k == 0 and i % 2 == 0),
                                  stop=False, skip_group_check=True)
                        pe.matmul(o, w_hi[:, s, cols], nT_lo[:, kk, :], start=False, stop=False, skip_group_check=True)
                        last = pe.matmul(o, w_lo[:, s, cols], nT_hi[:, kk, :], start=False,
                                         stop=(s != first_slot and k == 3), skip_group_check=True)
                return last

            def body(f, c, down=True, gu=True, first_norm=None, first=False, hooks=((), (), ())):
                i = FFN.index(f) * NC
                if gu:
                    wait(pe, h_ready, c + i)
                    weights(SLOT_A, c + AB0[f])
                    col_group(SLOT_A, 0, first_norm).then_inc(w_used[SLOT_A], 1)
                for hook in hooks[0]:
                    hook()
                if gu:
                    weights(SLOT_B, c + AB0[f])
                    col_group(SLOT_B, 0, first_norm).then_inc(w_used[SLOT_B], 1)
                for hook in hooks[1]:
                    hook()
                if down:
                    weights(SLOT_D, c - 1 + D0[f])
                    pe.wait_ge(ht_lo, c + i)
                    last_chunk = not gu
                    for t in range(T):
                        for j in range(2):
                            for n in range(2):
                                last = mm3(ps[:, 4 + 2 * t + n, :], hT_hi[:, j, t * P:(t + 1) * P], hT_lo[:, j, t * P:(t + 1) * P],
                                           w_hi[:, SLOT_D, j * D + n * NB:j * D + (n + 1) * NB],
                                           w_lo[:, SLOT_D, j * D + n * NB:j * D + (n + 1) * NB],
                                           start=(first and j == 0), stop=(last_chunk and j == 1))
                        if last_chunk and t == 0:
                            last.then_inc(down_done, 1)
                    last.then_inc(w_used[SLOT_D], 1)
                for hook in hooks[2]:
                    hook()

            def sum_columns(f_sums, n, acc):
                if n:
                    for half in range(2):
                        pe.wait_ge(ada_done[half], n_ada[FFN[n - 1]] + KD)
                wait(pe, gate_out, 2 * n_gates[FFN[n - 1]] if n else 0)
                wait(pe, cols_out, n)
                for i, (off, *_) in enumerate(f_sums):
                    for k in range(KD):
                        last = pe.matmul(ps[:, 3, KD * i + k:KD * i + k + 1], acc[:, off + k * P:off + (k + 1) * P],
                                         ones[:, 0:1], start=True, stop=True, skip_group_check=True)
                last.then_inc(acc_cols, 1)

            acc_flat = mod_acc.rearrange("p a b -> p (a b)")

            def sum_gate(f, i, half):
                off = gates[f][i][0] + half * NB
                n = 2 * (n_gates[f] + i) + half
                pe.wait_ge(ada_done[0], n_ada[f] + KD)
                if i:
                    for h in range(2):
                        pe.wait_ge(ada_done[h], n_ada[f] + KD + 2)
                wait(pe, gate_out, n - 1)
                if i == 0 and half == 1:
                    wait(pe, cols_out, n_cols[f] + 1 if col_sums[f] else 0)
                pe.matmul(ps[:, 2 + half, :], ones[:], acc_flat[:, off:off + NB], start=True, stop=True).then_inc(acc_gate, 1)

            def ffn(f):
                r = NORM[f]
                norm(f)
                body(f, 0, down=False, first_norm=TR[f])
                body(f, 1, first=True)
                with pe.Fori(2, NC - 2) as c:
                    body(f, c)
                body(f, NC - 2, hooks=([lambda: sum_columns(col_sums[f], n_cols[f], acc_flat)] if col_sums[f] else (),
                                       [lambda: sum_gate(f, 0, 0)], ()))
                body(f, NC - 1, hooks=([lambda: sum_gate(f, 0, 1)], (), ()))
                body(f, NC, gu=False)
                for i in range(1, len(gates[f])):
                    sum_gate(f, i, 0)
                    sum_gate(f, i, 1)

            pe.wait_ge(const_ready, 2)
            pe.wait_ge(small_loaded, SMALL)
            for b in range(2):
                last = pe.transpose(ps[:, 7, b * P:b * P + VECS[b]], vec_rows[0:VECS[b], b, :], ident[0:VECS[b], 0:VECS[b]])
            last.then_inc(vec_tr, 1)
            pe.wait_ge(rel_ready, 1)
            for h in range(H):
                if h >= 4:
                    pe.wait_ge(toe_sb, h - 3)
                pe.matmul(ps[:, h % 4, 0:CAUSAL], rel_bc[0:BUCKETS, h, :], onehot[0:BUCKETS, :], start=True, stop=True)\
                    .then_inc(toe_mm, 1)
            pe.wait_ge(toe_sb, H)
            pe.wait_ge(ada_done[0], 4)
            pe.wait_ge(ada_done[1], 4)
            sum_columns([(0,), (D,)], 0, first_acc)
            pe.wait_ge(vec_ready, 2)
            ffn("F0")

            m1 = AB0["M1"]
            norm("M1")

            def group_free(g):
                wait(pe, grp_out, 2 * (g - 1))

            def group_half(g, s, first_norm=None):
                weights(s, use1(s, g))
                col_group(s, 2 * (g % 2), first_norm, SLOT_B if g == KI else SLOT_A).then_inc(w_used[s], 1)

            def value_half(g, s):
                weights(s, use1(s, g))
                row_group(s, [ps[:, 2 * (g % 2) + t, :] for t in range(T)], NB, None, 4 * s,
                          start=(s == SLOT_A), stop=(s == SLOT_B)).then_inc(w_used[s], 1)

            def r_group(g, base, use, n, first_norm=None):
                group_free(g + base)
                banks = [ps[:, 2 * (g % 2) + t, 0:n] for t in range(T)]
                weights(SLOT_A, use)
                row_group(SLOT_A, banks, n, first_norm, 0, start=True).then_inc(w_used[SLOT_A], 1)
                weights(SLOT_B, use)
                row_group(SLOT_B, banks, n, first_norm, 4, stop=True).then_inc(w_used[SLOT_B], 1)

            def head(i, h):
                return qkT[DH * (h % 2):DH * (h % 2) + DH, i, h // 2, :]

            group_half(0, SLOT_A, TR["M1"])
            group_half(0, SLOT_B, TR["M1"])
            pe.wait_ge(gate_out, 2 * n_gates["F1"])
            group_half(1, SLOT_A)
            group_half(1, SLOT_B)
            group_free(2)
            group_half(2, SLOT_A)
            pe.wait_ge(grp_out, 4)
            for h in range(H):
                if h >= 4:
                    pe.wait_ge(z_out, h - 3)
                q, k = head(TQB, h), head(TKB, h)
                pe.matmul(ps[:, 4 + h % 4, 0:S], k[:, 0:P], q, start=True, stop=True, skip_group_check=True)
                pe.matmul(ps[:, 4 + h % 4, S:CAUSAL], k[:, P:S], q[:, P:S], start=True, stop=True,
                          skip_group_check=True).then_inc(z_mm, 1)
            group_half(2, SLOT_B)
            weights(SLOT_A, m1 + KI)
            pe.wait_ge(z_out, H)
            for k in range(KD):
                for t in range(T):
                    last = mm3(ps[:, 4 + t, 0:72], nT_hi[:, k, t * P:(t + 1) * P], nT_lo[:, k, t * P:(t + 1) * P],
                               w_hi[:, SLOT_A, k * 72:(k + 1) * 72], w_lo[:, SLOT_A, k * 72:(k + 1) * 72],
                               start=(k == 0), stop=(k == KD - 1))
            last.then_inc(w_used[SLOT_A], 1)
            group_free(3)
            group_half(3, SLOT_B)
            pe.wait_ge(ki_ready, 1)
            for t in range(T):
                last = pe.transpose(ps[:, 6, t * P:(t + 1) * P], ki2[:, t, :], ident[:])
            last.then_inc(ki_tr, 1)
            group_half(3, SLOT_A)
            pe.wait_ge(kiT_ready, 1)
            pe.wait_ge(grp_out, 6)
            for h in range(H):
                if h >= 4:
                    pe.wait_ge(idx_relu, h - 3)
                q = head(TQI, h)
                k = kiT[DH * (h % 2):DH * (h % 2) + DH, :]
                pe.matmul(ps[:, 4 + h % 4, 0:S], q[:, P:S], k, start=True, stop=True, skip_group_check=True)
                pe.matmul(ps[:, 4 + h % 4, S:CAUSAL], q[:, 0:P], k[:, 0:P], start=True, stop=True,
                          skip_group_check=True).then_inc(idx_mm, 1)
            value_half(4, SLOT_A)
            pe.wait_ge(u_masked, 2)
            for h in range(H):
                if h >= 4:
                    pe.wait_ge(r_out, h - 3)
                else:
                    pe.wait_ge(idx_relu, h + 5)
                b = ps[:, 4 + h % 4, :]
                pe.matmul(b[:, 0:CAUSAL], tri[:], u_sb[:, h, :], start=True, stop=False, skip_group_check=True)
                pe.matmul(b[:, P:S], ones[:], u_sb[:, h, S:CAUSAL], start=False, stop=True,
                          skip_group_check=True).then_inc(r_mm, 1)
            value_half(4, SLOT_B)
            group_free(5)
            group_half(5, SLOT_A)
            pe.wait_ge(a_masked, 2)
            pe.wait_ge(r_out, H)
            pe.wait_ge(grp_out, 10)
            for h in range(H):
                v = [v_row[:, 1, s, h * DH:(h + 1) * DH] for s in range(2)]
                o = [ps[:, 4 + t, h * DH:(h + 1) * DH] for t in range(T)]
                pe.matmul(o[0], z_sb[:, h, 0:P], v[0], start=True, stop=True, skip_group_check=True)
                pe.matmul(o[1], z_sb[:, h, P:S], v[0], start=True, stop=False, skip_group_check=True)
                last = pe.matmul(o[1], z_sb[:, h, S:CAUSAL], v[1], start=False, stop=True, skip_group_check=True)
            last.then_inc(ob_mm, 1)
            group_half(5, SLOT_B)
            value_half(6, SLOT_A)

            def out_transposes(half, bank):
                for j in range(2):
                    for i in range(2):
                        for t in range(T):
                            last = pe.transpose(ps[:, bank + j, i * S + t * P:i * S + (t + 1) * P],
                                                y_row[:, t, half * NB + (2 * j + i) * P:half * NB + (2 * j + i + 1) * P], ident[:])
                    last.then_inc(n_tr, 1)

            pe.wait_ge(ob_ready, 1)
            pe.wait_ge(grp_out, 12)
            out_transposes(1, 2)
            pe.wait_ge(ob_out, T)
            for h in range(H):
                if h >= 4:
                    pe.wait_ge(l_out, h - 3)
                q, k = head(TQA, h), head(TKA, h)
                pe.matmul(ps[:, 4 + h % 4, 0:S], q[:, P:S], k, start=True, stop=True, skip_group_check=True)
                pe.matmul(ps[:, 4 + h % 4, S:CAUSAL], q[:, 0:P], k[:, 0:P], start=True, stop=True,
                          skip_group_check=True).then_inc(l_mm, 1)
            value_half(6, SLOT_B)
            pe.wait_ge(l_out, H)

            def probs_times_v(h):
                pe.wait_ge(pT_out, h + 1)
                v = [v_row[:, 0, s, h * DH:(h + 1) * DH] for s in range(2)]
                o = [ps[:, t, h * DH:(h + 1) * DH] for t in range(T)]
                pe.matmul(o[1], e_sb[:, h, 0:P], v[0], start=True, stop=False, skip_group_check=True)
                pe.matmul(o[1], e_sb[:, h, P:S], v[1], start=False, stop=True, skip_group_check=True)
                return pe.matmul(o[0], e_sb[:, h, S:CAUSAL], v[0], start=True, stop=True, skip_group_check=True)

            for h in range(H):
                if h >= 2:
                    pe.wait_ge(pT_out, h - 1)
                pe.wait_ge(p_exp, 2 * h + 2)
                for i in range(3):
                    last = pe.transpose(ps[:, 6 + h % 2, i * P:(i + 1) * P], z_sb[:, h, i * P:(i + 1) * P], ident[:])
                last.then_inc(p_tr, 1)
                if h == 0:
                    pe.wait_ge(grp_out, 14)
                else:
                    probs_times_v(h - 1)
            probs_times_v(H - 1).then_inc(oa_mm, 1)
            banks = [[ps[:, output_at("M1", t) + n, :] for t in range(T)] for n in range(2)]
            pe.wait_ge(n_lo, 4 * TR["O1"] + 2)
            for n, (s, use) in enumerate(((SLOT_B, m1 + 7), (SLOT_D, D0["M1"]))):
                weights(s, use)
                row_group(s, banks[n], NB, None, 4, start=True).then_inc(w_used[s], 1)
            pe.wait_ge(o_ready, 1)
            pe.wait_ge(pT_out, H)
            out_transposes(0, 6)
            pe.wait_ge(n_lo, 4 * TR["O1"] + 4)
            for t in range(T):
                for n, (s, use) in enumerate(((SLOT_A, m1 + 8), (SLOT_B, m1 + 8))):
                    weights(s, use)
                    last = row_group(s, banks[n], NB, None, 0, stop=True, tiles=(t,))
                    if t == 1:
                        last.then_inc(w_used[s], 1)
                if t == 0:
                    last.then_inc(mix_half, 1)

            def out_linear(r, use):
                pe.wait_ge(n_lo, 4 * r + 4)
                for n in range(2):
                    banks = [ps[:, 4 + 2 * t + n, :] for t in range(T)]
                    for s in (SLOT_A, SLOT_B):
                        weights(s, use + n)
                        last = row_group(s, banks, NB, None, 4 * s, start=(s == SLOT_A), stop=(s == SLOT_B))
                        last.then_inc(w_used[s], 1)

            ffn("F1")
            ffn("F2")

            m2 = AB0["M2"]
            norm("M2")
            r_group(0, 7, m2, NB, first_norm=TR["M2"])
            pe.wait_ge(gate_out, 2 * n_gates["F3"])
            r_group(1, 7, m2 + 1, QL)
            r_group(2, 7, m2 + 2, KVL + ROPE)
            pe.wait_ge(dft_loaded, 32)
            pe.wait_ge(grp_out, 14 + 2)
            for g in range(4):
                for k in range(2):
                    last = pe.matmul(ps[:, 4 + g, :], uf[:, k, g * P:(g + 1) * P], dft[:, k, :], start=(k == 0), stop=(k == 1))
                last.then_inc(cu_mm, 1)
            r_group(3, 7, m2 + 3, NB)
            r_group(4, 7, m2 + 4, NB)
            pe.wait_ge(cu_out, 4)
            for g in range(4):
                o = ps[:, 4 + g // 2, (g % 2) * S:(g % 2 + 1) * S]
                pe.matmul(o, dftd[:, 0, :], cu[:, g, 0:S], start=True, stop=False, skip_group_check=True)
                last = pe.matmul(o, dftd[:, 1, :], cu[:, g, S:2 * S], start=False, stop=True, skip_group_check=True)
            last.then_inc(f_mm, 1)
            r_group(5, 7, m2 + 5, NB)
            pe.wait_ge(lat_ready, 4)
            pe.wait_ge(f_out, 4)
            for k in range(5):
                for t in range(T):
                    last = pe.transpose(ps[:, (6, 6, 7, 7, 4)[k], (k % 2) * S + t * P:(k % 2) * S + (t + 1) * P],
                                        lat[:, t, k * P:(k + 1) * P], ident[:])
            last.then_inc(lat_tr, 1)
            r_group(6, 7, m2 + 6, NB)
            pe.wait_ge(f_lo, 1)
            pe.wait_ge(lat_out, 5)
            for s in (SLOT_A, SLOT_B):
                weights(s, m2 + 7)
                banks = [ps[:, 4 + 2 * t + s, :] for t in range(T)]
                row_group(s, banks, NB, None, 4, start=True, stop=True).then_inc(w_used[s], 1)
            pe.wait_ge(lat_lo, 2)
            pe.wait_ge(grp_out, 28)
            weights(SLOT_D, D0["M2"])
            for t in range(T):
                for n in range(2):
                    for k in range(2):
                        last = mm3(ps[:, 2 * t + n, :], hT_hi[:, k, t * P:(t + 1) * P], hT_lo[:, k, t * P:(t + 1) * P],
                                   w_hi[:, SLOT_D, k * D + n * NB:k * D + (n + 1) * NB],
                                   w_lo[:, SLOT_D, k * D + n * NB:k * D + (n + 1) * NB], start=(k == 0), stop=(k == 1))
            last.then_inc(w_used[SLOT_D], 1)
            pe.wait_ge(ya_out, T)
            for s in (SLOT_A, SLOT_B):
                weights(s, m2 + 8)
                banks = [ps[:, 4 + 2 * t + s, 0:QL] for t in range(T)]
                row_group(s, banks, QL, None, 0, nk=3, start=True, stop=True).then_inc(w_used[s], 1)
            for i in range(8):
                src = k_row if i < 4 else q_row
                if i % 4 == 0:
                    pe.wait_ge(qk_ready, i // 4 + 1)
                    pe.wait_ge(up_out, 4)
                if i >= 4:
                    pe.wait_ge(qkT_out, i - 3)
                for j in range(2):
                    h = 2 * (i % 4) + j
                    for t in range(T):
                        last = pe.transpose(ps[0:QH, i % 4, j * S + t * P:j * S + (t + 1) * P], src[:, t, h * QH:(h + 1) * QH], ident[:])
                last.then_inc(qk_tr, 1)
            pe.wait_ge(qkT_out, 8)

            def scores(h):
                if h >= 4:
                    pe.wait_ge(s_exp, 2 * (h - 3))
                for t in range(T):
                    last = pe.matmul(ps[:, (4, 5, 2, 3)[h % 4], t * S:(t + 1) * S], qT[0:QH, h, t * P:(t + 1) * P], kT[0:QH, h, :],
                                     start=True, stop=True, skip_group_check=True)
                last.then_inc(s_mm, 1)

            for h in range(3):
                scores(h)
            for h in range(H):
                pe.wait_ge(s_exp, 2 * h + 2)
                if h >= 2:
                    pe.wait_ge(sT_out, h - 1)
                for s in range(2):
                    for t in range(T):
                        last = pe.transpose(ps[:, 6 + h % 2, s * S + t * P:s * S + (t + 1) * P],
                                            prob4[:, h % 4, t * S + s * P:t * S + (s + 1) * P], ident[:])
                last.then_inc(s_tr, 1)
                if h + 3 < H:
                    scores(h + 3)
                pe.wait_ge(sT_out, h + 1)
                for t in range(T):
                    for s in range(2):
                        last = pe.matmul(ps[:, t, h * DH:(h + 1) * DH], probT[:, h % 2, s * S + t * P:s * S + (t + 1) * P],
                                         kv_row[:, s, h * P + QK:(h + 1) * P], start=(s == 0), stop=(s == 1),
                                         skip_group_check=True)
                last.then_inc(om_mm, 1)
            pe.wait_ge(om_out, T)
            for k in range(4):
                for t in range(T):
                    last = pe.transpose(ps[:, 4 + k // 2, (k % 2) * S + t * P:(k % 2) * S + (t + 1) * P],
                                        y_row[:, t, k * P:(k + 1) * P], ident[:])
            last.then_inc(omT_mm, 1)
            pe.wait_ge(omT_lo, 1)
            for s in (SLOT_A, SLOT_B):
                weights(s, m2 + 9)
                banks = [ps[:, 2 * t + s, :] for t in range(T)]
                row_group(s, banks, NB, None, 0, start=True, stop=True).then_inc(w_used[s], 1)
            norm_transposes(lambda t: pe.wait_ge(yb_out, t + 1))
            out_linear(TR["O2"], m2 + 10)
            ffn("F3")


def onehot_buckets():
    import math
    import numpy as np
    n = np.maximum(255 - np.arange(CAUSAL), 0)
    exact = BUCKETS // 2
    large = exact + (np.log(np.maximum(n, 1).astype(np.float32) / exact) / math.log(128 / exact)
                     * (BUCKETS - exact)).astype(np.int32)
    bucket = np.where(n < exact, n, np.minimum(large, BUCKETS - 1))
    return (bucket[None, :] == np.arange(BUCKETS)[:, None]).astype(np.float32)


def dft_tables():
    import numpy as np
    s, d = np.arange(S), np.arange(P)
    ws = 2 * np.pi * ((s[:, None] * s[None, :]) % S) / S
    wd = 2 * np.pi * ((d[:, None] * d[None, :]) % P) / P
    over_s = np.concatenate([np.cos(ws), np.sin(ws)], 1) / np.sqrt(S)
    over_d = np.concatenate([np.cos(wd), -np.sin(wd)], 1) / np.sqrt(P)
    return over_s.astype(np.float32), over_d.astype(np.float32)


def inverse_frequencies():
    import numpy as np
    e = np.arange(16, dtype=np.float32) * np.float32(2.0) / np.float32(32)
    return (np.float32(1.0) / (np.float32(10000.0) ** e)).astype(np.float32)[None, :]


_OUTS = [((1, 256, 1024), "float32")]


def kernel(**inputs):
    import numpy as np
    import concourse.bacc as bacc
    from concourse.bass_utils import run_bass_kernel_spmd

    nc = bacc.Bacc("TRN2", target_bir_lowering=False, num_devices=1)
    arrays, aps = {}, {}
    over_s, over_d = dft_tables()
    shape_constants = {"onehot": onehot_buckets(), "dft_s": over_s, "dft_d": over_d, "inv_freq": inverse_frequencies()}
    for name, v in {**inputs, **shape_constants}.items():
        v = np.ascontiguousarray(v)
        arrays[f"in_{name}"] = v
        aps[name] = nc.dram_tensor(f"in_{name}", v.shape, mybir.dt.from_np(v.dtype), kind="ExternalInput").ap()
    out = nc.dram_tensor("out", _OUTS[0][0], F32, kind="ExternalOutput").ap()
    program(nc, aps, out)
    r = run_bass_kernel_spmd(nc, [arrays], core_ids=[0])
    return r.results[0]["out"]
```

```python
from contextlib import ExitStack

import concourse.bass as bass
from concourse import mybir

F32 = mybir.dt.float32
F32R = mybir.dt.float32r
I32 = mybir.dt.int32
ALU = mybir.AluOpType
ACT = mybir.ActivationFunctionType
AX = mybir.AxisListType

P = 128
D = 1024
S = 256
T = S // P
KD = D // P
F = 2816
FC = 256
NC = F // FC
NB = 512
PIECE = 2048
H = 8
DH = 64
CAUSAL = 384
TOPK = 64
BUCKETS = 32
EPS = 1e-6
DONE = -3.0e38
FUTURE = -2.0e38
OFF = -1.0e30
ROUND = 12582912.0
TWO_PI = (6.28125, 0.0019350051879882812, 3.0199159819e-07)
PI = 3.1415925
SLOT_A, SLOT_B, SLOT_D = 0, 1, 2
ADA = 3072
ARENA = 18944
QK, ROPE, QH = 64, 32, 96
QL, KVL = 384, 256


def program(nc, a, out):
    ctx = ExitStack()
    with ctx:
        def sb(name, shape, dt=F32):
            return ctx.enter_context(nc.sbuf_tensor(name, shape, dt))

        def sem(name):
            return ctx.enter_context(nc.semaphore(name))

        x_res = sb("x_res", [P, T, D])
        y_row = sb("y_row", [P, T, D])
        nT = sb("nT", [P, KD, S])
        nT_hi = sb("nT_hi", [P, KD, S], F32R)
        nT_lo = sb("nT_lo", [P, KD, S], F32R)
        w_raw = sb("w_raw", [P, 3, PIECE])
        w_hi = sb("w_hi", [P, 3, PIECE], F32R)
        w_lo = sb("w_lo", [P, 3, PIECE], F32R)
        sil = sb("sil", [P, 2, S])
        h_act = sb("h_act", [P, 2, S])
        hT_hi = sb("hT_hi", [P, 2, S], F32R)
        hT_lo = sb("hT_lo", [P, 2, S], F32R)
        gate = sb("gate", [P, 2, D])
        arena = sb("arena", [P, ARENA])
        ident = sb("ident", [P, P])
        ones = sb("ones", [P, P])
        tri = sb("tri", [P, P])
        vec_rows = sb("vec_rows", [P, 2, P])
        vec_col = sb("vec_col", [P, 2, P])
        mod_col = sb("mod_col", [P, 6, 2, KD])
        c_in = sb("c_in", [P, 2, KD])
        c_act = sb("c_act", [P, 2, KD])
        stat = sb("stat", [P, 64])
        minus_half = sb("minus_half", [P, 4])
        angle = sb("angle", [P, T, 16])
        trig = sb("trig", [P, 6, T, 16])
        pos_i = sb("pos_i", [P, T], I32)
        pos_f = sb("pos_f", [P, T])
        freq = sb("freq", [P, 16])
        gki = sb("gki", [P, DH])
        ps = ctx.enter_context(nc.psum_tensor("ps", [P, 8, NB], F32))
        toe_dram = nc.dram_tensor("toe_scratch", [P * 3 * P * H], F32, kind="Internal").ap()

        def carve(at, *shape):
            n = 1
            for s in shape:
                n *= s
            assert at + n <= ARENA, (at, shape)
            v = arena[:, at:at + n]
            if len(shape) == 2:
                v = v.rearrange("p (a b) -> p a b", b=shape[1])
            if len(shape) == 3:
                v = v.rearrange("p (a b c) -> p a b c", b=shape[1], c=shape[2])
            return v

        mod_acc = carve(0, 2, ADA)
        ada_raw = carve(2 * ADA, 2, ADA)
        post_gain = carve(4 * ADA, 2, D)
        first_acc = carve(4 * ADA + 2 * D, 2 * D)
        first_raw = carve(2 * ADA, 3, 2 * D)
        qkT = carve(0, 5, 4, S)
        TQI, TQB, TKB, TKA, TQA = range(5)
        v_row = carve(5120, 2, T, NB)
        z_sb = carve(7168, H, CAUSAL)
        u_sb = carve(10240, H, CAUSAL)
        e_sb = carve(13312, H, CAUSAL)
        score = carve(16384, CAUSAL)
        work = carve(16768, CAUSAL)
        relu = carve(17152, 4, CAUSAL)
        kw_row = h_act[:, :, 0:72]
        ki2 = sil[:, :, 0:P]
        kiT = h_act[:, 0, :]
        wi = stat[:, 32:48]
        ob_T = qkT[:, TQI]
        toe_bc = carve(0, H, CAUSAL)
        rel_bc = carve(3072, H, P)
        rel_in = carve(4096, H)
        onehot = carve(4104, CAUSAL)
        bias = nT
        sig = carve(0, T, 2 * D)
        uf = carve(4096, T, NB)
        dft = carve(5120, 2, NB)
        dftd = carve(6144, 2, P)
        cu = carve(6400, 4, NB)
        lat = carve(8448, T, QL + KVL + ROPE)
        q_row = carve(9792, T, H * QH)
        k_row = carve(11328, T, H * QH)
        kv_row = carve(12864, T, H * P)
        qT = carve(14912, H, S)
        kT = carve(4096, H, S)
        prob = carve(6144, 2, NB * 2)
        probT = carve(16960, 2, NB)

        x_hi = w_hi[:, SLOT_D, :].rearrange("p (k n) -> p k n", n=S)
        x_lo = w_lo[:, SLOT_D, :].rearrange("p (k n) -> p k n", n=S)

        raw_loaded = [sem(f"raw_loaded{s}") for s in range(3)]
        hi_ready = [sem(f"hi_ready{s}") for s in range(3)]
        lo_ready = [sem(f"lo_ready{s}") for s in range(3)]
        w_used = [sem(f"w_used{s}") for s in range(3)]
        small_loaded = sem("small_loaded")
        rel_loaded = sem("rel_loaded")
        x_loaded = sem("x_loaded")
        const_ready = sem("const_ready")
        pool_step = sem("pool_step")
        c_loaded = sem("c_loaded")
        c_ready = sem("c_ready")
        vec_tr = sem("vec_tr")
        vec_ready = sem("vec_ready")
        toe_mm = sem("toe_mm")
        toe_sb = sem("toe_sb")
        toe_stored = sem("toe_stored")
        bias_loaded = sem("bias_loaded")
        rel_ready = sem("rel_ready")
        first_loaded = [sem(f"first_loaded{s}") for s in range(3)]
        ada_loaded = [sem(f"ada_loaded{s}") for s in range(2)]
        ada_done = [sem(f"ada_done{s}") for s in range(2)]
        acc_zero = sem("acc_zero")
        acc_cols = sem("acc_cols")
        cols_out = sem("cols_out")
        acc_gate = sem("acc_gate")
        gate_out = sem("gate_out")
        gate_loaded = [sem(f"gate_loaded{s}") for s in range(2)]
        post_loaded = [sem(f"post_loaded{s}") for s in range(2)]
        sq_done = sem("sq_done")
        ki_sq = sem("ki_sq")
        rms_done = sem("rms_done")
        y_ready = sem("y_ready")
        n_tr = sem("n_tr")
        n_ready = sem("n_ready")
        n_hi = sem("n_hi")
        n_lo = sem("n_lo")
        h_done = sem("h_done")
        silu_done = sem("silu_done")
        h_ready = sem("h_ready")
        ht_hi = sem("ht_hi")
        ht_lo = sem("ht_lo")
        mix_half = sem("mix_half")
        down_done = sem("down_done")
        fsq_done = sem("fsq_done")
        dve_step = sem("dve_step")
        grp_out = sem("grp_out")
        out_stored = sem("out_stored")
        sp_settled = sem("sp_settled")

        ki_ready, ki_tr, kiT_ready = map(sem, ["ki_ready", "ki_tr", "kiT_ready"])
        idx_mm, idx_relu, idx_acc = map(sem, ["idx_mm", "idx_relu", "idx_acc"])
        score_causal, sel_ready, mask_ready = map(sem, ["score_causal", "sel_ready", "mask_ready"])
        z_mm, z_out, z_ln, u_ready, u_masked = map(sem, ["z_mm", "z_out", "z_ln", "u_ready", "u_masked"])
        r_mm, r_out, loga_ready, a_exp, a_masked, ob_mm, ob_out = map(
            sem, ["r_mm", "r_out", "loga_ready", "a_exp", "a_masked", "ob_mm", "ob_out"])
        l_mm, l_out, lmax_ready, p_exp, p_tr, pT_out, oa_mm, oa_out = map(
            sem, ["l_mm", "l_out", "lmax_ready", "p_exp", "p_tr", "pT_out", "oa_mm", "oa_out"])
        osq_done = sem("osq_done")
        q_scaled = sem("q_scaled")
        dft_loaded, cu_mm, cu_out, f_mm, f_out, f_hi, f_lo = map(
            sem, ["dft_loaded", "cu_mm", "cu_out", "f_mm", "f_out", "f_hi", "f_lo"])
        trig_arg, trig_done, trig_ready = map(sem, ["trig_arg", "trig_done", "trig_ready"])
        lat_sq, lat_ready, lat_tr, lat_out, lat_hi, lat_lo = map(
            sem, ["lat_sq", "lat_ready", "lat_tr", "lat_out", "lat_hi", "lat_lo"])
        up_out, qk_ready, qk_tr, qkT_out = map(sem, ["up_out", "qk_ready", "qk_tr", "qkT_out"])
        ya_out, yb_out = map(sem, ["ya_out", "yb_out"])
        s_mm, smax_ready, s_exp, s_tr, sT_out, om_mm, om_out = map(
            sem, ["s_mm", "smax_ready", "s_exp", "s_tr", "sT_out", "om_mm", "om_out"])
        omT_mm, omT_out, omT_hi, omT_lo = map(sem, ["omT_mm", "omT_out", "omT_hi", "omT_lo"])

        top_found, top_taken, o_ready, ob_ready = map(sem, ["top_found", "top_taken", "o_ready", "ob_ready"])
        SMALL = 16 * 13
        VECS = (104, 101)

        A0 = {"F0": 0, "M1": NC, "F1": NC + 8, "F2": 2 * NC + 8, "M2": 3 * NC + 8, "F3": 4 * NC + 8}
        B0 = {"F0": 0, "M1": NC, "F1": NC + 9, "F2": 2 * NC + 9, "M2": 3 * NC + 9, "F3": 3 * NC + 21}
        D0 = {"F0": 0, "M1": NC, "F1": NC + 2, "F2": 2 * NC + 2, "M2": 3 * NC + 2, "F3": 3 * NC + 4}
        FFN = ["F0", "F1", "F2", "F3"]
        ffn_w = {
            "F0": (a["w_ffn_gate"][0, 0], a["w_ffn_up"][0, 0], a["w_ffn_down"][0, 0]),
            "F1": (a["w_ffn_gate"][0, 1], a["w_ffn_up"][0, 1], a["w_ffn_down"][0, 1]),
            "F2": (a["ffn1_w_gate_2"][0], a["ffn1_w_up_2"][0], a["ffn1_w_down_2"][0]),
            "F3": (a["ffn2_w_gate_2"][0], a["ffn2_w_up_2"][0], a["ffn2_w_down_2"][0]),
        }
        NORM = {"F0": 0, "M1": 1, "F1": 2, "F2": 3, "M2": 4, "F3": 5, "end": 6}
        w1, w2 = a["w_ada"][0], a["ada_w_2"][0]
        ada_steps = {
            "F0": [(w1, 2 * D, 3 * D, 0, 0), (w1, 6 * D, 2 * D, 0, D)],
            "F1": [(w1, 8 * D, D, 0, 0), (w2, 0, 2 * D, 1, 0)],
            "F2": [(w2, 2 * D, 3 * D, 1, 0), (w2, 6 * D, 2 * D, 1, D)],
            "F3": [(w2, 8 * D, D, 1, 0)],
        }
        ada_rest = {"F0": (w1, 5 * D, 0), "F2": (w2, 5 * D, 1)}
        col_sums = {
            "start": [(0, 0, 0, 0), (D, 0, 1, 0)],
            "F0 early": [(4 * D, 0, 6, 2), (5 * D, 0, 7, 2)],
            "F0 late": [(D, 0, 3, 1), (2 * D, 0, 4, 1)],
            "F1 late": [(ADA, 1, 0, 3), (ADA + D, 1, 1, 3)],
            "F2 early": [(4 * D, 1, 6, 5), (5 * D, 1, 7, 5)],
            "F2 late": [(D, 1, 3, 4), (2 * D, 1, 4, 4)],
        }
        COLS = list(col_sums)
        cols_bank = lambda batch: 0 if batch.endswith("late") else 3
        b1, b2 = a["b_ada"][0], a["ada_b_2"][0]
        gates = {
            "F0": [(0, b1[2 * D:3 * D], 0, a["g_post"][0, 0], 0.5), (3 * D, b1[5 * D:6 * D], 1, a["g_post"][0, 1], 1.0)],
            "F1": [(0, b1[8 * D:9 * D], 0, a["g_post"][0, 2], 0.5)],
            "F2": [(0, b2[2 * D:3 * D], 0, None, 0.5), (3 * D, b2[5 * D:6 * D], 1, None, 1.0)],
            "F3": [(0, b2[8 * D:9 * D], 0, None, 0.5)],
        }
        n_gates = {"F0": 0, "F1": 2, "F2": 3, "F3": 5}
        n_buf = {"F0": (0, 0), "F1": (1, 1), "F2": (2, 1), "F3": (3, 2)}
        n_ada = {"F0": 4, "F1": 14, "F2": 22, "F3": 32}
        gain_at = {1: (0, 80), 2: (0, 88), 3: (1, 72), 4: (1, 80), 5: (1, 88)}
        w_in = a["w_in"][0].rearrange("(k p) n -> p k n", p=P)
        w_in2 = a["w_in_2"][0].rearrange("(k p) n -> p k n", p=P)
        w_out = a["w_out"][0].rearrange("(k p) n -> p k n", p=P)
        w_out2 = a["w_out_2"][0].rearrange("(k p) n -> p k n", p=P)
        GROUPS1 = [("qb", 2120), ("kb", 2632), ("qi", 1536), ("ka", 512), ("vb", 3144), ("qa", 0), ("va", 1024)]
        KI = 3
        GROUPS2 = {"q": (512, QL), "kv": (896, KVL + ROPE), "uf": (0, NB), **{f"g{i}": (1184 + NB * i, NB) for i in range(4)}}
        ORDER2 = ["q 0", "q 1", "kv 0", "kv 1", "uf 0", "uf 1", "g0 0", "g0 1", "g1 0", "q_up 0", "q_up 1", "g1 1",
                  "g2 0", "g2 1", "g3 0", "fourier 0", "g3 1", "mla 0", "fourier 1", "mla 1",
                  "out 0 0", "out 0 1", "out 1 0", "out 1 1"]

        RMS = [f"F0 {t}" for t in range(T)]
        for stage, after in (("F0", "M1"), ("M1", "F1"), ("F1", "F2"), ("F2", "M2"), ("M2", "F3"), ("F3", "end")):
            if stage == "M1":
                RMS += ["index keys", "M1 out b", "M1 out a"]
            if stage == "M2":
                RMS += ["q latent", "kv latent"]
            if stage in ("F0", "M1", "F1"):
                RMS += [f"post {stage} {t}" for t in range(T)]
            RMS += [f"{after} {t}" for t in range(T)]
        TR = {"F0": 0, "M1": 1, "O1": 2, "F1": 3, "F2": 4, "M2": 5, "O2": 6, "F3": 7}

        def slot(t, s, n):
            return t[:, s, 0:n]

        def wait(e, s, v):
            if not (isinstance(v, int) and v <= 0):
                e.wait_ge(s, v)

        def gate_up(f, half, c):
            if half:
                return SLOT_B, c + B0[f]
            if isinstance(c, int) and c == 0:
                return SLOT_D, D0[f]
            return SLOT_A, c + (A0[f] - 1)

        def down_piece(f, c):
            if isinstance(c, int) and c == NC - 1:
                return SLOT_A, A0[f] + NC - 1
            return SLOT_D, c + (D0[f] + 1)

        def piece2(name):
            i = ORDER2.index(name)
            if i == 0:
                return SLOT_D, D0["M2"]
            return (SLOT_B, B0["M2"] + i // 2) if i % 2 else (SLOT_A, A0["M2"] + i // 2 - 1)

        def piece1(half, g):
            if half:
                return SLOT_B, B0["M1"] + g
            return (SLOT_D, D0["M1"]) if g == 0 else (SLOT_A, A0["M1"] + g - (1 if g < KI else 0))

        ki_piece = SLOT_A, A0["M1"] + KI - 1
        out1 = {(1, 0): (SLOT_B, B0["M1"] + 7), (1, 1): (SLOT_D, D0["M1"] + 1),
                (0, 0): (SLOT_A, A0["M1"] + 7), (0, 1): (SLOT_B, B0["M1"] + 8)}
        kv_up = SLOT_D, D0["M2"] + 1

        def used(e, piece):
            e.wait_ge(w_used[piece[0]], piece[1] + 1)

        def output_at(stage, t):
            return (4, 2)[t] if stage[0] == "M" else 4 + 2 * t

        def x_junk(half):
            return sil[:].rearrange("p t n -> p (t n)") if half == 0 else gate[:, 0, 0:NB]

        prob4 = prob.rearrange("p a (b n) -> p (a b) n", n=NB)

        def rms_ready(e, name):
            e.wait_ge(rms_done, RMS.index(name) + 1)

        def output_ready(e, stage, t):
            if stage[0] == "F" and t == 0:
                e.wait_ge(down_done, FFN.index(stage) + 1)
            elif stage[0] == "F":
                used(e, down_piece(stage, NC - 1))
            elif t == 0:
                e.wait_ge(mix_half, 1 if stage == "M1" else 2)
            else:
                e.wait_ge(w_used[SLOT_B], B0["F1" if stage == "M1" else "F3"])

        block = ctx.enter_context(nc.Block())

        @block.sync
        def _(sp):
            def raw_free(s, use):
                wait(sp, lo_ready[s], use)
                settle(use)

            def settle(v):
                if not isinstance(v, int):
                    sp.sem_inc(sp_settled, 1)

            def load(s, use, parts):
                raw_free(s, use)
                for dst, src in parts:
                    sp.dma_start(dst, src).then_inc(raw_loaded[s], 16)

            def load_k4(s, use, src, k0, c0, n, nk=4):
                dst = slot(w_raw, s, nk * n).rearrange("p (k n) -> p k n", n=n)
                m = nk // 2
                load(s, use, [(dst[:, 0:m], src[:, k0:k0 + m, c0:c0 + n]),
                              (dst[:, m:nk], src[:, k0 + m:k0 + nk, c0:c0 + n])])

            def load_gu(f, half, c):
                wg, wu, _ = ffn_w[f]
                s, use = gate_up(f, half, c)
                dst = w_raw[:, s, :].rearrange("p (k g n) -> p k g n", g=2, n=FC)
                raw_free(s, use)
                for g, w in enumerate((wg, wu)):
                    src = w.rearrange("(k p) n -> p k n", p=P)[:, 4 * half:4 * half + 4, bass.ds(c * FC, FC)]
                    sp.dma_start(dst[:, :, g, :], src).then_inc(raw_loaded[s], 16)

            def load_down(f, c):
                s, use = down_piece(f, c)
                src = ffn_w[f][2].rearrange("(c p) n -> p c n", p=P)
                dst = w_raw[:, s, :].rearrange("p (k n) -> p k n", n=D)
                raw_free(s, use)
                for j in range(2):
                    sp.dma_start(dst[:, j], src[:, bass.ds(c * 2 + j, 1), :].rearrange("p a n -> p (a n)")
                                 if not isinstance(c, int) else src[:, c * 2 + j, :]).then_inc(raw_loaded[s], 16)

            def load_ada(f, half, j):
                if half >= len(ada_steps[f]):
                    return
                w, c0, n, _, _ = ada_steps[f][half]
                src = w.rearrange("(p j) n -> p j n", j=KD)
                wait(sp, ada_done[half], j + n_ada[f])
                settle(j)
                sp.dma_start(ada_raw[:, half, 0:n], src[:, bass.ds(j, 1), c0:c0 + n].rearrange("p a n -> p (a n)")
                             if not isinstance(j, int) else src[:, j, c0:c0 + n]).then_inc(ada_loaded[half], 16)

            def load_ada_rest(f, step):
                if f not in ada_rest:
                    return
                w, c0, _ = ada_rest[f]
                half = step % 2
                sp.wait_ge(ada_done[half], n_ada[f] + KD + step // 2)
                sp.dma_start(ada_raw[:, half, 0:2 * D].rearrange("p (j n) -> p j n", n=D),
                             w.rearrange("(p j) n -> p j n", j=KD)[:, 2 * step:2 * step + 2, c0:c0 + D])\
                    .then_inc(ada_loaded[half], 16)

            def ffn_loads(f, next_a, next_b):
                load_gu(f, 0, 1)
                load_gu(f, 1, 1)
                wait(sp, h_done, 2 * NORM[f])

                def chunk(c):
                    load_down(f, c - 1)
                    load_ada(f, 0, c - 1)
                    load_ada(f, 1, c - 1)
                    load_gu(f, 0, c + 1)
                    load_gu(f, 1, c + 1)

                chunk(1)
                with sp.Fori(2, KD + 1) as c:
                    chunk(c)
                load_down(f, NC - 3)
                for i, (_, b, buf, post, _) in enumerate(gates[f]):
                    sp.dma_start(gate[:, buf, :], b.rearrange("(a n) -> a n", a=1).broadcast_to([P, D]))\
                        .then_inc(gate_loaded[buf], 16)
                    if post is not None:
                        sp.dma_start(post_gain[:, i, :], post.rearrange("(a n) -> a n", a=1).broadcast_to([P, D]))\
                            .then_inc(post_loaded[i], 16)
                load_ada_rest(f, 0)
                load_ada_rest(f, 1)
                load_gu(f, 0, NC - 1)
                load_gu(f, 1, NC - 1)
                load_down(f, NC - 2)
                load_ada_rest(f, 2)
                load_ada_rest(f, 3)
                load_down(f, NC - 1)
                next_b()
                next_a()

            sp.dma_start(c_in[:, 0, :], a["c"].rearrange("a (p j) -> (a p) j", j=KD)).then_inc(c_loaded, 16)
            sp.dma_start(c_in[:, 1, :], a["c_2"].rearrange("a (p j) -> (a p) j", j=KD)).then_inc(c_loaded, 16)
            sp.dma_start(rel_in[0:BUCKETS, :], a["rel_bias"]).then_inc(rel_loaded, 16)
            sp.dma_start(onehot[0:BUCKETS, :], a["onehot"]).then_inc(rel_loaded, 16)
            src = w1.rearrange("(p j) n -> p j n", j=KD)

            def load_first(j):
                if j >= 3:
                    sp.wait_ge(ada_done[(j - 3) % 2], (j - 3) // 2 + 1)
                m, row = j // 4, 2 * (j % 4)
                sp.dma_start(first_raw[:, j % 3, :].rearrange("p (j n) -> p j n", n=D), src[:, row:row + 2, m * D:(m + 1) * D])\
                    .then_inc(first_loaded[j % 3], 16)

            for j in range(3):
                load_first(j)
            for t in range(T):
                sp.dma_start(x_res[:, t, :], a["x"][0, t * P:(t + 1) * P, :]).then_inc(x_loaded, 16)
            for j in range(3, KD):
                load_first(j)
            load_gu("F0", 0, 0)
            load_gu("F0", 1, 0)
            sp.wait_ge(toe_sb, H)
            sp.dma_start(toe_dram.rearrange("(p n) -> p n", p=P), toe_bc.rearrange("p h n -> p (h n)"))\
                .then_inc(toe_stored, 16)
            def group1(g, half):
                load_k4(*piece1(half, g), w_in, 4 * half, GROUPS1[g][1], NB)

            def load2(name):
                s, use = piece2(name)
                what, *at = name.split()
                h = int(at[0])
                if what in GROUPS2:
                    load_k4(s, use, w_in2, 4 * h, *GROUPS2[what])
                elif what == "q_up":
                    dst = slot(w_raw, s, 3 * QL).rearrange("p (k n) -> p k n", n=QL)
                    src = a["w_q_up_2"][0].rearrange("(k p) n -> p k n", p=P)[:, :, h * QL:(h + 1) * QL]
                    load(s, use, [(dst[:, 0:2], src[:, 0:2]), (dst[:, 2:3], src[:, 2:3])])
                elif what == "out":
                    load_k4(s, use, w_out2, 4 * h, int(at[1]) * NB, NB)
                else:
                    w = a["w_fourier_out_2" if what == "fourier" else "w_mla_out_2"][0]
                    load_k4(s, use, w.rearrange("(k p) n -> p k n", p=P), 0, h * NB, NB)

            sp.wait_ge(toe_stored, 16)
            for half in range(2):
                sp.wait_ge(ada_done[half], 4)
            ffn_loads("F0", lambda: group1(0, 0), lambda: group1(0, 1))
            load_k4(*out1[1, 1], w_out, 4, NB, NB)
            for i in range(1, len(GROUPS1)):
                if i == KI:
                    dst = slot(w_raw, SLOT_A, KD * 72).rearrange("p (k n) -> p k n", n=72)
                    load(*ki_piece, [(dst[:, 4 * j:4 * j + 4], w_in[:, 4 * j:4 * j + 4, 2048:2120]) for j in range(2)])
                for half in (1, 0) if i == KI else (0, 1):
                    group1(i, half)
                if i == KI:
                    sp.wait_ge(n_lo, 4 * (TR["M1"] + 1))
                    pitch = H * CAUSAL
                    for h in range(H):
                        skew = bass.AP(toe_dram.tensor, toe_dram.offset + h * CAUSAL + P - 1, [[pitch - 1, P], [1, S]])
                        sp.dma_start(bias[:, h, :], skew).then_inc(bias_loaded, 16)
            load_k4(*out1[1, 0], w_out, 4, 0, NB)
            load_k4(*out1[0, 0], w_out, 0, 0, NB)
            load_k4(*out1[0, 1], w_out, 0, NB, NB)
            load_gu("F1", 0, 0)
            load_gu("F1", 1, 0)
            ffn_loads("F1", lambda: load_gu("F2", 0, 0), lambda: load_gu("F2", 1, 0))
            ffn_loads("F2", lambda: load2("q 0"), lambda: load2("q 1"))
            sp.wait_ge(h_done, 2 * NORM["M2"])
            sp.dma_start(dft[:], a["dft_s"].rearrange("(k p) n -> p k n", p=P)).then_inc(dft_loaded, 16)
            sp.dma_start(dftd[:], a["dft_d"].rearrange("p (k n) -> p k n", n=P)).then_inc(dft_loaded, 16)
            wkv = a["w_kv_up_2"][0].rearrange("(k p) n -> p k n", p=P)
            dst = w_raw[:, SLOT_D, :].rearrange("p (k n) -> p k n", n=D)
            for i, name in enumerate(ORDER2[2:]):
                load2(name)
                if i == 1:
                    load(*kv_up, [(dst[:, j], wkv[:, j, :]) for j in range(2)])
            load_gu("F3", 0, 0)
            load_gu("F3", 1, 0)
            nothing = lambda: None
            ffn_loads("F3", nothing, nothing)
            sp.wait_ge(gate_out, 12)
            sp.dma_start(post_gain[:, 0, :], a["final_norm_2"].rearrange("(a n) -> a n", a=1).broadcast_to([P, D]))\
                .then_inc(post_loaded[0], 16)
            for t in range(T):
                sp.wait_ge(y_ready, 12 + t + 1)
                sp.dma_start(out[0, t * P:(t + 1) * P, :], y_row[:, t, :]).then_inc(out_stored, 16)
            sp.wait_ge(out_stored, 16 * T)

        @block.gpsimd
        def _(pool):
            pool.memset(ones[:], 1.0).then_inc(pool_step, 1)
            pool.memset(minus_half[:], -0.5).then_inc(pool_step, 1)
            pool.wait_ge(pool_step, 2)
            pool.affine_select(out=ident[:], in_=ones[:], compare_op=ALU.is_equal, fill=0.0, base=0,
                               pattern=[[-1, P]], channel_multiplier=1).then_inc(const_ready, 1)
            pool.affine_select(out=tri[:], in_=ones[:], compare_op=ALU.is_ge, fill=0.0, base=0,
                               pattern=[[-1, P]], channel_multiplier=1).then_inc(const_ready, 1)
            pool.memset(first_acc, 0.0).then_inc(acc_zero, 1)

            def zero_acc(f):
                wait(pool, h_done, 2 * NORM[f])
                if f == "F0":
                    pool.wait_ge(toe_stored, 16)
                elif f == "F2":
                    pool.wait_ge(gate_out, 6)
                    pool.wait_ge(cols_out, COLS.index("F1 late") + 1)
                for half, (_, _, n, _, at) in enumerate(ada_steps[f]):
                    pool.memset(mod_acc[:, half, 0:at + n], 0.0).then_inc(acc_zero, 1)

            def rms(name, dst, ss, s, v):
                pool.wait_ge(s, v)
                pool.tensor_scalar(ss, ss, EPS, None, ALU.add).then_inc(pool_step, 1)
                pool.wait_ge(pool_step, 3 + len(made))
                pool.tensor_tensor(dst, ss, minus_half[:, 0:dst.shape[1]], ALU.pow).then_inc(rms_done, 1)
                made.append(name)

            def norm_rms(f):
                for t in range(T):
                    rms(f"{f} {t}", stat[:, 8 + t:9 + t], stat[:, t:t + 1], sq_done, 2 * NORM[f] + 1 + t)

            def post_rms(f):
                for t in range(T):
                    rms(f"post {f} {t}", stat[:, 10 + t:11 + t], stat[:, 2 + t:3 + t], fsq_done,
                        2 * {"F0": 0, "M1": 1, "F1": 2}[f] + 1 + t)

            made = []
            norm_rms("F0")
            zero_acc("F0")
            post_rms("F0")
            norm_rms("M1")
            rms("index keys", stat[:, 14:16], stat[:, 12:14], ki_sq, 1)

            def causal(v, reps, fill, strict_from=None):
                if strict_from is None:
                    return pool.affine_select(out=v, in_=v, compare_op=ALU.is_ge, fill=fill, base=0,
                                              pattern=[[0, reps], [-1, P]], channel_multiplier=1)
                return pool.affine_select(out=v, in_=v, compare_op=ALU.is_ge, fill=fill, base=-1,
                                          pattern=[[0, reps], [1, P]], channel_multiplier=-1)

            diag = lambda v: v[:, P:CAUSAL].rearrange("p (r x) -> p r x", x=P)
            pool.wait_ge(u_ready, 1)
            for c0 in (0, 2 * P):
                causal(u_sb[:, :, c0:c0 + P], H, 0.0, True).then_inc(u_masked, 1)
            pool.wait_ge(idx_acc, 2 * H)
            causal(diag(score), 2, FUTURE).then_inc(score_causal, 1)
            pool.wait_ge(a_exp, 1)
            for c0 in (0, 2 * P):
                causal(z_sb[:, :, c0:c0 + P], H, 0.0, True).then_inc(a_masked, 1)
            rms("M1 out b", stat[:, 12:14], stat[:, 4:6], osq_done, 2)
            pool.wait_ge(sel_ready, 1)
            causal(diag(work), 2, OFF).then_inc(mask_ready, 1)
            rms("M1 out a", stat[:, 14:16], stat[:, 6:8], osq_done, 4)
            post_rms("M1")
            norm_rms("F1")
            zero_acc("F1")
            post_rms("F1")
            norm_rms("F2")
            zero_acc("F2")
            norm_rms("M2")
            rms("q latent", stat[:, 48:50], stat[:, 4:6], lat_sq, 4)
            rms("kv latent", stat[:, 50:52], stat[:, 6:8], lat_sq, 4)
            norm_rms("F3")
            zero_acc("F3")
            norm_rms("end")
            assert made == RMS

        @block.scalar
        def _(act):
            copy = lambda o, i: act.activation(o, i, ACT.Copy)

            def split_hi(s, use, n=PIECE):
                act.wait_ge(raw_loaded[s], use * 32 + 32)
                wait(act, w_used[s], use)
                copy(slot(w_hi, s, n), slot(w_raw, s, n)).then_inc(hi_ready[s], 1)

            def norm(f):
                norm_squares(f)
                norm_hi(TR[f])

            def norm_squares(f):
                r = NORM[f]
                for t in range(T):
                    if r:
                        act.wait_ge(h_done, 2 * r - 1 + t)
                    else:
                        act.wait_ge(x_loaded, 16 * T)
                    act.activation(y_row[:, t, :], x_res[:, t, :], ACT.Square, scale=D ** -0.5, accum_out=stat[:, t:t + 1]).then_inc(sq_done, 1)

            def norm_hi(r):
                for j in range(KD // 2):
                    act.wait_ge(n_ready, 8 * r + 2 * j + 2)
                    copy(nT_hi[:, 2 * j:2 * j + 2, :], nT[:, 2 * j:2 * j + 2, :]).then_inc(n_hi, 1)

            def body(f, c, down=True, gu=True, nxt=PIECE):
                i = FFN.index(f) * NC
                if down and gu:
                    split_hi(*down_piece(f, c - 1))
                    act.wait_ge(h_ready, c + i)
                    copy(hT_hi[:], h_act[:]).then_inc(ht_hi, 1)
                elif down:
                    act.wait_ge(h_ready, c + i)
                    copy(nT_hi[:, 0:2, :], h_act[:]).then_inc(ht_hi, 1)
                    if nxt:
                        split_hi(SLOT_D, D0[f] + NC, nxt)
                if gu:
                    if isinstance(c, int) and c == NC - 1:
                        split_hi(*down_piece(f, c))
                    else:
                        split_hi(*gate_up(f, 0, c + 1))
                    used(act, gate_up(f, 1, c))
                    wait(act, h_ready, c + i)
                    b = 2 if isinstance(c, int) and c == 0 else 0
                    act.activation(sil[:], ps[:, b, :].rearrange("p (k n) -> p k n", n=S), ACT.Silu).then_inc(silu_done, 1)
                    if nxt:
                        split_hi(*gate_up(f, 1, c + 1), nxt)

            def ffn(f, nxt=PIECE):
                if f != "F0":
                    norm_squares(f)
                if f in ("F1", "F3"):
                    split_hi(*gate_up(f, 1, 0))
                norm_hi(TR[f])
                body(f, 0, down=False)
                body(f, 1)
                with act.Fori(2, NC - 1) as c:
                    body(f, c)
                body(f, NC - 1, nxt=nxt)
                body(f, NC, gu=False, nxt=nxt)

            def residual_sq(stage):
                for t in range(T):
                    output_ready(act, stage, t)
                    b = output_at(stage, t)
                    junk = nT[:, 4 * t:4 * t + 4, :].rearrange("p k n -> p (k n)")
                    act.activation(junk, ps[:, b:b + 2, :].rearrange("p b n -> p (b n)"),
                                   ACT.Square, scale=D ** -0.5, accum_out=stat[:, 2 + t:3 + t]).then_inc(fsq_done, 1)

            act.wait_ge(c_loaded, 32)
            act.activation(c_act[:], c_in[:], ACT.Silu).then_inc(c_ready, 1)
            for blk, rows in enumerate((
                [("b_ada", 72), ("g_pre", 24), ("g_out_a", 4), ("g_out_b", 4)],
                [("ada_b_2", 72), ("ffn1_norm_2", 8), ("mix_norm_2", 8), ("ffn2_norm_2", 8), ("q_norm_2", 3), ("kv_norm_2", 2)],
            )):
                at = 0
                for name, n in rows:
                    v = a[name]
                    v = v.rearrange("a b n -> (a b n)") if len(v.shape) == 3 else v.rearrange("a n -> (a n)")
                    act.dma_start(vec_rows[at:at + n, blk, :], v.rearrange("(r q) -> r q", q=P)).then_inc(small_loaded, 16)
                    at += n
            act.dma_start(gki[:], a["g_kidx"].broadcast_to([P, DH])).then_inc(small_loaded, 16)
            act.dma_start(freq[:], a["inv_freq"].broadcast_to([P, 16])).then_inc(small_loaded, 16)
            act.dma_start(pos_i[:], a["positions_2"].rearrange("a (t p) -> p (a t)", p=P), allow_slow_non_contiguous=True)\
                .then_inc(small_loaded, 16)
            for h in range(H):
                act.wait_ge(toe_mm, h + 1)
                copy(toe_bc[:, h, :], ps[:, h % 4, 0:CAUSAL]).then_inc(toe_sb, 1)
            norm_squares("F0")
            split_hi(*gate_up("F0", 0, 0))
            split_hi(*gate_up("F0", 1, 0))
            ffn("F0")
            residual_sq("F0")
            norm("M1")


            def transposed_group(g, i):
                used(act, piece1(0 if g == KI else 1, g))
                for b in range(2):
                    copy(qkT[:, i, 2 * b:2 * b + 2, :],
                         ps[:, 2 * (g % 2) + b, :].rearrange("p (k n) -> p k n", n=S)).then_inc(grp_out, 1)

            def row_group(g, i):
                used(act, piece1(1, g))
                for t in range(T):
                    copy(v_row[:, i, t, :], ps[:, 2 * (g % 2) + t, :]).then_inc(grp_out, 1)

            def out_squares(half, i):
                for t in range(T):
                    wait(act, osq_done, 2 * i + t - 1)
                    act.activation(x_junk(t), y_row[:, t, half * NB:(half + 1) * NB], ACT.Square, scale=NB ** -0.5,
                                   accum_out=stat[:, 4 + 2 * i + t:5 + 2 * i + t]).then_inc(osq_done, 1)

            split_hi(*piece1(0, 1))
            split_hi(*piece1(1, 1))
            split_hi(*out1[1, 1])
            transposed_group(0, TQB)
            split_hi(*piece1(0, 2))
            split_hi(*piece1(1, 2))
            transposed_group(1, TKB)
            split_hi(*ki_piece, KD * 72)
            for h in range(H):
                act.wait_ge(z_mm, h + 1)
                act.activation(z_sb[:, h, :], ps[:, 4 + h % 4, 0:CAUSAL], ACT.Copy, scale=DH ** -0.5).then_inc(z_out, 1)
            act.wait_ge(z_out, H)
            act.activation(e_sb[:], z_sb[:], ACT.Abs).then_inc(z_ln, 1)
            split_hi(*piece1(1, 3))
            act.wait_ge(z_ln, 1)
            act.activation(e_sb[:], e_sb[:], ACT.Exp, scale=-1.0).then_inc(z_ln, 1)
            split_hi(*piece1(0, 3))
            transposed_group(2, TQI)
            act.wait_ge(z_ln, 2)
            act.activation(e_sb[:], e_sb[:], ACT.Ln, bias=1.0).then_inc(z_ln, 1)
            split_hi(*piece1(0, 4))
            for h in range(H):
                act.wait_ge(idx_mm, h + 1)
                if h >= 4:
                    act.wait_ge(idx_acc, 2 * (h - 3))
                act.activation(relu[:, h % 4, :], ps[:, 4 + h % 4, 0:CAUSAL], ACT.Relu).then_inc(idx_relu, 1)
            split_hi(*piece1(1, 4))
            transposed_group(3, TKA)
            split_hi(*piece1(0, 5))
            act.wait_ge(loga_ready, 1)
            act.activation(z_sb[:], z_sb[:], ACT.Exp).then_inc(a_exp, 1)
            row_group(4, 1)
            split_hi(*piece1(1, 5))
            split_hi(*piece1(0, 6))
            act.wait_ge(ob_out, T)
            out_squares(1, 0)
            transposed_group(5, TQA)
            split_hi(*piece1(1, 6))
            split_hi(*out1[0, 0])
            for h in range(H):
                for t in range(T):
                    act.wait_ge(lmax_ready, h + 1)
                    cols = slice(0, S) if t else slice(S, CAUSAL)
                    act.activation(z_sb[:, h, cols], z_sb[:, h, cols], ACT.Exp,
                                   bias=stat[:, 16 + 2 * h + t:17 + 2 * h + t],
                                   accum_out=trig[:, 0, t, h:h + 1]).then_inc(p_exp, 1)
            row_group(6, 0)
            for j in range(2):
                act.wait_ge(n_ready, 8 * TR["O1"] + 2 * j + 2)
                copy(nT_hi[:, 4 + 2 * j:6 + 2 * j, :], ob_T[:, 2 * j:2 * j + 2, :]).then_inc(n_hi, 1)
            for h in range(H):
                if h == 4:
                    split_hi(*out1[1, 0])
                act.wait_ge(p_tr, h + 1)
                copy(e_sb[:, h, :], ps[:, 6 + h % 2, 0:CAUSAL]).then_inc(pT_out, 1)
            act.wait_ge(oa_out, T)
            out_squares(0, 1)
            split_hi(*out1[0, 1])
            for j in range(2):
                act.wait_ge(n_ready, 8 * TR["O1"] + 2 * j + 6)
                copy(nT_hi[:, 2 * j:2 * j + 2, :], nT[:, 2 * j:2 * j + 2, :]).then_inc(n_hi, 1)
            split_hi(*gate_up("F1", 0, 0))
            residual_sq("M1")
            ffn("F1")
            residual_sq("F1")
            ffn("F2", nxt=4 * QL)
            norm("M2")

            def hi2(name):
                split_hi(*piece2(name), {"q": 4 * QL, "kv": 4 * (KVL + ROPE), "q_up": 3 * QL}.get(name.split()[0], PIECE))

            def group_done(name):
                s, use = piece2(name + " 1")
                act.wait_ge(w_used[s], use + 1)

            def row_out(name, bank, dst, n):
                group_done(name)
                for t in range(T):
                    copy(dst[:, t], ps[:, bank + t, 0:n]).then_inc(grp_out, 1)

            def gate_group(i):
                group_done(f"g{i}")
                for t in range(T):
                    act.activation(sig[:, t, i * NB:(i + 1) * NB], ps[:, 2 * ((3 + i) % 2) + t, :], ACT.Sigmoid).then_inc(grp_out, 1)

            hi2("kv 0")
            hi2("kv 1")
            row_out("q", 0, lat[:, :, 0:QL], QL)
            hi2("uf 0")
            hi2("uf 1")
            split_hi(*kv_up)
            row_out("kv", 2, lat[:, :, QL:], KVL + ROPE)
            act.wait_ge(grp_out, 14 + 4)
            for t in range(T):
                wait(act, lat_sq, 2 * t)
                act.activation(x_junk(0)[:, 0:QL], lat[:, t, 0:QL], ACT.Square, scale=QL ** -0.5,
                               accum_out=stat[:, 4 + t:5 + t]).then_inc(lat_sq, 1)
                act.activation(x_junk(1)[:, 0:KVL], lat[:, t, QL:QL + KVL], ACT.Square, scale=KVL ** -0.5,
                               accum_out=stat[:, 6 + t:7 + t]).then_inc(lat_sq, 1)
            hi2("g0 0")
            act.wait_ge(trig_arg, 1)
            act.activation(trig[:, 1], trig[:, 0], ACT.Sin).then_inc(trig_done, 1)
            act.activation(trig[:, 2], trig[:, 0], ACT.Sin, scale=0.5).then_inc(trig_done, 1)
            row_out("uf", 0, uf, NB)
            hi2("g0 1")
            act.wait_ge(lat_out, 5)
            copy(hT_hi[:], h_act[:]).then_inc(lat_hi, 1)
            hi2("g1 0")
            for g in range(4):
                act.wait_ge(cu_mm, g + 1)
                copy(cu[:, g, :], ps[:, 4 + g, :]).then_inc(cu_out, 1)
            hi2("q_up 0")
            gate_group(0)
            used(act, kv_up)
            copy(x_hi[:, 0:3, :], nT[:, 0:3, :]).then_inc(lat_hi, 1)
            for t in range(T):
                for n in range(2):
                    copy(kv_row[:, t, n * NB:(n + 1) * NB], ps[:, 4 + 2 * t + n, :]).then_inc(up_out, 1)
            hi2("q_up 1")
            hi2("g1 1")
            hi2("g2 0")
            gate_group(1)
            hi2("g2 1")
            act.wait_ge(f_out, 4)
            copy(x_hi[:, 4:8, :], nT[:, 4:8, :]).then_inc(f_hi, 1)
            hi2("g3 0")
            for i in range(8):
                act.wait_ge(qk_tr, i + 1)
                dst = kT if i < 4 else qT
                copy(dst[0:QH, 2 * (i % 4):2 * (i % 4) + 2, :],
                     ps[0:QH, 4 + i % 4, :].rearrange("p (k n) -> p k n", n=S)).then_inc(qkT_out, 1)
            hi2("fourier 0")
            gate_group(2)
            for h in range(H):
                act.wait_ge(smax_ready, h + 1)
                if h >= 4:
                    act.wait_ge(s_tr, h - 3)
                for t in range(T):
                    act.activation(prob4[:, h % 4, t * S:(t + 1) * S], ps[:, 4 + h % 3, t * S:(t + 1) * S], ACT.Exp,
                                   bias=stat[:, 16 + 2 * h + t:17 + 2 * h + t],
                                   accum_out=trig[:, 0, t, h:h + 1]).then_inc(s_exp, 1)
                if h == 1:
                    hi2("g3 1")
            hi2("mla 0")
            act.wait_ge(omT_out, 4)
            copy(x_hi[:, 0:4, :], nT[:, 0:4, :]).then_inc(omT_hi, 1)
            gate_group(3)
            hi2("fourier 1")
            hi2("mla 1")
            hi2("out 0 0")
            for j in range(KD // 2):
                act.wait_ge(n_ready, 8 * TR["O2"] + 2 * j + 2)
                copy(nT_hi[:, 2 * j:2 * j + 2, :], nT[:, 2 * j:2 * j + 2, :]).then_inc(n_hi, 1)
                if j == 1:
                    hi2("out 0 1")
            hi2("out 1 0")
            hi2("out 1 1")
            used(act, piece2("mla 1"))
            split_hi(*gate_up("F3", 0, 0))
            ffn("F3", nxt=0)
            for t in range(T):
                act.wait_ge(h_done, 11 + t)
                act.activation(y_row[:, t, :], x_res[:, t, :], ACT.Square, scale=D ** -0.5, accum_out=stat[:, t:t + 1]).then_inc(sq_done, 1)

        @block.vector
        def _(dve):
            steps = [0]

            def link(ins):
                steps[0] += 1
                ins.then_inc(dve_step, 1)
                dve.wait_ge(dve_step, steps[0])

            def split_lo(s, use, n=PIECE):
                dve.wait_ge(hi_ready[s], use + 1)
                dve.tensor_tensor(slot(w_lo, s, n), slot(w_raw, s, n), slot(w_hi, s, n).bitcast(F32),
                                  ALU.subtract).then_inc(lo_ready[s], 1)

            def norm(f):
                r = NORM[f]
                if r:
                    norm_rows(f)
                batch = {"F0": "start", "M1": "F0 late", "F2": "F1 late", "M2": "F2 late"}.get(f)
                if batch:
                    mods_out(batch)
                cols = mod_col[:, r]
                norm_out(TR[f], lambda k, src: (dve.tensor_scalar(nT[:, k, :], src, cols[:, 0, k:k + 1], cols[:, 1, k:k + 1],
                                                              ALU.mult, ALU.add)))

            def norm_rows(f):
                for t in range(T):
                    rms_ready(dve, f"{f} {t}")
                    dve.tensor_scalar(y_row[:, t, :], x_res[:, t, :], stat[:, 8 + t:9 + t], None, ALU.mult).then_inc(y_ready, 1)

            def norm_out(r, scaled):
                def lo(j):
                    dve.wait_ge(n_hi, 4 * r + j + 1)
                    dve.tensor_tensor(nT_lo[:, 2 * j:2 * j + 2, :], nT[:, 2 * j:2 * j + 2, :],
                                      nT_hi[:, 2 * j:2 * j + 2, :].bitcast(F32), ALU.subtract).then_inc(n_lo, 1)
                for j in range(KD // 2):
                    dve.wait_ge(n_tr, 4 * r + j + 1)
                    for k in (2 * j, 2 * j + 1):
                        scaled(k, ps[:, 4 + j, (k % 2) * S:(k % 2 + 1) * S]).then_inc(n_ready, 1)
                    if j:
                        lo(j - 1)
                lo(KD // 2 - 1)

            def mods_out(batch):
                dve.wait_ge(acc_cols, COLS.index(batch) + 1)
                for i, (_, blk, m, r) in enumerate(col_sums[batch]):
                    src = ps[:, cols_bank(batch), KD * i:KD * i + KD]
                    b = vec_col[:, blk, KD * m:KD * m + KD]
                    if m % 3 == 0:
                        last = dve.tensor_tensor(mod_col[:, r, 1, :], src, b, ALU.add)
                        link(last)
                    else:
                        g = gain_at.get(r, (0, 72))
                        link(dve.tensor_tensor(mod_col[:, r, 0, :], src, b, ALU.add))
                        link(dve.scalar_tensor_tensor(mod_col[:, r, 0, :], mod_col[:, r, 0, :], 1.0,
                                                      vec_col[:, g[0], g[1]:g[1] + KD], ALU.add, ALU.mult))
                dve.sem_inc(cols_out, 1)

            def gate_half(f, i, half):
                _, _, buf, post, factor = gates[f][i]
                n = 2 * (n_gates[f] + i) + half
                v = gate[:, buf, half * NB:(half + 1) * NB]
                dve.wait_ge(gate_loaded[buf], 16 * (n_buf[f][buf] + 1))
                dve.wait_ge(acc_gate, n + 1)
                link(dve.tensor_tensor(v, ps[:, 2 + half, :], v, ALU.add))
                if post is None:
                    dve.tensor_scalar(v, v, factor, None, ALU.mult).then_inc(gate_out, 1)
                else:
                    dve.wait_ge(post_loaded[i], 16 * {"F0": 1, "F1": 2}[f])
                    dve.scalar_tensor_tensor(v, v, factor, post_gain[:, i, half * NB:(half + 1) * NB],
                                             ALU.mult, ALU.mult).then_inc(gate_out, 1)

            def ada(f, half, j):
                if half >= len(ada_steps[f]):
                    return
                _, _, n, blk, at = ada_steps[f][half]
                dve.wait_ge(ada_loaded[half], j * 16 + 16 * (n_ada[f] - 3))
                wait(dve, ada_done[half], j + n_ada[f])
                cj = c_act[:, blk, bass.ds(j, 1)] if not isinstance(j, int) else c_act[:, blk, j:j + 1]
                acc = mod_acc[:, half, at:at + n]
                dve.scalar_tensor_tensor(acc, ada_raw[:, half, 0:n], cj, acc, ALU.mult, ALU.add).then_inc(ada_done[half], 1)

            def rest(f, step):
                if f not in ada_rest:
                    return
                blk, half = ada_rest[f][2], step % 2
                acc = mod_acc[:, 1, 0:D]
                dve.wait_ge(ada_loaded[half], 16 * (n_ada[f] - 3 + KD + step // 2))
                if step:
                    dve.wait_ge(ada_done[1 - half], n_ada[f] + KD + (step + 1) // 2)
                link(dve.scalar_tensor_tensor(acc, ada_raw[:, half, 0:D], c_act[:, blk, 2 * step:2 * step + 1], acc,
                                              ALU.mult, ALU.add))
                dve.scalar_tensor_tensor(acc, ada_raw[:, half, D:2 * D], c_act[:, blk, 2 * step + 1:2 * step + 2], acc,
                                         ALU.mult, ALU.add).then_inc(ada_done[half], 1)

            def body(f, c, down=True, gu=True, nxt=PIECE, mods=False, hooks=((), (), ())):
                i = FFN.index(f) * NC
                if down and gu:
                    split_lo(*down_piece(f, c - 1))
                    dve.wait_ge(ht_hi, c + i)
                    dve.tensor_tensor(hT_lo[:], h_act[:], hT_hi[:].bitcast(F32), ALU.subtract).then_inc(ht_lo, 1)
                    for hook in hooks[0]:
                        hook()
                    if mods:
                        ada(f, 0, c - 1)
                    for hook in hooks[1]:
                        hook()
                    if mods:
                        ada(f, 1, c - 1)
                elif down:
                    dve.wait_ge(ht_hi, c + i)
                    dve.tensor_tensor(nT_lo[:, 0:2, :], h_act[:], nT_hi[:, 0:2, :].bitcast(F32), ALU.subtract).then_inc(ht_lo, 1)
                    for hook in hooks[1]:
                        hook()
                    if nxt:
                        split_lo(SLOT_D, D0[f] + NC, nxt)
                if gu:
                    if isinstance(c, int) and c == NC - 1:
                        split_lo(*down_piece(f, c))
                    else:
                        split_lo(*gate_up(f, 0, c + 1))
                    dve.wait_ge(silu_done, c + i + 1)
                    wait(dve, ht_lo, c + i)
                    b = 3 if isinstance(c, int) and c == 0 else 1
                    dve.tensor_tensor(h_act[:], ps[:, b, :].rearrange("p (k n) -> p k n", n=S), sil[:], ALU.mult)\
                        .then_inc(h_ready, 1)
                    if nxt:
                        split_lo(*gate_up(f, 1, c + 1), nxt)
                for hook in hooks[2]:
                    hook()

            def ffn(f, nxt=PIECE):
                norm(f)
                if f != "F2":
                    split_lo(*gate_up(f, 1, 0))
                body(f, 0, down=False)
                dve.wait_ge(acc_zero, 1 + {"F0": 2, "F1": 4, "F2": 6, "F3": 7}[f])
                with dve.Fori(1, KD + 1) as c:
                    body(f, c, mods=True)
                body(f, NC - 2, hooks=([lambda: rest(f, 0)],
                                       [lambda: mods_out(f"{f} early")] if f"{f} early" in COLS else (),
                                       [lambda: rest(f, 1), lambda: gate_half(f, 0, 0)]))
                body(f, NC - 1, nxt=nxt, hooks=([lambda: rest(f, 2)], [lambda: gate_half(f, 0, 1)], ()))
                body(f, NC, gu=False, nxt=nxt, hooks=((), [lambda: rest(f, 3)], ()))

            def residual(stage, buf, post):
                for t in range(T):
                    b = output_at(stage, t)
                    src = ps[:, b:b + 2, :].rearrange("p b n -> p (b n)")
                    if post:
                        dve.wait_ge(fsq_done, 2 * {"F0": 0, "M1": 1, "F1": 2}[stage] + 1 + t)
                    else:
                        output_ready(dve, stage, t)
                    link(dve.tensor_tensor(y_row[:, t, :], src, gate[:, buf, :], ALU.mult))
                    if post:
                        rms_ready(dve, f"post {stage} {t}")
                        dve.scalar_tensor_tensor(x_res[:, t, :], y_row[:, t, :], stat[:, 10 + t:11 + t], x_res[:, t, :],
                                                 ALU.mult, ALU.add).then_inc(h_done, 1)
                    else:
                        dve.tensor_tensor(x_res[:, t, :], x_res[:, t, :], y_row[:, t, :], ALU.add).then_inc(h_done, 1)

            def vectors():
                dve.wait_ge(vec_tr, 1)
                for b in range(2):
                    dve.tensor_copy(vec_col[:, b, 0:VECS[b]], ps[:, 7, b * P:b * P + VECS[b]]).then_inc(vec_ready, 1)

            dve.wait_ge(rel_loaded, 32)
            dve.tensor_copy(rel_bc[0:BUCKETS], rel_in[0:BUCKETS, :].rearrange("p (h o) -> p h o", o=1)
                            .broadcast_to([BUCKETS, H, P])).then_inc(rel_ready, 1)
            dve.wait_ge(c_ready, 1)
            dve.wait_ge(acc_zero, 1)
            for j in range(KD):
                dve.wait_ge(first_loaded[j % 3], 16 * (j // 3 + 1))
                if j:
                    dve.wait_ge(ada_done[(j - 1) % 2], (j - 1) // 2 + 1)
                m, row = j // 4, 2 * (j % 4)
                acc = first_acc[:, m * D:(m + 1) * D]
                link(dve.scalar_tensor_tensor(acc, first_raw[:, j % 3, 0:D], c_act[:, 0, row:row + 1], acc, ALU.mult, ALU.add))
                dve.scalar_tensor_tensor(acc, first_raw[:, j % 3, D:2 * D], c_act[:, 0, row + 1:row + 2], acc,
                                         ALU.mult, ALU.add).then_inc(ada_done[j % 2], 1)
                if j == 4:
                    vectors()
                    norm_rows("F0")
            split_lo(*gate_up("F0", 0, 0))
            ffn("F0")
            residual("F0", 0, True)

            norm("M1")
            gate_half("F0", 1, 0)
            gate_half("F0", 1, 1)
            split_lo(*piece1(0, 1))
            split_lo(*piece1(1, 1))
            split_lo(*out1[1, 1])
            split_lo(*piece1(0, 2))
            split_lo(*piece1(1, 2))
            split_lo(*ki_piece, KD * 72)
            split_lo(*piece1(1, 3))
            used(dve, ki_piece)
            for t in range(T):
                link(dve.tensor_copy(kw_row[:, t, :], ps[:, 4 + t, 0:72]))
                link(dve.tensor_scalar(wi[:, t * H:(t + 1) * H], kw_row[:, t, 64:72], (H * DH) ** -0.5, None, ALU.mult))
            link(dve.scalar_tensor_tensor(ki2[:, :, 0:DH], kw_row[:, :, 0:DH], 1.0 / DH, kw_row[:, :, 0:DH], ALU.mult, ALU.mult))
            dve.tensor_reduce(stat[:, 12:14], ki2[:, :, 0:DH], AX.X, ALU.add).then_inc(ki_sq, 1)
            rms_ready(dve, "index keys")
            for t in range(T):
                for half in range(2):
                    link(dve.scalar_tensor_tensor(ki2[:, t, half * DH:(half + 1) * DH], kw_row[:, t, 0:DH], stat[:, 14 + t:15 + t],
                                                  gki[:], ALU.mult, ALU.mult))
            dve.sem_inc(ki_ready, 1)
            split_lo(*piece1(0, 3))
            dve.wait_ge(ki_tr, 1)
            dve.tensor_copy(kiT[:], ps[:, 6, 0:S]).then_inc(kiT_ready, 1)
            dve.wait_ge(z_ln, 3)
            dve.scalar_tensor_tensor(u_sb[:], z_sb[:], 0.0, e_sb[:], ALU.max, ALU.add).then_inc(u_ready, 1)
            split_lo(*piece1(0, 4))
            for h in range(H):
                dve.wait_ge(idx_relu, h + 1)
                for t in (1, 0):
                    cols = slice(0, S) if t else slice(S, CAUSAL)
                    w = wi[:, t * H + h:t * H + h + 1]
                    if h == 0:
                        dve.tensor_scalar(score[:, cols], relu[:, 0, cols], w, None, ALU.mult).then_inc(idx_acc, 1)
                    else:
                        dve.wait_ge(idx_acc, 2 * h)
                        dve.scalar_tensor_tensor(score[:, cols], relu[:, h % 4, cols], w, score[:, cols],
                                                 ALU.mult, ALU.add).then_inc(idx_acc, 1)

            def topk(first, last):
                for r in range(first, last):
                    for t in (1, 0):
                        cols = slice(0, S) if t else slice(S, CAUSAL)
                        src = score if r == 0 else work
                        dve.max(stat[:, 48 + 8 * t:56 + 8 * t], src[:, cols]).then_inc(top_found, 1)
                    for t in (1, 0):
                        cols = slice(0, S) if t else slice(S, CAUSAL)
                        src = score if r == 0 else work
                        dve.wait_ge(top_found, 2 * r + 2 - t)
                        dve.match_replace(out=work[:, cols], in_to_replace=stat[:, 48 + 8 * t:56 + 8 * t],
                                          in_values=src[:, cols], imm_value=DONE).then_inc(top_taken, 1)
                    dve.wait_ge(top_taken, 2 * r + 2)

            split_lo(*piece1(1, 4))
            dve.wait_ge(score_causal, 1)
            topk(0, 1)
            for h in range(H):
                dve.wait_ge(r_mm, h + 1)
                dve.tensor_tensor(z_sb[:, h, :], z_sb[:, h, :], ps[:, 4 + h % 4, 0:CAUSAL], ALU.subtract).then_inc(r_out, 1)
            dve.wait_ge(r_out, H)
            dve.tensor_scalar(z_sb[:], z_sb[:], 0.0, None, ALU.min).then_inc(loga_ready, 1)
            split_lo(*piece1(0, 5))
            topk(1, 5)
            split_lo(*piece1(1, 5))
            split_lo(*piece1(0, 6))
            for t in range(T):
                dve.wait_ge(ob_mm, 1)
                dve.tensor_copy(y_row[:, t, NB:2 * NB], ps[:, 4 + t, :]).then_inc(ob_out, 1)
            topk(5, TOPK // 8)
            dve.tensor_scalar(work[:], work[:], DONE, OFF, ALU.not_equal, ALU.mult).then_inc(sel_ready, 1)
            rms_ready(dve, "M1 out b")
            for t in range(T):
                v = y_row[:, t, NB:2 * NB]
                link(dve.tensor_scalar(v, v, stat[:, 12 + t:13 + t], None, ALU.mult))
            dve.sem_inc(ob_ready, 1)
            dve.wait_ge(bias_loaded, 16 * H)
            dve.wait_ge(mask_ready, 1)
            dve.wait_ge(r_mm, H)
            for cols, src in ((slice(0, S), bias[:, :, :]), (slice(S, CAUSAL), bias[:, :, P:S])):
                w = work[:, cols]
                n = w.shape[1]
                link(dve.tensor_tensor(u_sb[:, :, cols], src, w.rearrange("p (o n) -> p o n", o=1).broadcast_to([P, H, n]), ALU.add))
            split_lo(*piece1(1, 6))

            def out_half(first_bank, first_k, j0, o_T):
                for j in range(2):
                    dve.wait_ge(n_tr, 4 * TR["O1"] + j0 + j + 1)
                    for i in range(2):
                        k = 2 * j + i
                        dve.tensor_scalar(o_T[:, k, :], ps[:, first_bank + j, i * S:(i + 1) * S],
                                          vec_col[:, 0, 96 + first_k + k:97 + first_k + k], None, ALU.mult).then_inc(n_ready, 1)

            def out_lo(first_k, j0, o_T):
                for j in range(2):
                    dve.wait_ge(n_hi, 4 * TR["O1"] + j0 + j + 1)
                    k = slice(first_k + 2 * j, first_k + 2 * j + 2)
                    dve.tensor_tensor(nT_lo[:, k, :], o_T[:, 2 * j:2 * j + 2, :], nT_hi[:, k, :].bitcast(F32),
                                      ALU.subtract).then_inc(n_lo, 1)

            out_half(2, 4, 0, ob_T)
            for h in range(H):
                dve.wait_ge(l_mm, h + 1)
                link(dve.scalar_tensor_tensor(z_sb[:, h, :], ps[:, 4 + h % 4, 0:CAUSAL], DH ** -0.5, u_sb[:, h, :],
                                              ALU.mult, ALU.add))
                dve.sem_inc(l_out, 1)
                for t in range(T):
                    cols = slice(0, S) if t else slice(S, CAUSAL)
                    m = stat[:, 16 + 2 * h + t:17 + 2 * h + t]
                    link(dve.tensor_reduce(m, z_sb[:, h, cols], AX.X, ALU.max, negate=True))
                dve.sem_inc(lmax_ready, 1)
            split_lo(*out1[0, 0])
            dve.wait_ge(p_exp, 2 * H)
            link(dve.reciprocal(trig[:, 1, :, 0:H], trig[:, 0, :, 0:H]))
            out_lo(4, 0, ob_T)
            split_lo(*out1[1, 0])
            dve.wait_ge(oa_mm, 1)
            for t in range(T):
                rs = trig[:, 1, t, 0:H].rearrange("p (h o) -> p h o", o=1).broadcast_to([P, H, DH])
                dve.tensor_tensor(y_row[:, t, 0:NB].rearrange("p (h d) -> p h d", d=DH),
                                  ps[:, t, :].rearrange("p (h d) -> p h d", d=DH), rs, ALU.mult).then_inc(oa_out, 1)
            rms_ready(dve, "M1 out a")
            for t in range(T):
                v = y_row[:, t, 0:NB]
                link(dve.tensor_scalar(v, v, stat[:, 14 + t:15 + t], None, ALU.mult))
            dve.sem_inc(o_ready, 1)
            out_half(6, 0, 2, nT)
            out_lo(0, 2, nT)
            split_lo(*out1[0, 1])
            split_lo(*gate_up("F1", 0, 0))
            residual("M1", 1, True)
            ffn("F1")
            residual("F1", 0, True)
            ffn("F2", nxt=4 * QL)
            residual("F2", 0, False)

            norm("M2")
            gate_half("F2", 1, 0)
            gate_half("F2", 1, 1)

            def lo2(name):
                split_lo(*piece2(name), {"q": 4 * QL, "kv": 4 * (KVL + ROPE), "q_up": 3 * QL}.get(name.split()[0], PIECE))

            lo2("kv 0")
            lo2("kv 1")
            link(dve.tensor_copy(pos_f[:], pos_i[:]))
            for t in range(T):
                link(dve.tensor_scalar(angle[:, t, :], freq[:], pos_f[:, t:t + 1], None, ALU.mult))
            link(dve.tensor_scalar(trig[:, 3], angle[:], 0.15915494309189535, ROUND, ALU.mult, ALU.add))
            link(dve.tensor_scalar(trig[:, 3], trig[:, 3], ROUND, None, ALU.subtract))
            for part in TWO_PI:
                link(dve.scalar_tensor_tensor(angle[:], trig[:, 3], -part, angle[:], ALU.mult, ALU.add))
            dve.tensor_scalar(trig[:, 0], angle[:], PI, -PI, ALU.min, ALU.max).then_inc(trig_arg, 1)
            lo2("uf 0")
            lo2("uf 1")
            rms_ready(dve, "kv latent")
            for t in range(T):
                dve.tensor_scalar(lat[:, t, 0:QL], lat[:, t, 0:QL], stat[:, 48 + t:49 + t], None, ALU.mult).then_inc(lat_ready, 1)
                dve.tensor_scalar(lat[:, t, QL:QL + KVL], lat[:, t, QL:QL + KVL], stat[:, 50 + t:51 + t], None, ALU.mult)\
                    .then_inc(lat_ready, 1)
            lo2("g0 0")
            split_lo(*kv_up)
            dve.wait_ge(trig_done, 2)
            link(dve.tensor_tensor(trig[:, 4], trig[:, 2], trig[:, 2], ALU.mult))
            link(dve.tensor_scalar(trig[:, 4], trig[:, 4], -2.0, 1.0, ALU.mult, ALU.add))
            dve.wait_ge(lat_tr, 1)
            for k in (3, 4, 0, 1, 2):
                src = ps[:, (6, 6, 7, 7, 5)[k], (k % 2) * S:(k % 2 + 1) * S]
                dst = nT[:, k, :] if k < 3 else h_act[:, k - 3, :]
                dve.tensor_scalar(dst, src, vec_col[:, 1, 96 + k:97 + k], None, ALU.mult).then_inc(lat_out, 1)
            lo2("g0 1")
            dve.wait_ge(lat_hi, 1)
            dve.tensor_tensor(hT_lo[:], h_act[:], hT_hi[:].bitcast(F32), ALU.subtract).then_inc(lat_lo, 1)
            lo2("g1 0")
            cos, sin = trig[:, 4], trig[:, 1]

            def rotate(x1, x2, o1, o2, tmp, co, si):
                link(dve.tensor_tensor(tmp[:, 0], x1, co, ALU.mult))
                link(dve.tensor_tensor(tmp[:, 1], x2, si, ALU.mult))
                link(dve.tensor_tensor(tmp[:, 2], x2, co, ALU.mult))
                link(dve.tensor_tensor(tmp[:, 3], x1, si, ALU.mult))
                link(dve.tensor_tensor(o1, tmp[:, 0], tmp[:, 1], ALU.subtract))
                link(dve.tensor_tensor(o2, tmp[:, 2], tmp[:, 3], ALU.add))

            tmp = sil[:].rearrange("p t n -> p (t n)").rearrange("p (q h r) -> p q h r", q=4, r=16)
            k_rot = trig[:, 2, :, :]
            k_rot2 = trig[:, 5, :, :]
            for t in range(T):
                x = lat[:, t, QL + KVL:QL + KVL + ROPE]
                rotate(x[:, 0:16], x[:, 16:32], k_rot[:, t, :], k_rot2[:, t, :],
                       tmp[:, :, 0, :], cos[:, t, :], sin[:, t, :])
            for t in range(T):
                kr = k_row[:, t, :].rearrange("p (h d) -> p h d", d=QH)
                for o, src in ((QK, k_rot), (QK + 16, k_rot2)):
                    link(dve.tensor_copy(kr[:, :, o:o + 16], src[:, t, :].rearrange("p (o r) -> p o r", o=1).broadcast_to([P, H, 16])))
            lo2("q_up 0")
            dve.wait_ge(lat_hi, 2)
            dve.tensor_tensor(x_lo[:, 0:3, :], nT[:, 0:3, :], x_hi[:, 0:3, :].bitcast(F32), ALU.subtract).then_inc(lat_lo, 1)
            dve.wait_ge(up_out, 4)
            for t in range(T):
                kr = k_row[:, t, :].rearrange("p (h d) -> p h d", d=QH)
                link(dve.tensor_copy(kr[:, :, 0:QK], kv_row[:, t, :].rearrange("p (h d) -> p h d", d=P)[:, :, 0:QK]))
            dve.sem_inc(qk_ready, 1)
            lo2("q_up 1")
            lo2("g1 1")
            s, use = piece2("q_up 1")
            dve.wait_ge(w_used[s], use + 1)
            for t in range(T):
                for n in range(2):
                    dve.tensor_scalar(q_row[:, t, n * QL:(n + 1) * QL], ps[:, 4 + 2 * t + n, 0:QL], QH ** -0.5, None,
                                      ALU.mult).then_inc(q_scaled, 1)
            lo2("g2 0")
            dve.wait_ge(q_scaled, 4)
            for t in range(T):
                qr = q_row[:, t, :].rearrange("p (h d) -> p h d", d=QH)
                co = cos[:, t, :].rearrange("p (o r) -> p o r", o=1).broadcast_to([P, H, 16])
                si = sin[:, t, :].rearrange("p (o r) -> p o r", o=1).broadcast_to([P, H, 16])
                rotate(qr[:, :, QK:QK + 16], qr[:, :, QK + 16:QH], qr[:, :, QK:QK + 16], qr[:, :, QK + 16:QH], tmp, co, si)
            dve.sem_inc(qk_ready, 1)
            dve.wait_ge(f_mm, 1)
            for g in range(4):
                dve.tensor_copy(nT[:, 4 + g, :], ps[:, 4 + g // 2, (g % 2) * S:(g % 2 + 1) * S]).then_inc(f_out, 1)
            lo2("g2 1")
            dve.wait_ge(f_hi, 1)
            dve.tensor_tensor(x_lo[:, 4:8, :], nT[:, 4:8, :], x_hi[:, 4:8, :].bitcast(F32), ALU.subtract).then_inc(f_lo, 1)
            lo2("g3 0")
            lo2("fourier 0")

            def softmax_max(h):
                dve.wait_ge(s_mm, h + 1)
                m = stat[:, 16 + 2 * h:18 + 2 * h]
                dve.tensor_reduce(m, ps[:, 4 + h % 3, :].rearrange("p (t n) -> p t n", n=S), AX.X, ALU.max,
                                  negate=True).then_inc(smax_ready, 1)

            def probs_out(h):
                dve.wait_ge(s_tr, h + 1)
                if h >= 2:
                    dve.wait_ge(om_mm, h - 1)
                dve.tensor_copy(probT[:, h % 2, :], ps[:, 7, :]).then_inc(sT_out, 1)

            softmax_max(0)
            softmax_max(1)
            for h in range(H):
                if h + 2 < H:
                    softmax_max(h + 2)
                probs_out(h)
                if h == 2:
                    lo2("g3 1")
            dve.wait_ge(s_exp, 2 * H)
            link(dve.reciprocal(trig[:, 2, :, 0:H], trig[:, 0, :, 0:H]))
            dve.wait_ge(om_mm, H)
            for t in range(T):
                rs = trig[:, 2, t, 0:H].rearrange("p (h o) -> p h o", o=1).broadcast_to([P, H, DH])
                dve.tensor_tensor(y_row[:, t, 0:NB].rearrange("p (h d) -> p h d", d=DH),
                                  ps[:, 2 + t, :].rearrange("p (h d) -> p h d", d=DH), rs, ALU.mult).then_inc(om_out, 1)

            def gate_ya(n):
                s, use = piece2(f"fourier {n}")
                dve.wait_ge(w_used[s], use + 1)
                v = sig[:, :, n * NB:(n + 1) * NB]
                dve.tensor_tensor(v, ps[:, 4:6, :], v, ALU.mult).then_inc(ya_out, 1)

            def gate_yb(n):
                s, use = piece2(f"mla {n}")
                dve.wait_ge(w_used[s], use + 1)
                dve.wait_ge(grp_out, 24 + 2 * n + 2)
                v = y_row[:, :, n * NB:(n + 1) * NB]
                b = 2 - 2 * n
                link(dve.tensor_tensor(v, ps[:, b:b + 2, :], sig[:, :, D + n * NB:D + (n + 1) * NB], ALU.mult))
                dve.tensor_tensor(v, v, sig[:, :, n * NB:(n + 1) * NB], ALU.add).then_inc(yb_out, 1)

            gate_ya(0)
            lo2("mla 0")
            dve.wait_ge(omT_mm, 1)
            for k in range(4):
                dve.tensor_copy(nT[:, k, :], ps[:, 6 + k // 2, (k % 2) * S:(k % 2 + 1) * S]).then_inc(omT_out, 1)
            dve.wait_ge(omT_hi, 1)
            dve.tensor_tensor(x_lo[:, 0:4, :], nT[:, 0:4, :], x_hi[:, 0:4, :].bitcast(F32), ALU.subtract).then_inc(omT_lo, 1)
            lo2("fourier 1")
            gate_yb(0)
            lo2("mla 1")

            def y_out(j):
                dve.wait_ge(n_tr, 4 * TR["O2"] + j + 1)
                for i in range(2):
                    dve.tensor_copy(nT[:, 2 * j + i, :], ps[:, 6 + j % 2, i * S:(i + 1) * S]).then_inc(n_ready, 1)

            def y_lo(j):
                dve.wait_ge(n_hi, 4 * TR["O2"] + j + 1)
                k = slice(2 * j, 2 * j + 2)
                dve.tensor_tensor(nT_lo[:, k, :], nT[:, k, :], nT_hi[:, k, :].bitcast(F32), ALU.subtract).then_inc(n_lo, 1)

            gate_ya(1)
            lo2("out 0 0")
            y_out(0)
            y_out(1)
            y_lo(0)
            y_lo(1)
            gate_yb(1)
            lo2("out 0 1")
            y_out(2)
            y_out(3)
            y_lo(2)
            y_lo(3)
            lo2("out 1 0")
            lo2("out 1 1")
            split_lo(*gate_up("F3", 0, 0))
            residual("M2", 1, False)
            ffn("F3", nxt=0)
            residual("F3", 0, False)
            dve.wait_ge(post_loaded[0], 48)
            for t in range(T):
                rms_ready(dve, f"end {t}")
                dve.scalar_tensor_tensor(y_row[:, t, :], x_res[:, t, :], stat[:, 8 + t:9 + t], post_gain[:, 0, :],
                                         ALU.mult, ALU.mult).then_inc(y_ready, 1)

        @block.tensor
        def _(pe):
            def mm3(o, xh, xl, wh, wl, start, stop):
                pe.matmul(o, xh, wh, start=start, stop=False, skip_group_check=True)
                pe.matmul(o, xh, wl, start=False, stop=False, skip_group_check=True)
                return pe.matmul(o, xl, wh, start=False, stop=stop, skip_group_check=True)

            def weights(s, use):
                pe.wait_ge(lo_ready[s], use + 1)

            def norm_transposes(ready):
                for j in range(KD // 2):
                    for k in (2 * j, 2 * j + 1):
                        for t in range(T):
                            if j == 0 and k == 0:
                                ready(t)
                            last = pe.transpose(ps[:, 4 + j, (k % 2) * S + t * P:(k % 2) * S + (t + 1) * P],
                                                y_row[:, t, k * P:(k + 1) * P], ident[:])
                    last.then_inc(n_tr, 1)

            def norm(f):
                r = NORM[f]
                norm_transposes(lambda t: pe.wait_ge(y_ready, 2 * r + 1 + t))

            def row_group(s, out_banks, n, first_norm=None, k_at=None, nk=4, x=None, start=None, stop=None, tiles=range(T)):
                for k in range(nk):
                    kk = k_at + k
                    if first_norm is not None and kk % 2 == 0:
                        pe.wait_ge(n_lo, 4 * first_norm + kk // 2 + 1)
                    for t in tiles:
                        xh, xl = x or (nT_hi, nT_lo)
                        last = mm3(out_banks[t], xh[:, kk, t * P:(t + 1) * P], xl[:, kk, t * P:(t + 1) * P],
                                   w_hi[:, s, k * n:(k + 1) * n], w_lo[:, s, k * n:(k + 1) * n],
                                   start=(k == 0 and bool(start)), stop=(k == nk - 1 and bool(stop)))
                return last

            def col_group(s, half, bank, first_norm=None, first_half=0):
                for k in range(4):
                    kk = 4 * half + k
                    if first_norm is not None and kk % 2 == 0:
                        pe.wait_ge(n_lo, 4 * first_norm + kk // 2 + 1)
                    for i in range(4):
                        o = ps[:, bank + i // 2, (i % 2) * S:(i % 2 + 1) * S]
                        cols = slice(k * NB + i * P, k * NB + (i + 1) * P)
                        pe.matmul(o, w_hi[:, s, cols], nT_hi[:, kk, :], start=(half == first_half and k == 0 and i % 2 == 0),
                                  stop=False, skip_group_check=True)
                        pe.matmul(o, w_hi[:, s, cols], nT_lo[:, kk, :], start=False, stop=False, skip_group_check=True)
                        last = pe.matmul(o, w_lo[:, s, cols], nT_hi[:, kk, :], start=False,
                                         stop=(half != first_half and k == 3), skip_group_check=True)
                return last

            def body(f, c, down=True, gu=True, first_norm=None, first=False, hooks=((), (), ())):
                i = FFN.index(f) * NC
                first_chunk = isinstance(c, int) and c == 0
                bank = 2 if first_chunk else 0

                def gate_up_half(half):
                    s, use = gate_up(f, half, c)
                    weights(s, use)
                    col_group(s, half, bank, first_norm).then_inc(w_used[s], 1)

                if gu:
                    if not (isinstance(c, int) and c <= 1):
                        pe.wait_ge(h_ready, c + i)
                    gate_up_half(0)
                for hook in hooks[0]:
                    hook()
                if gu:
                    gate_up_half(1)
                for hook in hooks[1]:
                    hook()
                if down:
                    s, use = down_piece(f, c - 1)
                    weights(s, use)
                    pe.wait_ge(ht_lo, c + i)
                    last_chunk = not gu
                    xh, xl = (nT_hi, nT_lo) if last_chunk else (hT_hi, hT_lo)
                    for t in range(T):
                        for j in range(2):
                            for n in range(2):
                                last = mm3(ps[:, 4 + 2 * t + n, :], xh[:, j, t * P:(t + 1) * P], xl[:, j, t * P:(t + 1) * P],
                                           w_hi[:, s, j * D + n * NB:j * D + (n + 1) * NB],
                                           w_lo[:, s, j * D + n * NB:j * D + (n + 1) * NB],
                                           start=(first and j == 0), stop=(last_chunk and j == 1))
                        if last_chunk and t == 0:
                            last.then_inc(down_done, 1)
                    last.then_inc(w_used[s], 1)
                for hook in hooks[2]:
                    hook()

            def sum_columns(batch, acc):
                n, f, bank = COLS.index(batch), batch.split()[0], cols_bank(batch)
                if n:
                    for half in range(2):
                        pe.wait_ge(ada_done[half], n_ada[f] + KD)
                    wait(pe, gate_out, 2 * n_gates[f])
                    if bank == 0:
                        pe.wait_ge(h_ready, (FFN.index(f) + 1) * NC)
                wait(pe, cols_out, n)
                for i, (off, *_) in enumerate(col_sums[batch]):
                    if n == 0:
                        if i:
                            norm("F0")
                        for half in range(2):
                            pe.wait_ge(ada_done[half], 2 * i + 2)
                    for k in range(KD):
                        last = pe.matmul(ps[:, bank, KD * i + k:KD * i + k + 1], acc[:, off + k * P:off + (k + 1) * P],
                                         ones[:, 0:1], start=True, stop=True, skip_group_check=True)
                last.then_inc(acc_cols, 1)

            acc_flat = mod_acc.rearrange("p a b -> p (a b)")

            def sum_gate(f, i, half):
                off = gates[f][i][0] + half * NB
                n = 2 * (n_gates[f] + i) + half
                pe.wait_ge(ada_done[0], n_ada[f] + KD)
                if i:
                    for h in range(2):
                        pe.wait_ge(ada_done[h], n_ada[f] + KD + 2)
                wait(pe, gate_out, n - 1)
                if i == 0 and half == 1 and f"{f} early" in COLS:
                    pe.wait_ge(cols_out, COLS.index(f"{f} early") + 1)
                pe.matmul(ps[:, 2 + half, :], ones[:], acc_flat[:, off:off + NB], start=True, stop=True).then_inc(acc_gate, 1)

            def ffn(f):
                r = NORM[f]
                if r:
                    norm(f)
                body(f, 0, down=False, first_norm=TR[f])
                body(f, 1, first=True)
                with pe.Fori(2, NC - 2) as c:
                    body(f, c)
                body(f, NC - 2, hooks=([lambda: sum_columns(f"{f} early", acc_flat)] if f"{f} early" in COLS else (),
                                       [lambda: sum_gate(f, 0, 0)], ()))
                body(f, NC - 1, hooks=([lambda: sum_gate(f, 0, 1)], (), ()))
                body(f, NC, gu=False)
                if f"{f} late" in COLS:
                    sum_columns(f"{f} late", acc_flat)
                for i in range(1, len(gates[f])):
                    sum_gate(f, i, 0)
                    sum_gate(f, i, 1)

            pe.wait_ge(const_ready, 2)
            pe.wait_ge(rel_ready, 1)
            for h in range(H):
                if h >= 4:
                    pe.wait_ge(toe_sb, h - 3)
                pe.matmul(ps[:, h % 4, 0:CAUSAL], rel_bc[0:BUCKETS, h, :], onehot[0:BUCKETS, :], start=True, stop=True)\
                    .then_inc(toe_mm, 1)
            pe.wait_ge(toe_sb, H)
            pe.wait_ge(small_loaded, SMALL)
            for b in range(2):
                last = pe.transpose(ps[:, 7, b * P:b * P + VECS[b]], vec_rows[0:VECS[b], b, :], ident[0:VECS[b], 0:VECS[b]])
            last.then_inc(vec_tr, 1)
            pe.wait_ge(vec_ready, 2)
            sum_columns("start", first_acc)
            ffn("F0")

            norm("M1")

            def group_free(g):
                wait(pe, grp_out, 2 * (g - 1))

            def group_half(g, half, first_norm=None):
                s, use = piece1(half, g)
                weights(s, use)
                col_group(s, half, 2 * (g % 2), first_norm, 1 if g == KI else 0).then_inc(w_used[s], 1)

            def value_half(g, half):
                s, use = piece1(half, g)
                weights(s, use)
                row_group(s, [ps[:, 2 * (g % 2) + t, :] for t in range(T)], NB, None, 4 * half,
                          start=(half == 0), stop=(half == 1)).then_inc(w_used[s], 1)

            def head(i, h):
                return qkT[DH * (h % 2):DH * (h % 2) + DH, i, h // 2, :]

            group_half(0, 0, TR["M1"])
            group_half(0, 1, TR["M1"])
            pe.wait_ge(gate_out, 2 * n_gates["F1"])
            group_half(1, 0)
            group_half(1, 1)
            group_free(2)
            group_half(2, 0)
            pe.wait_ge(grp_out, 4)
            for h in range(H):
                if h >= 4:
                    pe.wait_ge(z_out, h - 3)
                q, k = head(TQB, h), head(TKB, h)
                pe.matmul(ps[:, 4 + h % 4, 0:S], k[:, 0:P], q, start=True, stop=True, skip_group_check=True)
                pe.matmul(ps[:, 4 + h % 4, S:CAUSAL], k[:, P:S], q[:, P:S], start=True, stop=True,
                          skip_group_check=True).then_inc(z_mm, 1)
            group_half(2, 1)
            weights(*ki_piece)
            pe.wait_ge(z_out, H)
            for k in range(KD):
                for t in range(T):
                    last = mm3(ps[:, 4 + t, 0:72], nT_hi[:, k, t * P:(t + 1) * P], nT_lo[:, k, t * P:(t + 1) * P],
                               w_hi[:, SLOT_A, k * 72:(k + 1) * 72], w_lo[:, SLOT_A, k * 72:(k + 1) * 72],
                               start=(k == 0), stop=(k == KD - 1))
            last.then_inc(w_used[SLOT_A], 1)
            group_free(3)
            group_half(3, 1)
            pe.wait_ge(ki_ready, 1)
            for t in range(T):
                last = pe.transpose(ps[:, 6, t * P:(t + 1) * P], ki2[:, t, :], ident[:])
            last.then_inc(ki_tr, 1)
            group_half(3, 0)
            pe.wait_ge(kiT_ready, 1)
            pe.wait_ge(grp_out, 6)
            for h in range(H):
                if h >= 4:
                    pe.wait_ge(idx_relu, h - 3)
                q = head(TQI, h)
                k = kiT[DH * (h % 2):DH * (h % 2) + DH, :]
                pe.matmul(ps[:, 4 + h % 4, 0:S], q[:, P:S], k, start=True, stop=True, skip_group_check=True)
                pe.matmul(ps[:, 4 + h % 4, S:CAUSAL], q[:, 0:P], k[:, 0:P], start=True, stop=True,
                          skip_group_check=True).then_inc(idx_mm, 1)
            value_half(4, 0)
            pe.wait_ge(u_masked, 2)
            for h in range(H):
                if h >= 4:
                    pe.wait_ge(r_out, h - 3)
                else:
                    pe.wait_ge(idx_relu, h + 5)
                b = ps[:, 4 + h % 4, :]
                pe.matmul(b[:, 0:CAUSAL], tri[:], u_sb[:, h, :], start=True, stop=False, skip_group_check=True)
                pe.matmul(b[:, P:S], ones[:], u_sb[:, h, S:CAUSAL], start=False, stop=True,
                          skip_group_check=True).then_inc(r_mm, 1)
            value_half(4, 1)
            group_free(5)
            group_half(5, 0)
            pe.wait_ge(a_masked, 2)
            pe.wait_ge(r_out, H)
            pe.wait_ge(grp_out, 10)
            for h in range(H):
                v = [v_row[:, 1, s, h * DH:(h + 1) * DH] for s in range(2)]
                o = [ps[:, 4 + t, h * DH:(h + 1) * DH] for t in range(T)]
                pe.matmul(o[0], z_sb[:, h, 0:P], v[0], start=True, stop=True, skip_group_check=True)
                pe.matmul(o[1], z_sb[:, h, P:S], v[0], start=True, stop=False, skip_group_check=True)
                last = pe.matmul(o[1], z_sb[:, h, S:CAUSAL], v[1], start=False, stop=True, skip_group_check=True)
            last.then_inc(ob_mm, 1)
            group_half(5, 1)
            value_half(6, 0)

            def out_transposes(half, bank):
                for j in range(2):
                    for i in range(2):
                        for t in range(T):
                            last = pe.transpose(ps[:, bank + j, i * S + t * P:i * S + (t + 1) * P],
                                                y_row[:, t, half * NB + (2 * j + i) * P:half * NB + (2 * j + i + 1) * P], ident[:])
                    last.then_inc(n_tr, 1)

            pe.wait_ge(ob_ready, 1)
            pe.wait_ge(grp_out, 12)
            out_transposes(1, 2)
            pe.wait_ge(ob_out, T)
            for h in range(H):
                if h >= 4:
                    pe.wait_ge(l_out, h - 3)
                q, k = head(TQA, h), head(TKA, h)
                pe.matmul(ps[:, 4 + h % 4, 0:S], q[:, P:S], k, start=True, stop=True, skip_group_check=True)
                pe.matmul(ps[:, 4 + h % 4, S:CAUSAL], q[:, 0:P], k[:, 0:P], start=True, stop=True,
                          skip_group_check=True).then_inc(l_mm, 1)
            value_half(6, 1)
            pe.wait_ge(l_out, H)

            def probs_times_v(h):
                pe.wait_ge(pT_out, h + 1)
                v = [v_row[:, 0, s, h * DH:(h + 1) * DH] for s in range(2)]
                o = [ps[:, t, h * DH:(h + 1) * DH] for t in range(T)]
                pe.matmul(o[1], e_sb[:, h, 0:P], v[0], start=True, stop=False, skip_group_check=True)
                pe.matmul(o[1], e_sb[:, h, P:S], v[1], start=False, stop=True, skip_group_check=True)
                return pe.matmul(o[0], e_sb[:, h, S:CAUSAL], v[0], start=True, stop=True, skip_group_check=True)

            for h in range(H):
                if h >= 2:
                    pe.wait_ge(pT_out, h - 1)
                pe.wait_ge(p_exp, 2 * h + 2)
                for i in range(3):
                    last = pe.transpose(ps[:, 6 + h % 2, i * P:(i + 1) * P], z_sb[:, h, i * P:(i + 1) * P], ident[:])
                last.then_inc(p_tr, 1)
                if h == 0:
                    pe.wait_ge(grp_out, 14)
                else:
                    probs_times_v(h - 1)
            probs_times_v(H - 1).then_inc(oa_mm, 1)
            banks = [[ps[:, output_at("M1", t) + n, :] for t in range(T)] for n in range(2)]
            pe.wait_ge(n_lo, 4 * TR["O1"] + 2)
            for n, (s, use) in enumerate((out1[1, 0], out1[1, 1])):
                weights(s, use)
                row_group(s, banks[n], NB, None, 4, start=True).then_inc(w_used[s], 1)
            pe.wait_ge(o_ready, 1)
            pe.wait_ge(pT_out, H)
            out_transposes(0, 6)
            pe.wait_ge(n_lo, 4 * TR["O1"] + 4)
            for t in range(T):
                for n, (s, use) in enumerate((out1[0, 0], out1[0, 1])):
                    weights(s, use)
                    last = row_group(s, banks[n], NB, None, 0, stop=True, tiles=(t,))
                    if t == 1:
                        last.then_inc(w_used[s], 1)
                if t == 0:
                    last.then_inc(mix_half, 1)

            ffn("F1")
            ffn("F2")

            norm("M2")

            def half2(name, n, banks, first_norm=None):
                s, use = piece2(name)
                h = int(name[-1])
                weights(s, use)
                row_group(s, [ps[:, b, 0:n] for b in banks], n, first_norm, 4 * h, start=(h == 0), stop=(h == 1))\
                    .then_inc(w_used[s], 1)

            for h in range(2):
                half2(f"q {h}", QL, (0, 1), TR["M2"])
            pe.wait_ge(gate_out, 2 * n_gates["F3"])
            for h in range(2):
                half2(f"kv {h}", KVL + ROPE, (2, 3))
            pe.wait_ge(grp_out, 16)
            for h in range(2):
                half2(f"uf {h}", NB, (0, 1))
            pe.wait_ge(lat_ready, 4)
            for k in range(5):
                for t in range(T):
                    last = pe.transpose(ps[:, (6, 6, 7, 7, 5)[k], (k % 2) * S + t * P:(k % 2) * S + (t + 1) * P],
                                        lat[:, t, k * P:(k + 1) * P], ident[:])
            last.then_inc(lat_tr, 1)
            pe.wait_ge(grp_out, 18)
            half2("g0 0", NB, (2, 3))
            pe.wait_ge(dft_loaded, 32)
            pe.wait_ge(grp_out, 20)
            pe.wait_ge(lat_out, 5)
            for g in range(4):
                for k in range(2):
                    last = pe.matmul(ps[:, 4 + g, :], uf[:, k, g * P:(g + 1) * P], dft[:, k, :], start=(k == 0), stop=(k == 1))
                last.then_inc(cu_mm, 1)
            half2("g0 1", NB, (2, 3))
            pe.wait_ge(lat_lo, 1)
            pe.wait_ge(cu_out, 4)
            weights(*kv_up)
            for t in range(T):
                for n in range(2):
                    for k in range(2):
                        last = mm3(ps[:, 4 + 2 * t + n, :], hT_hi[:, k, t * P:(t + 1) * P], hT_lo[:, k, t * P:(t + 1) * P],
                                   w_hi[:, SLOT_D, k * D + n * NB:k * D + (n + 1) * NB],
                                   w_lo[:, SLOT_D, k * D + n * NB:k * D + (n + 1) * NB], start=(k == 0), stop=(k == 1))
            last.then_inc(w_used[SLOT_D], 1)
            half2("g1 0", NB, (0, 1))
            pe.wait_ge(up_out, 4)
            pe.wait_ge(lat_lo, 2)
            for n in range(2):
                s, use = piece2(f"q_up {n}")
                weights(s, use)
                row_group(s, [ps[:, 4 + 2 * t + n, 0:QL] for t in range(T)], QL, None, 0, nk=3, x=(x_hi, x_lo),
                          start=True, stop=True).then_inc(w_used[s], 1)
            half2("g1 1", NB, (0, 1))
            pe.wait_ge(q_scaled, 4)
            for g in range(4):
                o = ps[:, 4 + g // 2, (g % 2) * S:(g % 2 + 1) * S]
                pe.matmul(o, dftd[:, 0, :], cu[:, g, 0:S], start=True, stop=False, skip_group_check=True)
                last = pe.matmul(o, dftd[:, 1, :], cu[:, g, S:2 * S], start=False, stop=True, skip_group_check=True)
            last.then_inc(f_mm, 1)
            pe.wait_ge(grp_out, 22)
            half2("g2 0", NB, (2, 3))
            pe.wait_ge(f_out, 4)
            for i in range(8):
                src = k_row if i < 4 else q_row
                if i % 4 == 0:
                    pe.wait_ge(qk_ready, i // 4 + 1)
                if i >= 4:
                    pe.wait_ge(qkT_out, i - 3)
                for j in range(2):
                    h = 2 * (i % 4) + j
                    for t in range(T):
                        last = pe.transpose(ps[0:QH, 4 + i % 4, j * S + t * P:j * S + (t + 1) * P],
                                            src[:, t, h * QH:(h + 1) * QH], ident[:])
                last.then_inc(qk_tr, 1)
            half2("g2 1", NB, (2, 3))
            pe.wait_ge(grp_out, 24)
            half2("g3 0", NB, (0, 1))
            pe.wait_ge(qkT_out, 8)

            def scores(h):
                if h >= 3:
                    pe.wait_ge(s_exp, 2 * (h - 2))
                for t in range(T):
                    last = pe.matmul(ps[:, 4 + h % 3, t * S:(t + 1) * S], qT[0:QH, h, t * P:(t + 1) * P], kT[0:QH, h, :],
                                     start=True, stop=True, skip_group_check=True)
                last.then_inc(s_mm, 1)

            def weighted(h):
                pe.wait_ge(sT_out, h + 1)
                for t in range(T):
                    for k in range(2):
                        last = pe.matmul(ps[:, 2 + t, h * DH:(h + 1) * DH], probT[:, h % 2, k * S + t * P:k * S + (t + 1) * P],
                                         kv_row[:, k, h * P + QK:(h + 1) * P], start=(k == 0), stop=(k == 1),
                                         skip_group_check=True)
                last.then_inc(om_mm, 1)

            for h in range(3):
                scores(h)
            pe.wait_ge(grp_out, 26)
            for h in range(H):
                pe.wait_ge(s_exp, 2 * h + 2)
                if h >= 1:
                    pe.wait_ge(sT_out, h)
                for k in range(2):
                    for t in range(T):
                        last = pe.transpose(ps[:, 7, k * S + t * P:k * S + (t + 1) * P],
                                            prob4[:, h % 4, t * S + k * P:t * S + (k + 1) * P], ident[:])
                last.then_inc(s_tr, 1)
                if h + 3 < H:
                    scores(h + 3)
                if h >= 1:
                    weighted(h - 1)
            weighted(H - 1)

            def linear2(name, banks, k0):
                s, use = piece2(name)
                weights(s, use)
                row_group(s, [ps[:, b, :] for b in banks], NB, None, 0, x=(x_hi[:, k0:k0 + 4, :], x_lo[:, k0:k0 + 4, :]),
                          start=True, stop=True).then_inc(w_used[s], 1)

            pe.wait_ge(f_lo, 1)
            linear2("fourier 0", (4, 5), 4)
            pe.wait_ge(om_out, T)
            pe.wait_ge(sT_out, H)
            for k in range(4):
                for t in range(T):
                    last = pe.transpose(ps[:, 6 + k // 2, (k % 2) * S + t * P:(k % 2) * S + (t + 1) * P],
                                        y_row[:, t, k * P:(k + 1) * P], ident[:])
            last.then_inc(omT_mm, 1)
            half2("g3 1", NB, (0, 1))
            pe.wait_ge(omT_lo, 1)
            linear2("mla 0", (2, 3), 0)
            pe.wait_ge(ya_out, 1)
            linear2("fourier 1", (4, 5), 4)
            pe.wait_ge(grp_out, 28)
            linear2("mla 1", (0, 1), 0)

            def y_transposes(half):
                pe.wait_ge(yb_out, half + 1)
                for j in range(2):
                    for i in range(2):
                        k = 4 * half + 2 * j + i
                        if half:
                            pe.wait_ge(n_ready, 8 * TR["O2"] + 2 * j + 2)
                        for t in range(T):
                            last = pe.transpose(ps[:, 6 + j, i * S + t * P:i * S + (t + 1) * P],
                                                y_row[:, t, k * P:(k + 1) * P], ident[:])
                    last.then_inc(n_tr, 1)

            y_transposes(0)
            banks = [[ps[:, output_at("M2", t) + n, :] for t in range(T)] for n in range(2)]
            pe.wait_ge(ya_out, 2)
            pe.wait_ge(n_lo, 4 * TR["O2"] + 2)
            for n in range(2):
                s, use = piece2(f"out 0 {n}")
                weights(s, use)
                row_group(s, banks[n], NB, None, 0, start=True).then_inc(w_used[s], 1)
                if n == 0:
                    y_transposes(1)
            pe.wait_ge(n_lo, 4 * TR["O2"] + 4)
            for t in range(T):
                for n in range(2):
                    s, use = piece2(f"out 1 {n}")
                    weights(s, use)
                    last = row_group(s, banks[n], NB, None, 4, stop=True, tiles=(t,))
                    if t == 1:
                        last.then_inc(w_used[s], 1)
                if t == 0:
                    last.then_inc(mix_half, 1)

            ffn("F3")


def onehot_buckets():
    import math
    import numpy as np
    n = np.maximum(255 - np.arange(CAUSAL), 0)
    exact = BUCKETS // 2
    large = exact + (np.log(np.maximum(n, 1).astype(np.float32) / exact) / math.log(128 / exact)
                     * (BUCKETS - exact)).astype(np.int32)
    bucket = np.where(n < exact, n, np.minimum(large, BUCKETS - 1))
    return (bucket[None, :] == np.arange(BUCKETS)[:, None]).astype(np.float32)


def dft_tables():
    import numpy as np
    s, d = np.arange(S), np.arange(P)
    ws = 2 * np.pi * ((s[:, None] * s[None, :]) % S) / S
    wd = 2 * np.pi * ((d[:, None] * d[None, :]) % P) / P
    over_s = np.concatenate([np.cos(ws), np.sin(ws)], 1) / np.sqrt(S)
    over_d = np.concatenate([np.cos(wd), -np.sin(wd)], 1) / np.sqrt(P)
    return over_s.astype(np.float32), over_d.astype(np.float32)


def inverse_frequencies():
    import numpy as np
    e = np.arange(16, dtype=np.float32) * np.float32(2.0) / np.float32(32)
    return (np.float32(1.0) / (np.float32(10000.0) ** e)).astype(np.float32)[None, :]


_OUTS = [((1, 256, 1024), "float32")]


def kernel(**inputs):
    import numpy as np
    import concourse.bacc as bacc
    from concourse.bass_utils import run_bass_kernel_spmd

    nc = bacc.Bacc("TRN2", target_bir_lowering=False, num_devices=1)
    arrays, aps = {}, {}
    over_s, over_d = dft_tables()
    shape_constants = {"onehot": onehot_buckets(), "dft_s": over_s, "dft_d": over_d, "inv_freq": inverse_frequencies()}
    for name, v in {**inputs, **shape_constants}.items():
        v = np.ascontiguousarray(v)
        arrays[f"in_{name}"] = v
        aps[name] = nc.dram_tensor(f"in_{name}", v.shape, mybir.dt.from_np(v.dtype), kind="ExternalInput").ap()
    out = nc.dram_tensor("out", _OUTS[0][0], F32, kind="ExternalOutput").ap()
    program(nc, aps, out)
    r = run_bass_kernel_spmd(nc, [arrays], core_ids=[0])
    return r.results[0]["out"]
```
